# Optimizing a Trainium2 kernel written in Bass

```python
import math
import jax, jax.numpy as jnp
from jax import lax
import numpy as np

D_MODEL = 1024
BATCH = 1
SEQ = 512
DEPTH = 1

MIX_WIDTH = D_MODEL
SSM_WIDTH = MIX_WIDTH // 2
ATTN_WIDTH = MIX_WIDTH - SSM_WIDTH
SSM_GROUP = 16
SSM_GROUPS = SSM_WIDTH // SSM_GROUP
SSM_STATE = 64
HEAD_DIM = 64
N_HEADS = ATTN_WIDTH // HEAD_DIM
IDX_HEADS = 8
IDX_DIM = 64
TOPK_MAX = 256
QBLOCK = 32
NUM_BUCKETS = 32
MAX_DISTANCE = 128
EPS = 1e-6
DT_MIN = 1e-3
DT_MAX = 1e-1
SPLITS = (SSM_WIDTH, SSM_WIDTH, ATTN_WIDTH, ATTN_WIDTH, ATTN_WIDTH, ATTN_WIDTH,
          IDX_HEADS * IDX_DIM, IDX_DIM, IDX_HEADS)
IN_WIDTH = 2 * SSM_WIDTH + 4 * ATTN_WIDTH + IDX_HEADS * IDX_DIM + IDX_DIM + IDX_HEADS


def rms_norm(x, g):
    xf = x.astype(jnp.float32)
    xf = xf * lax.rsqrt(jnp.mean(xf * xf, axis=-1, keepdims=True) + EPS)
    return (xf * g.astype(jnp.float32)).astype(x.dtype)

def t5_causal_bucket(dist):
    max_exact = NUM_BUCKETS // 2
    is_small = dist < max_exact
    d = jnp.maximum(dist, 1).astype(jnp.float32)
    large = max_exact + (jnp.log(d / max_exact) / math.log(MAX_DISTANCE / max_exact)
                         * (NUM_BUCKETS - max_exact)).astype(jnp.int32)
    large = jnp.minimum(large, NUM_BUCKETS - 1)
    return jnp.where(is_small, dist, large)

def _ssm_combine(e1, e2):
    a1, b1 = e1
    a2, b2 = e2
    return a1 * a2, a2 * b1 + b2

def s5_mixer(u, a_re, a_im, log_dt, b_re, b_im, c_re, c_im, d_skip, w_glu, b_glu):
    bsz, seq, _ = u.shape
    uf = u.astype(jnp.float32)
    ug = uf.reshape(bsz, seq, SSM_GROUPS, SSM_GROUP)
    lam = lax.complex(a_re.astype(jnp.float32), a_im.astype(jnp.float32))
    dt = jnp.exp(log_dt.astype(jnp.float32))[:, None]
    lam_bar = jnp.exp(lam * dt)
    b_mat = lax.complex(b_re.astype(jnp.float32), b_im.astype(jnp.float32))
    b_bar = ((lam_bar - 1.0) / lam)[..., None] * b_mat
    bu = jnp.einsum('gpc,bsgc->bsgp', b_bar, ug.astype(jnp.complex64))
    a_seq = jnp.broadcast_to(lam_bar, (1, seq) + lam_bar.shape)
    _, states = lax.associative_scan(_ssm_combine, (a_seq, bu), axis=1)
    c_mat = lax.complex(c_re.astype(jnp.float32), c_im.astype(jnp.float32))
    y = jnp.einsum('gcp,bsgp->bsgc', c_mat, states).real.reshape(bsz, seq, SSM_WIDTH)
    y = y + d_skip.astype(jnp.float32) * uf
    z = jax.nn.gelu(y)
    z = z * jax.nn.sigmoid(z @ w_glu.astype(jnp.float32) + b_glu.astype(jnp.float32))
    return z.astype(u.dtype)

def dsa_mixer(q, k, v, q_idx, k_idx, w_idx, q_gain, k_gain, rel_bias):
    bsz, seq = q.shape[0], q.shape[1]
    topk = min(TOPK_MAX, seq // 4)
    nb = seq // QBLOCK
    scale = HEAD_DIM ** -0.5
    q = rms_norm(q.reshape(bsz, seq, N_HEADS, HEAD_DIM), q_gain)
    k = rms_norm(k.reshape(bsz, seq, N_HEADS, HEAD_DIM), k_gain)
    v = v.reshape(bsz, seq, N_HEADS, HEAD_DIM)
    q_idx = q_idx.reshape(bsz, seq, IDX_HEADS, IDX_DIM)
    w_idx = w_idx * (IDX_HEADS ** -0.5)
    key_pos = jnp.arange(seq, dtype=jnp.int32)

    def to_blocks(t):
        return jnp.moveaxis(t.reshape((bsz, nb, QBLOCK) + t.shape[2:]), 1, 0)

    gather = jax.vmap(lambda src, idx: src[idx])

    def block(args):
        qb, qib, wib, pos = args
        rel = jnp.einsum('bqhd,bsd->bqhs', qib, k_idx)
        score = jnp.einsum('bqh,bqhs->bqs', wib, jax.nn.relu(rel)).astype(jnp.float32)
        causal = key_pos[None, :] <= pos[:, None]
        score = jnp.where(causal[None], score, -jnp.inf)
        _, sel = lax.top_k(score, topk)
        k_sel = gather(k, sel)
        v_sel = gather(v, sel)
        logits = jnp.einsum('bqhd,bqkhd->bqhk', qb, k_sel).astype(jnp.float32) * scale
        dist = pos[None, :, None] - sel
        bias = rel_bias[t5_causal_bucket(jnp.maximum(dist, 0))]
        logits = logits + jnp.transpose(bias, (0, 1, 3, 2)).astype(jnp.float32)
        logits = jnp.where((dist >= 0)[:, :, None, :], logits, -jnp.inf)
        p = jax.nn.softmax(logits, axis=-1).astype(v.dtype)
        return jnp.einsum('bqhk,bqkhd->bqhd', p, v_sel)

    out = lax.map(block, (to_blocks(q), to_blocks(q_idx), to_blocks(w_idx),
                          key_pos.reshape(nb, QBLOCK)))
    return jnp.moveaxis(out, 0, 1).reshape(bsz, seq, ATTN_WIDTH)

def first_inputs(seed: int = 0) -> dict:
    key = jax.random.key(seed)
    ks = jax.random.split(key, 24)
    f32 = jnp.float32
    x = jax.random.normal(ks[0], (BATCH, SEQ, D_MODEL), f32)
    c = jax.random.normal(ks[1], (BATCH, D_MODEL), f32)
    rel_bias = 0.5 * jax.random.normal(ks[2], (NUM_BUCKETS, N_HEADS), f32)
    norm_g = 1.0 + 0.05 * jax.random.normal(ks[3], (DEPTH, D_MODEL), f32)
    w_ada = 0.5 * D_MODEL ** -0.5 * jax.random.normal(ks[4], (DEPTH, D_MODEL, 3 * D_MODEL), f32)
    b_ada = 0.01 * jax.random.normal(ks[5], (DEPTH, 3 * D_MODEL), f32)
    w_in = D_MODEL ** -0.5 * jax.random.normal(ks[6], (DEPTH, D_MODEL, IN_WIDTH), f32)
    q_gain = 1.0 + 0.05 * jax.random.normal(ks[7], (DEPTH, HEAD_DIM), f32)
    k_gain = 1.0 + 0.05 * jax.random.normal(ks[8], (DEPTH, HEAD_DIM), f32)
    n = jnp.arange(SSM_STATE, dtype=f32)
    a_re = -0.5 + 0.01 * jax.random.normal(ks[9], (DEPTH, SSM_GROUPS, SSM_STATE), f32)
    a_im = math.pi * n + 0.01 * jax.random.normal(ks[10], (DEPTH, SSM_GROUPS, SSM_STATE), f32)
    log_dt = jax.random.uniform(ks[11], (DEPTH, SSM_GROUPS), f32,
                                minval=math.log(DT_MIN), maxval=math.log(DT_MAX))
    b_re = (2 * SSM_GROUP) ** -0.5 * jax.random.normal(ks[12], (DEPTH, SSM_GROUPS, SSM_STATE, SSM_GROUP), f32)
    b_im = (2 * SSM_GROUP) ** -0.5 * jax.random.normal(ks[13], (DEPTH, SSM_GROUPS, SSM_STATE, SSM_GROUP), f32)
    c_re = (2 * SSM_STATE) ** -0.5 * jax.random.normal(ks[14], (DEPTH, SSM_GROUPS, SSM_GROUP, SSM_STATE), f32)
    c_im = (2 * SSM_STATE) ** -0.5 * jax.random.normal(ks[15], (DEPTH, SSM_GROUPS, SSM_GROUP, SSM_STATE), f32)
    d_skip = jax.random.normal(ks[16], (DEPTH, SSM_WIDTH), f32)
    w_glu = SSM_WIDTH ** -0.5 * jax.random.normal(ks[17], (DEPTH, SSM_WIDTH, SSM_WIDTH), f32)
    b_glu = 0.01 * jax.random.normal(ks[18], (DEPTH, SSM_WIDTH), f32)
    w_out = MIX_WIDTH ** -0.5 * jax.random.normal(ks[19], (DEPTH, MIX_WIDTH, D_MODEL), f32)
    return {"x": x, "c": c, "rel_bias": rel_bias, "norm_g": norm_g, "w_ada": w_ada,
            "b_ada": b_ada, "w_in": w_in, "q_gain": q_gain, "k_gain": k_gain,
            "a_re": a_re, "a_im": a_im, "log_dt": log_dt, "b_re": b_re, "b_im": b_im,
            "c_re": c_re, "c_im": c_im, "d_skip": d_skip, "w_glu": w_glu, "b_glu": b_glu,
            "w_out": w_out}

def first_block(x, c, rel_bias, norm_g, w_ada, b_ada, w_in, q_gain, k_gain, a_re, a_im,
              log_dt, b_re, b_im, c_re, c_im, d_skip, w_glu, b_glu, w_out):
    split_points = np.cumsum(SPLITS)[:-1].tolist()
    cond = jax.nn.silu(c)
    for l in range(DEPTH):
        mod = cond @ w_ada[l] + b_ada[l]
        shift, scale, gate = jnp.split(mod, 3, axis=-1)
        h = rms_norm(x, norm_g[l]) * (1.0 + scale[:, None, :]) + shift[:, None, :]
        proj = h @ w_in[l]
        ssm_u, ssm_z, q, k, v, attn_z, q_idx, k_idx, w_idx = jnp.split(proj, split_points, axis=-1)
        y_ssm = s5_mixer(ssm_u, a_re[l], a_im[l], log_dt[l], b_re[l], b_im[l], c_re[l], c_im[l],
                         d_skip[l], w_glu[l], b_glu[l]) * jax.nn.silu(ssm_z)
        y_attn = dsa_mixer(q, k, v, q_idx, k_idx, w_idx, q_gain[l], k_gain[l], rel_bias) * jax.nn.silu(attn_z)
        y = jnp.concatenate([y_ssm, y_attn], axis=-1) @ w_out[l]
        x = x + gate[:, None, :] * y
    return x


POOL_WINDOWS = (2, 4, 8, 16)
N_POOL_GROUPS = len(POOL_WINDOWS)
POOL_GROUP = D_MODEL // 8
POOL_WIDTH = POOL_GROUP * N_POOL_GROUPS
N_HEADS_2 = D_MODEL // HEAD_DIM
N_KV_GROUPS = 2
HEADS_PER_GROUP = N_HEADS_2 // N_KV_GROUPS
ATTN_WIDTH_2 = N_HEADS_2 * HEAD_DIM
N_NSA_BRANCHES = 3
KV_WIDTH = N_NSA_BRANCHES * 2 * N_KV_GROUPS * HEAD_DIM
CMP_BLOCK = 32
CMP_STRIDE = 16
CMP_HIDDEN = 128
SLC_BLOCK = 64
SLC_TOP_N = 8
WINDOW = 512
Q_BLOCK = 32
ROPE_THETA = 10000.0
SCALE = HEAD_DIM ** -0.5
FORCE_BONUS = 1000.0
NEG_INF = -1e30
N_MERGE = 2
OFF_Q = POOL_WIDTH
OFF_KV = OFF_Q + ATTN_WIDTH_2
OFF_NSA_G = OFF_KV + KV_WIDTH
OFF_MERGE_G = OFF_NSA_G + N_NSA_BRANCHES * N_HEADS_2
IN_WIDTH_2 = OFF_MERGE_G + N_MERGE * D_MODEL
D_FF = 2752
CONV_WIDTH = 3


def rms_norm_2(x, w):
    xf = x.astype(jnp.float32)
    y = xf * lax.rsqrt(jnp.mean(xf * xf, axis=-1, keepdims=True) + EPS)
    return (y * w.astype(jnp.float32)).astype(x.dtype)

def rope(x, pos):
    half = HEAD_DIM // 2
    freqs = ROPE_THETA ** (-jnp.arange(half, dtype=jnp.float32) / half)
    ang = pos.astype(jnp.float32)[:, None] * freqs[None, :]
    shp = (1, pos.shape[0]) + (1,) * (x.ndim - 3) + (half,)
    cos = jnp.cos(ang).reshape(shp)
    sin = jnp.sin(ang).reshape(shp)
    xf = x.astype(jnp.float32)
    x1, x2 = xf[..., :half], xf[..., half:]
    return jnp.concatenate([x1 * cos - x2 * sin, x2 * cos + x1 * sin], axis=-1).astype(x.dtype)

def masked_softmax(s, mask):
    s = jnp.where(mask, s.astype(jnp.float32), NEG_INF)
    p = jax.nn.softmax(s, axis=-1)
    return jnp.where(mask, p, 0.0)

def pool_mixer(u, pool_w, pool_scale):
    B, S, _ = u.shape
    ug = u.reshape(B, S, N_POOL_GROUPS, POOL_GROUP).astype(jnp.float32)
    c = jnp.pad(jnp.cumsum(ug, axis=1), ((0, 0), (1, 0), (0, 0), (0, 0)))
    t = jnp.arange(S)
    outs = []
    for gi, w in enumerate(POOL_WINDOWS):
        lo = jnp.maximum(t + 1 - w, 0)
        cnt = jnp.minimum(t + 1, w).astype(jnp.float32)
        outs.append((c[:, 1:, gi] - c[:, lo, gi]) / cnt[None, :, None])
    pooled = jnp.stack(outs, axis=2) - ug
    y = jnp.einsum('bsgc,gcd->bsgd', pooled.astype(u.dtype), pool_w)
    return y.reshape(B, S, POOL_WIDTH) * pool_scale

def compress(k, pos_emb, w1, b1, w2):
    B, S = k.shape[0], k.shape[1]
    n_cmp = (S - CMP_BLOCK) // CMP_STRIDE + 1
    idx = np.arange(n_cmp)[:, None] * CMP_STRIDE + np.arange(CMP_BLOCK)[None, :]
    blk = k[:, idx] + pos_emb[None, None, :, None, :]
    flat = jnp.moveaxis(blk, 3, 2).reshape(B, n_cmp, N_KV_GROUPS, CMP_BLOCK * HEAD_DIM)
    hid = jax.nn.gelu(flat @ w1 + b1)
    return hid @ w2

def nsa_attention(q, k, v, nsa_g, cmp_pos, cmp_w1, cmp_b1, cmp_w2):
    B, S = q.shape[0], q.shape[1]
    k_c, k_s, k_w = k[:, :, 0], k[:, :, 1], k[:, :, 2]
    v_c, v_s, v_w = v[:, :, 0], v[:, :, 1], v[:, :, 2]
    k_cmp = compress(k_c, cmp_pos[0], cmp_w1[0], cmp_b1[0], cmp_w2[0])
    v_cmp = compress(v_c, cmp_pos[1], cmp_w1[1], cmp_b1[1], cmp_w2[1])
    n_cmp = k_cmp.shape[1]
    cmp_end = jnp.asarray(np.arange(n_cmp) * CMP_STRIDE + CMP_BLOCK - 1, dtype=jnp.int32)
    n_slc = S // SLC_BLOCK
    n_sel = min(SLC_TOP_N, n_slc)
    ci = np.arange(n_cmp)[:, None]
    sj = np.arange(n_slc)[None, :]
    overlap = jnp.asarray(((ci * CMP_STRIDE < (sj + 1) * SLC_BLOCK) &
                           (ci * CMP_STRIDE + CMP_BLOCK > sj * SLC_BLOCK)).astype(np.float32))
    ks_blk = k_s.reshape(B, n_slc, SLC_BLOCK, N_KV_GROUPS, HEAD_DIM).transpose(0, 3, 1, 2, 4)
    vs_blk = v_s.reshape(B, n_slc, SLC_BLOCK, N_KV_GROUPS, HEAD_DIM).transpose(0, 3, 1, 2, 4)
    pad = ((0, 0), (WINDOW, 0), (0, 0), (0, 0))
    kw_pad = jnp.pad(k_w, pad)
    vw_pad = jnp.pad(v_w, pad)
    b_ix = jnp.arange(B)[:, None, None, None]
    g_ix = jnp.arange(N_KV_GROUPS)[None, :, None, None]
    blk_ids = jnp.arange(n_slc)

    def chunk(args):
        qc, gc, start = args
        tq = start + jnp.arange(Q_BLOCK)
        qg = qc.reshape(B, Q_BLOCK, N_KV_GROUPS, HEADS_PER_GROUP, HEAD_DIM)
        s_c = jnp.einsum('bqghd,bngd->bghqn', qg, k_cmp)
        p_c = masked_softmax(s_c, cmp_end[None, :] <= tq[:, None])
        o_c = jnp.einsum('bghqn,bngd->bqghd', p_c.astype(v_cmp.dtype), v_cmp)
        imp = jnp.einsum('bghqn,nj->bgqj', p_c, overlap)
        cur = tq // SLC_BLOCK
        forced = ((blk_ids[None] == 0) | (blk_ids[None] == cur[:, None]) |
                  (blk_ids[None] == cur[:, None] - 1)).astype(jnp.float32)
        valid_b = blk_ids[None] * SLC_BLOCK <= tq[:, None]
        score = jnp.where(valid_b, imp + FORCE_BONUS * forced, NEG_INF)
        _, idx = lax.top_k(score, n_sel)
        kg = ks_blk[b_ix, g_ix, idx]
        vg = vs_blk[b_ix, g_ix, idx]
        m_tok = n_sel * SLC_BLOCK
        kpos = idx[..., None] * SLC_BLOCK + jnp.arange(SLC_BLOCK)
        mask_s = (kpos <= tq[None, None, :, None, None]).reshape(B, N_KV_GROUPS, 1, Q_BLOCK, m_tok)
        s_s = jnp.einsum('bqghd,bgqnld->bghqnl', qg, kg).reshape(B, N_KV_GROUPS, HEADS_PER_GROUP, Q_BLOCK, m_tok)
        p_s = masked_softmax(s_s, mask_s)
        o_s = jnp.einsum('bghqm,bgqmd->bqghd', p_s.astype(vg.dtype),
                         vg.reshape(B, N_KV_GROUPS, Q_BLOCK, m_tok, HEAD_DIM))
        kw = lax.dynamic_slice_in_dim(kw_pad, start, Q_BLOCK + WINDOW, axis=1)
        vw = lax.dynamic_slice_in_dim(vw_pad, start, Q_BLOCK + WINDOW, axis=1)
        kp = start - WINDOW + jnp.arange(Q_BLOCK + WINDOW)
        dist = tq[:, None] - kp[None, :]
        mask_w = (dist >= 0) & (dist < WINDOW) & (kp[None, :] >= 0)
        s_w = jnp.einsum('bqghd,bkgd->bghqk', qg, kw)
        p_w = masked_softmax(s_w, mask_w)
        o_w = jnp.einsum('bghqk,bkgd->bqghd', p_w.astype(vw.dtype), vw)
        gc = gc.reshape(B, Q_BLOCK, N_KV_GROUPS, HEADS_PER_GROUP, N_NSA_BRANCHES)
        o = gc[..., 0:1] * o_c + gc[..., 1:2] * o_s + gc[..., 2:3] * o_w
        return o.reshape(B, Q_BLOCK, ATTN_WIDTH_2)

    n_q = S // Q_BLOCK
    q_chunks = q.reshape(B, n_q, Q_BLOCK, N_HEADS_2, HEAD_DIM).transpose(1, 0, 2, 3, 4)
    g_chunks = nsa_g.reshape(B, n_q, Q_BLOCK, N_HEADS_2, N_NSA_BRANCHES).transpose(1, 0, 2, 3, 4)
    starts = jnp.arange(n_q, dtype=jnp.int32) * Q_BLOCK
    out = lax.map(chunk, (q_chunks, g_chunks, starts))
    return out.transpose(1, 0, 2, 3).reshape(B, S, ATTN_WIDTH_2)

def token_mixer(h, w_in, pool_w, pool_scale, q_norm_w, k_norm_w, cmp_pos, cmp_w1, cmp_b1,
                cmp_w2, w_pool_br, w_attn_br, w_o):
    B, S, _ = h.shape
    z = h @ w_in
    u_pool = z[..., :OFF_Q]
    q = z[..., OFF_Q:OFF_KV].reshape(B, S, N_HEADS_2, HEAD_DIM)
    kv = z[..., OFF_KV:OFF_NSA_G].reshape(B, S, N_NSA_BRANCHES, 2, N_KV_GROUPS, HEAD_DIM)
    nsa_g = jax.nn.sigmoid(z[..., OFF_NSA_G:OFF_MERGE_G].astype(jnp.float32)).astype(h.dtype)
    nsa_g = nsa_g.reshape(B, S, N_HEADS_2, N_NSA_BRANCHES)
    merge_g = jax.nn.sigmoid(z[..., OFF_MERGE_G:].astype(jnp.float32)).astype(h.dtype)
    merge_g = merge_g.reshape(B, S, N_MERGE, D_MODEL)
    pos = jnp.arange(S)
    q = rope(rms_norm_2(q, q_norm_w), pos) * SCALE
    k = rope(rms_norm_2(kv[:, :, :, 0], k_norm_w[:, None, :]), pos)
    v = kv[:, :, :, 1]
    y_pool = pool_mixer(u_pool, pool_w, pool_scale) @ w_pool_br
    y_attn = nsa_attention(q, k, v, nsa_g, cmp_pos, cmp_w1, cmp_b1, cmp_w2) @ w_attn_br
    merged = merge_g[:, :, 0] * y_pool + merge_g[:, :, 1] * y_attn
    return merged @ w_o

def conv_ffn(h, w_up, conv_w, conv_b, w_down):
    S = h.shape[1]
    u = h @ w_up
    up = jnp.pad(u, ((0, 0), (CONV_WIDTH - 1, 0), (0, 0)))
    c = conv_b + conv_w[0] * up[:, 0:S]
    for tap in range(1, CONV_WIDTH):
        c = c + conv_w[tap] * up[:, tap:tap + S]
    gate, val = jnp.split(c, 2, axis=-1)
    return (jax.nn.silu(gate) * val) @ w_down

def second_inputs(seed: int = 0) -> dict:
    key = jax.random.key(seed)
    ks = jax.random.split(key, 20)
    f32 = jnp.float32
    nrm = lambda k, shape, s: jax.random.normal(k, shape, f32) * s
    L = DEPTH
    return {
        "x": jax.random.normal(ks[0], (BATCH, SEQ, D_MODEL), f32),
        "attn_norm_w": 1.0 + nrm(ks[1], (L, D_MODEL), 0.05),
        "w_in": nrm(ks[2], (L, D_MODEL, IN_WIDTH_2), D_MODEL ** -0.5),
        "pool_w": nrm(ks[3], (L, N_POOL_GROUPS, POOL_GROUP, POOL_GROUP), POOL_GROUP ** -0.5),
        "pool_scale": 1.0 + nrm(ks[4], (L, POOL_WIDTH), 0.1),
        "q_norm_w": 1.0 + nrm(ks[5], (L, HEAD_DIM), 0.05),
        "k_norm_w": 1.0 + nrm(ks[6], (L, N_NSA_BRANCHES, HEAD_DIM), 0.05),
        "cmp_pos": nrm(ks[7], (L, 2, CMP_BLOCK, HEAD_DIM), 0.5),
        "cmp_w1": nrm(ks[8], (L, 2, CMP_BLOCK * HEAD_DIM, CMP_HIDDEN), (CMP_BLOCK * HEAD_DIM) ** -0.5),
        "cmp_b1": nrm(ks[9], (L, 2, CMP_HIDDEN), 0.02),
        "cmp_w2": nrm(ks[10], (L, 2, CMP_HIDDEN, HEAD_DIM), CMP_HIDDEN ** -0.5),
        "w_pool_br": nrm(ks[11], (L, POOL_WIDTH, D_MODEL), POOL_WIDTH ** -0.5),
        "w_attn_br": nrm(ks[12], (L, ATTN_WIDTH_2, D_MODEL), ATTN_WIDTH_2 ** -0.5),
        "w_o": nrm(ks[13], (L, D_MODEL, D_MODEL), D_MODEL ** -0.5),
        "ffn_norm_w": 1.0 + nrm(ks[14], (L, D_MODEL), 0.05),
        "w_up": nrm(ks[15], (L, D_MODEL, 2 * D_FF), D_MODEL ** -0.5),
        "conv_w": nrm(ks[16], (L, CONV_WIDTH, 2 * D_FF), CONV_WIDTH ** -0.5),
        "conv_b": nrm(ks[17], (L, 2 * D_FF), 0.02),
        "w_down": nrm(ks[18], (L, D_FF, D_MODEL), D_FF ** -0.5),
    }

def second_block(x, attn_norm_w, w_in, pool_w, pool_scale, q_norm_w, k_norm_w, cmp_pos, cmp_w1,
              cmp_b1, cmp_w2, w_pool_br, w_attn_br, w_o, ffn_norm_w, w_up, conv_w, conv_b, w_down):
    for l in range(DEPTH):
        h = rms_norm_2(x, attn_norm_w[l])
        x = x + token_mixer(h, w_in[l], pool_w[l], pool_scale[l], q_norm_w[l], k_norm_w[l],
                            cmp_pos[l], cmp_w1[l], cmp_b1[l], cmp_w2[l], w_pool_br[l],
                            w_attn_br[l], w_o[l])
        h = rms_norm_2(x, ffn_norm_w[l])
        x = x + conv_ffn(h, w_up[l], conv_w[l], conv_b[l], w_down[l])
    return x


def setup_inputs(seed=0):
    out = dict(first_inputs(seed))
    for name, value in second_inputs(seed + 1).items():
        if name != "x":
            out[name + "_2"] = value
    return out


def reference(
    x, c, rel_bias, norm_g, w_ada, b_ada, w_in, q_gain, k_gain, a_re, a_im, log_dt, b_re, b_im,
    c_re, c_im, d_skip, w_glu, b_glu, w_out, attn_norm_w_2, w_in_2, pool_w_2, pool_scale_2,
    q_norm_w_2, k_norm_w_2, cmp_pos_2, cmp_w1_2, cmp_b1_2, cmp_w2_2, w_pool_br_2, w_attn_br_2,
    w_o_2, ffn_norm_w_2, w_up_2, conv_w_2, conv_b_2, w_down_2,
):
    x = first_block(
        x, c, rel_bias, norm_g, w_ada, b_ada, w_in, q_gain, k_gain, a_re, a_im, log_dt, b_re,
        b_im, c_re, c_im, d_skip, w_glu, b_glu, w_out,
    )
    return second_block(
        x, attn_norm_w_2, w_in_2, pool_w_2, pool_scale_2, q_norm_w_2, k_norm_w_2, cmp_pos_2,
        cmp_w1_2, cmp_b1_2, cmp_w2_2, w_pool_br_2, w_attn_br_2, w_o_2, ffn_norm_w_2, w_up_2,
        conv_w_2, conv_b_2, w_down_2,
    )


_drawn_inputs = setup_inputs


def setup_inputs(seed=0):
    import zlib

    import numpy as np

    out = dict(_drawn_inputs(seed))
    spreads = {}
    factors = {'rel_bias': 4.714,
     'norm_g': 7.694,
     'b_ada': 8.0,
     'q_gain': 8.0,
     'k_gain': 8.0,
     'a_re': 64.0,
     'a_im': 64.0,
     'log_dt': 64.0,
     'b_re': 64.0,
     'b_im': 64.0,
     'c_re': 64.0,
     'c_im': 64.0,
     'w_glu': 3.007,
     'b_glu': 64.0,
     'q_norm_w_2': 38.002,
     'k_norm_w_2': 42.723,
     'cmp_b1_2': 64.0,
     'conv_b_2': 33.856,
     'attn_norm_w_2': 4.286,
     'pool_scale_2': 8.0,
     'cmp_pos_2': 5.92,
     'cmp_w1_2': 3.41,
     'ffn_norm_w_2': 8.0}
    for name, (base, spread) in spreads.items():
        noise = np.random.default_rng([zlib.crc32(name.encode()), seed]).standard_normal(out[name].shape)
        drawn = base * np.exp(spread * noise) if base else spread * noise
        out[name] = __import__('jax').numpy.asarray(drawn.astype(out[name].dtype))
    for name, factor in factors.items():
        out[name] = (out[name] * factor).astype(out[name].dtype)
    return out
```

```python
import math
from contextlib import ExitStack

import numpy as np

import concourse.bass as bass
from concourse import mybir

S = 512
D = 1024
KT = D // 128
TT = S // 128
NEG = -1.0e30
SCORE_MASK = -1.0e30
TAKEN = -3.0e38
EPS = 1e-6
TOPK = min(256, S // 4)
G, GC, ST = 32, 16, 64
L = 8
NCH = S // L
QG = 8
NQ = G // QG
W_IN1 = 3656
W_IN2 = 4400
OFF_KV, OFF_NG, OFF_MG = 1536, 2304, 2352
NCMP = 31
DFF = 2752
FT = 22
SQ2PI = math.sqrt(2.0 / math.pi)


def program(nc, x, c, rel_bias, norm_g, w_ada, b_ada, w_in, q_gain, k_gain, a_re, a_im, log_dt,
            b_re, b_im, c_re, c_im, d_skip, w_glu, b_glu, w_out, attn_norm_w_2, w_in_2, pool_w_2,
            pool_scale_2, q_norm_w_2, k_norm_w_2, cmp_pos_2, cmp_w1_2, cmp_b1_2, cmp_w2_2,
            w_pool_br_2, w_attn_br_2, w_o_2, ffn_norm_w_2, w_up_2, conv_w_2, conv_b_2, w_down_2,
            k_ident, k_bucket, k_tri, k_rope, k_cmpmask, k_rowvalid, k_cnt, k_flip, out):
    f32 = mybir.dt.float32
    i32 = mybir.dt.int32
    ALU = mybir.AluOpType
    ACT = mybir.ActivationFunctionType
    X = mybir.AxisListType.X
    ctx = ExitStack()
    with ctx:
        def sem(name):
            return ctx.enter_context(nc.semaphore(name))

        ARENA = 53200
        arena = ctx.enter_context(nc.sbuf_tensor("arena", [128, ARENA], f32))
        bank = [ctx.enter_context(nc.psum_tensor(f"bank{i}", [128, 512], f32)) for i in range(8)]

        class Zone:
            def __init__(self, at, end=ARENA):
                self.at, self.end = at, end

            def take(self, words, *shape):
                a = arena[:, self.at:self.at + words]
                self.at += words
                assert self.at <= self.end, (self.at, self.end)
                if len(shape) > 1:
                    names = "abcd"[:len(shape)]
                    a = a.rearrange(f"p ({' '.join(names)}) -> p {' '.join(names)}",
                                    **{n: s for n, s in zip(names, shape)})
                return a

        z = Zone(0)
        slot = [z.take(4096) for _ in range(2)]
        XROW0 = z.at
        xrow = z.take(4096, TT, D)
        hT = z.take(4096, KT, S)
        ident = z.take(128)
        trim = z.take(512)
        tri = trim[:, 384:512]
        ropeT = z.take(TT * 64, TT, 2, 32)
        cmpmask = z.take(TT * 32, TT, 32)
        rowvalid = z.take(TT)
        cnt = z.take(64, 4, 16)
        colv = z.take(64)
        colr = z.take(128)
        modc = z.take(40)
        silc = z.take(16)
        stat = z.take(192)
        sml = z.take(64)
        halves = z.take(32)
        gains = z.take(384)
        BASE = z.at

        z = Zone(BASE)
        u = z.take(2048, TT, S)
        sz = z.take(2048, TT, S)
        yT = z.take(2048, TT, S)
        qiT = z.take(2048, TT, S)
        kiT = z.take(512)
        wi = z.take(32, TT, 8)
        score = z.take(2048, TT, S)
        reluq = z.take(1024, 2, S)
        row = z.take(2048, TT, 512)
        kT = z.take(2048, TT, S)
        qT = z.take(2048, TT, S)
        v1 = z.take(2048, TT, 512)
        sqt = reluq[:, 0, :]
        U = arena[:, XROW0:XROW0 + 2048].rearrange("p (a b) -> p a b", a=G)
        az = arena[:, XROW0 + 2048:XROW0 + 4096].rearrange("p (a b) -> p a b", a=TT)
        zq = Zone(z.at - 2048 - 2048)
        onehot, rb_row, rb_in = zq.take(640), zq.take(640), zq.take(8)
        SSM0 = z.at
        X1, X2 = z.take(512, G, GC), z.take(512, G, GC)
        Y1, Y2 = z.take(512, G, GC), z.take(512, G, GC)
        pw = z.take(2 * 9 * 32, 2, 9, 32)
        sp = z.take(32 * 32, 32, 32)
        CL = z.take(QG * 9 * GC, QG, 9, GC)
        Zt = z.take(1024, QG, L, GC)
        Tm = z.take(1024, QG, 128)
        Wn = z.take(1024, QG, 128)
        KX0 = z.at
        Kx = z.take(QG * 240, QG, 240)
        E1, E2 = z.take(512, QG, NCH), z.take(512, QG, NCH)
        Vb, Vs = z.take(512, QG, NCH), z.take(512, QG, NCH)
        r8 = z.take(512, QG, NCH)
        G0 = z.at
        g1, g2 = z.take(1152), z.take(1152)
        zq = Zone(KX0)
        craw, lraw = zq.take(1024, 2, 4, 128), zq.take(256, 2, 128)
        zq = Zone(G0)
        bre, bim = zq.take(512, G, GC), zq.take(512, G, GC)
        END1 = z.at

        z = Zone(SSM0)
        biasT = z.take(4096, 8, 512)
        biasR = arena[:, z.at:z.at + 4096].rearrange("p (a b) -> p a b", a=8)
        mb = z.take(1024, 2, 512)
        lg = z.take(1024, 2, 512)
        pr = z.take(1024, 2, 512)
        pT = z.take(1024, 2, 512)
        zz = z.take(2048, TT, S)
        gt = z.take(1024, 2, 512)
        gate_b = z.take(1024)
        badr = z.take(1024)
        silb = z.take(1024, KT, 128)
        orow, oT = row, qiT

        z = Zone(BASE)
        upT = z.take(2048, 4, S)
        plT = z.take(2048, 4, S)
        ypT = z.take(2048, 4, S)
        pwS = z.take(512, 4, 128)
        row2 = z.take(2048, TT, 512)
        tmp2 = z.take(1024)
        qT2 = z.take(4096, 8, S)
        ksT = z.take(2048, 4, S)
        kcT = z.take(1024, 2, S)
        vs2 = z.take(1024, 2, TT, 128)
        ngs = z.take(TT * 48, TT, 48)
        posr, posT = z.take(64), z.take(64, 2, 32)
        w2s = z.take(192)
        hid = z.take(256, 4, 64)
        kcmp = z.take(64, 2, 32)
        vbd = z.take(512, 2, 256)
        pc = row2[:, 0:2, :]
        pTc = row2[:, 2, :]
        pr2 = z.take(2048, 2, 2, 512)
        pT2 = z.take(2048, 2, 2, 512)
        OB0 = z.at
        ob = z.take(4096, TT, D)
        mg = z.take(4096, TT, D)
        END2 = z.at
        oT2 = qT2
        xn2 = ob
        kvr = arena[:, OB0:OB0 + 2048].rearrange("p (a b) -> p a b", a=TT)
        kdup = arena[:, OB0 + 2048:OB0 + 4096].rearrange("p (a b) -> p a b", a=TT)
        q2b = arena[:, OB0 + 4096:OB0 + 6144].rearrange("p (a b) -> p a b", a=TT)
        mT = hT

        z = Zone(BASE)
        aT = z.take(FT * 512, FT, S)
        cvw = z.take(2 * 88, 2, 4, FT)
        cvr = z.take(2 * 128, 2, 128)
        fc = z.take(4 * 512, 2, 2, 512)
        ft = z.take(2 * 512, 2, 512)
        xn3 = arena[:, BASE:BASE + 4096].rearrange("p (a b) -> p a b", a=TT)


        PROJ, AUX = {}, {}

        def name_proj(*names):
            for n in names:
                PROJ[n] = len(PROJ)

        def name_aux(*names):
            for n in names:
                AUX[n] = len(AUX)

        def four(name):
            return [(name, t) for t in range(TT)]

        def ssm_names(q):
            return [("k", q, 0), ("k", q, 1), ("z", q, 0), ("z", q, 1)]

        name_aux("cols", "lam", "c1", "c2", "rb", "rb2", "mod", *[("x", k) for k in range(KT)])
        name_proj(*four("u"))
        name_aux(*ssm_names(0))
        name_proj(*four("qi"))
        name_aux(("v", 0))
        name_proj("ki", "wi")
        name_aux(("y", 0), *[("rel", i, h) for i in range(1, TT) for h in range(8)], *ssm_names(1))
        name_proj(*four("k"))
        name_aux(("v", 1), *four("kt"), ("y", 1))
        name_proj(*four("q"))
        name_aux(*ssm_names(2), *four("qt"), ("v", 2))
        name_proj(*four("v"))
        name_aux(("y", 2), *ssm_names(3))
        name_proj(*four("z"))
        name_aux(("v", 3))
        name_proj(*four("az"))
        name_aux(("y", 3))
        name_proj("gate0", "gate1")
        name_aux(*[("flip", h) for h in range(8)])
        UNITS1 = [(i, h) for i in range(TT) for h in range(8)]
        NU1 = len(UNITS1)
        for n in range(NU1 + 2):
            for kind, m in (("qk", n), ("pt", n - 1), ("pv", n - 2)):
                if 0 <= m < NU1:
                    name_aux((kind, m))
        name_proj(*four("glu"))
        name_aux(*four("ot"))
        name_proj(*four("out0"), *four("out1"))
        name_aux(*[("h2", k) for k in range(KT)], "pos")
        name_proj(*four("up"), *four("kv1"), *four("kv2"), *four("q2a"))
        name_aux(*[("ks", n) for n in range(4)], ("kc", 0), ("kc", 1))
        name_aux(*[("hid", a, g) for a in range(2) for g in range(2)])
        name_proj(*four("q2b"))
        name_aux(*[("qt2", m) for m in range(4)], "kcm", "vcm")
        name_proj(*four("m00"))
        name_aux(*[("qt2", m) for m in range(4, 8)])
        name_proj(*four("ypm"), *four("yp0"), *four("m01"), *four("yp1"))
        for i in range(TT + 1):
            if i < TT:
                name_aux(("cq", i, 0), ("cq", i, 1))
            if i >= 1:
                name_aux(("cp", i - 1), ("cv", i - 1, 0), ("cv", i - 1, 1))
        UNITS2 = [(i, h) for i in range(TT) for h in range(16)]
        NU2 = len(UNITS2)
        for n in range(NU2 + 2):
            if n < NU2:
                name_aux(("qs", n), ("qw", n))
            if 0 <= n - 1 < NU2:
                name_aux(("ps", n - 1), ("pw", n - 1))
            if 0 <= n - 2 < NU2:
                name_aux(("pv2", n - 2))
        name_proj(*four("m10"))
        name_aux(*[("o2", m) for m in range(8)])
        name_proj(*four("ya0"), *four("m11"), *four("ya1"))
        name_aux(*[("mt", m) for m in range(8)])
        name_proj(*four("wo0"), *four("wo1"))
        name_aux(("cvt", 0), ("cvt", 1), *[("h3", k) for k in range(KT)])
        for j in range(FT):
            name_proj(("fg", j), ("fv", j))
        for a in range(2):
            name_proj(*four(f"dn{a}"))

        proj_done, aux_done = sem("proj_done"), sem("aux_done")
        proj_free = [sem(f"proj_free{b}") for b in range(4)]
        aux_free = [sem(f"aux_free{b}") for b in range(4)]

        def pbank(name):
            return bank[PROJ[name] % 4]

        def abank(name):
            return bank[4 + AUX[name] % 4]

        def proj_ready(eng, name):
            eng.wait_ge(proj_done, PROJ[name] + 1)

        def aux_ready(eng, name):
            eng.wait_ge(aux_done, AUX[name] + 1)

        def proj_out(eng, name):
            eng.wait_ge(proj_free[PROJ[name] % 4], PROJ[name] // 4 + 1)

        def aux_out(eng, name):
            eng.wait_ge(aux_free[AUX[name] % 4], AUX[name] // 4 + 1)

        def pfree(name):
            return proj_free[PROJ[name] % 4]

        def afree(name):
            return aux_free[AUX[name] % 4]

        def cols_of(w, k0, k1, c0, c1):
            return w[0, k0 * 128:k1 * 128, c0:c1].rearrange("(k p) n -> p k n", p=128)

        def slot_view(s, kt, n):
            return slot[s][:, 0:kt * n].rearrange("p (k n) -> p k n", k=kt)

        CHUNKS = []

        def chunk(name, last, kt, n, parts):
            CHUNKS.append((name, last, kt, n, parts))

        for j in range(4):
            chunk(("ada", j), ("used", j + 1) if j < 3 else ("aux", "mod"), KT, 512, [(0, 512, lambda j=j: cols_of(w_ada, 0, KT, 512 * j, 512 * j + 512))])

        def w1chunk(name, last, c0):
            chunk(name, ("proj", last), KT, 512, [(0, 512, lambda: cols_of(w_in, 0, KT, c0, c0 + 512))])

        w1chunk("u", ("u", 3), 0)
        w1chunk("qi", ("qi", 3), 3072)
        chunk("ki", ("proj", "wi"), KT, 136,
              [(0, 64, lambda: cols_of(w_in, 0, KT, 3584, 3648)),
               (64, 136, lambda: cols_of(w_in, 0, KT, 3584, 3656))])
        for name, c0 in (("k", 1536), ("q", 1024), ("v", 2048), ("z", 512), ("az", 2560)):
            w1chunk(name, (name, 3), c0)
        for j in range(2):
            chunk(("gate", j), ("proj", f"gate{j}"), KT, 512,
                  [(0, 512, lambda j=j: cols_of(w_ada, 0, KT, 2048 + 512 * j, 2560 + 512 * j))])
        chunk("glu", ("proj", ("glu", 3)), 4, 512, [(0, 512, lambda: cols_of(w_glu, 0, 4, 0, 512))])
        for j in range(2):
            chunk(("out", j), ("proj", (f"out{j}", 3)), KT, 512,
                  [(0, 512, lambda j=j: cols_of(w_out, 0, KT, 512 * j, 512 * j + 512))])
        def wchunk(name, last, w, kt, c0, n=512):
            chunk(name, ("proj", last), kt, n, [(0, n, lambda: cols_of(w, 0, kt, c0, c0 + n))])

        wchunk("up", ("up", 3), w_in_2, KT, 0)
        wchunk("kv1", ("kv1", 3), w_in_2, KT, OFF_KV)
        wchunk("kv2", ("kv2", 3), w_in_2, KT, OFF_KV + 512, 304)
        wchunk("q2a", ("q2a", 3), w_in_2, KT, 512)
        for a in range(2):
            src = cmp_w1_2[0, a].rearrange("(l d) n -> d l n", d=64)
            chunk(("c1", a), ("aux", ("hid", a, 1)), 32, 128,
                  [(None, slice(0, 64), lambda src=src: src), (None, slice(64, 128), lambda src=src: src)])
        wchunk("q2b", ("q2b", 3), w_in_2, KT, 1024)
        wchunk("m00", ("m00", 3), w_in_2, KT, OFF_MG)
        wchunk("yp0", ("yp0", 3), w_pool_br_2, 4, 0)
        wchunk("m01", ("m01", 3), w_in_2, KT, OFF_MG + 512)
        wchunk("yp1", ("yp1", 3), w_pool_br_2, 4, 512)
        wchunk("m10", ("m10", 3), w_in_2, KT, OFF_MG + 1024)
        wchunk("ya0", ("ya0", 3), w_attn_br_2, KT, 0)
        wchunk("m11", ("m11", 3), w_in_2, KT, OFF_MG + 1536)
        wchunk("ya1", ("ya1", 3), w_attn_br_2, KT, 512)
        wchunk("wo0", ("wo0", 3), w_o_2, KT, 0)
        wchunk("wo1", ("wo1", 3), w_o_2, KT, 512)
        for J in range(FT // 2):
            n = 256 if J < FT // 2 - 1 else 192
            chunk(("f", J), ("proj", ("fv", 2 * J + 1)), KT, 512,
                  [(0, n, lambda J=J, n=n: cols_of(w_up_2, 0, KT, 256 * J, 256 * J + n)),
                   (256, 256 + n, lambda J=J, n=n: cols_of(w_up_2, 0, KT, DFF + 256 * J, DFF + 256 * J + n))])
        for a in range(2):
            for b in range(3):
                last = ("used", 4 + 2 * a + b) if b < 2 else ("proj", (f"dn{a}", 3))
                if b < 2:
                    parts = [(0, 512, lambda a=a, b=b: cols_of(w_down_2, 8 * b, 8 * b + 8, 512 * a, 512 * a + 512))]
                else:
                    parts = [("down", a, None)]
                chunk(("d", a, b), last, 8 if b < 2 else 6, 512, parts)
        slot_full = [sem("slot0_full"), sem("slot1_full")]
        CH, count = {}, [0, 0]
        for n, (name, last, kt, cols, parts) in enumerate(CHUNKS):
            count[n % 2] += 16 * (2 if parts[0][0] == "down" else len(parts))
            CH[name] = (n % 2, count[n % 2], kt, cols)

        def weights(eng, name):
            s, full, kt, n = CH[name]
            eng.wait_ge(slot_full[s], full)
            return slot_view(s, kt, n)

        u_dram = nc.dram_tensor("u_dram", (G, GC, L, NCH), f32).ap()
        y_dram = nc.dram_tensor("y_dram", (G, GC, L, NCH), f32).ap()
        rb_dram = nc.dram_tensor("rb_dram", (8, 640), f32).ap()

        names = """x_in consts_in rows_in lam_in craw_in b_in ldt_in gains_in rb_in_s onehot_in
            vec_step act_step pool_step silc_done mod_done rows_done xn_done
            prep_x prep_y pool_ones u_ready u_saved U_in cl_done zt_done t_in v_swapped
            rot_done scan_done w_swapped s_done y_saved y_back rbrow_done rb_saved bias_in
            rel_used topk_done knorm_done qnorm_done lg_done exp_done mb_done mb_used
            o_done x_again z_done silb_done y_skip y_tanh gbias_done ys_done out_tanh badr_in x1_done
            az_tanh sz_tanh ms_done root_done rb_one""".split()
        S_ = {n: sem(n) for n in names}
        (x_in, consts_in, rows_in, lam_in, craw_in, b_in, ldt_in, gains_in, rb_in_s, onehot_in,
         vec_step, act_step, pool_step, silc_done, mod_done, rows_done, xn_done,
         prep_x, prep_y, pool_ones, u_ready, u_saved, U_in, cl_done, zt_done, t_in, v_swapped,
         rot_done, scan_done, w_swapped, s_done, y_saved, y_back, rbrow_done, rb_saved, bias_in,
         rel_used, topk_done, knorm_done, qnorm_done, lg_done, exp_done, mb_done, mb_used,
         o_done, x_again, z_done, silb_done, y_skip, y_tanh, gbias_done, ys_done, out_tanh, badr_in,
         x1_done, az_tanh, sz_tanh, ms_done, root_done, rb_one) = [S_[n] for n in names]

        class Steps:
            def __init__(self, eng, s):
                self.eng, self.s, self.n = eng, s, 0

            def __call__(self, ins):
                self.n += 1
                ins.then_inc(self.s, 1)
                self.eng.wait_ge(self.s, self.n)

        act_tanhc, consts_in2, chunk_used, rbtmp, out_done = [
            sem(n) for n in ("act_tanhc", "consts_in2", "chunk_used", "rbtmp", "out_done")]
        (small_in, krope_done, qrope_done, hid_done, pooled_done, cexp_done, exp2_done, o2_done, mg_done, conv_in,
         act_done, hid_in, hid_tanh, clg_done, lg2_done, cvw_done, tap_done, gatec_done, ftanh_done, pw_in, x2_done,
         x3_done, kgain_done, qgain_done, ngs_done, kdup_done) = [sem(n) for n in """small_in krope_done qrope_done hid_done
            pooled_done cexp_done exp2_done o2_done mg_done conv_in act_done hid_in hid_tanh clg_done lg2_done cvw_done
            tap_done gatec_done ftanh_done pw_in x2_done x3_done kgain_done qgain_done ngs_done kdup_done""".split()]

        def by_rows(a):
            return a.rearrange("a (n p) -> (a n) p", p=128)

        ROWS = [(0, 8, by_rows(c)), (8, 8, by_rows(norm_g)), (16, 16, by_rows(b_ada[:, 0:2048])),
                (32, 8, by_rows(attn_norm_w_2)), (40, 8, by_rows(ffn_norm_w_2)), (48, 4, by_rows(d_skip)),
                (52, 4, by_rows(b_glu)), (56, 4, by_rows(pool_scale_2)), (60, 2, cmp_b1_2[0])]
        NROWS = len(ROWS)
        GAINS = [q_gain[0:1, :], k_gain[0:1, :], q_norm_w_2[0:1, :], k_norm_w_2[0, 0:1, :],
                 k_norm_w_2[0, 1:2, :], k_norm_w_2[0, 2:3, :]]

        block = ctx.enter_context(nc.Block())

        CV_C, CV_G, CV_ADA, CV_G2, CV_GF, CV_SKIP, CV_BGLU, CV_PS, CV_B1 = 0, 8, 16, 32, 40, 48, 52, 56, 60
        gq1, gk1 = gains[:, 0:64], gains[:, 64:128]

        @block.sync
        def _(sp_):
            sp_.dma_start(xrow, x[0].rearrange("(t p) d -> p t d", p=128)).then_inc(x_in, 16)
            for n, (name, last, kt, cols, parts) in enumerate(CHUNKS):
                if n >= 2:
                    kind, res = CHUNKS[n - 2][1]
                    if kind == "used":
                        sp_.wait_ge(chunk_used, res)
                    elif kind == "aux":
                        sp_.wait_ge(aux_done, AUX[res] + 1)
                    else:
                        sp_.wait_ge(proj_done, PROJ[res] + 1)
                w = slot_view(n % 2, kt, cols)
                for c0, c1, src in parts:
                    if c0 is None:
                        sp_.dma_start(w[c1, :, :], src()).then_inc(slot_full[n % 2], 16)
                    elif c0 == "down":
                        wd = w_down_2[0, 2048:DFF, 512 * c1:512 * c1 + 512]
                        sp_.dma_start(w[:, 0:5, :], wd[0:640, :].rearrange("(k p) n -> p k n", p=128))\
                           .then_inc(slot_full[n % 2], 16)
                        sp_.dma_start(w[0:64, 5, :], wd[640:704, :]).then_inc(slot_full[n % 2], 16)
                    else:
                        sp_.dma_start(w[:, :, c0:c1], src()).then_inc(slot_full[n % 2], 16)
            for n in range(8):
                a, t = n // 4, n % 4
                sp_.wait_ge(x3_done, n + 1)
                sp_.dma_start(out[0, 128 * t:128 * t + 128, 512 * a:512 * a + 512],
                              xrow[:, t, 512 * a:512 * a + 512]).then_inc(out_done, 16)
            sp_.wait_ge(out_done, 128)

        @block.tensor
        def _(pe):
            seen = [0, 0]

            def begin_aux(name):
                a = AUX[name]
                assert a == seen[0], (name, a, seen)
                seen[0] += 1
                if a >= 4:
                    pe.wait_ge(aux_free[a % 4], a // 4)
                return bank[4 + a % 4]

            def begin_proj(name):
                p = PROJ[name]
                assert p == seen[1], (name, p, seen)
                seen[1] += 1
                if p >= 4:
                    pe.wait_ge(proj_free[p % 4], p // 4)
                return bank[p % 4]

            def proj_rows(name, chunk_name, act, n=512):
                w = weights(pe, chunk_name)
                kt = w.shape[1]
                for t in range(TT):
                    ps = begin_proj((name, t))
                    for k in range(kt):
                        mm = pe.matmul(ps[:, 0:n], act[:, k, 128 * t:128 * t + 128], w[:, k, 0:n],
                                       start=(k == 0), stop=(k == kt - 1))
                    mm.then_inc(proj_done, 1)

            def proj_cols(name, chunk_name, act):
                w = weights(pe, chunk_name)
                kt = w.shape[1]
                for j in range(4):
                    ps = begin_proj((name, j))
                    for k in range(kt):
                        mm = pe.matmul(ps[:, :], w[:, k, 128 * j:128 * j + 128], act[:, k, :],
                                       start=(k == 0), stop=(k == kt - 1))
                    mm.then_inc(proj_done, 1)

            def turn(name, blocks):
                ps = begin_aux(name)
                at = 0
                for b in blocks:
                    p, f = b.shape[0], int(np.prod(b.shape[1:]))
                    mm = pe.transpose(ps[0:f, at:at + p], b, ident[0:p, 0:p])
                    at += p
                mm.then_inc(aux_done, 1)

            pe.wait_ge(consts_in, 16)
            pe.wait_ge(rows_in, 16 * NROWS)
            turn("cols", [colr[0:62, :]])
            pe.wait_ge(lam_in, 64)
            turn("lam", [lraw[0:32, 0, :], lraw[0:32, 1, :]])
            pe.wait_ge(craw_in, 64)
            for a in range(2):
                turn(f"c{a + 1}", [craw[:, a, m, :] for m in range(4)])
            pe.wait_ge(rb_in_s, 16)
            pe.wait_ge(rb_one, 1)
            pe.wait_ge(onehot_in, 16)
            for name, c0, n in (("rb", 0, 512), ("rb2", 512, 128)):
                pe.matmul(begin_aux(name)[0:8, 0:n], rb_in[0:33, :], onehot[0:33, c0:c0 + n],
                          start=True, stop=True).then_inc(aux_done, 1)
            pe.wait_ge(silc_done, 1)
            ps = begin_aux("mod")
            for j in range(4):
                w = weights(pe, ("ada", j))
                for m in range(4):
                    for k in range(KT):
                        mm = pe.matmul(ps[:, 4 * j + m:4 * j + m + 1], w[:, k, 128 * m:128 * m + 128],
                                       silc[:, k:k + 1], start=(k == 0), stop=(k == KT - 1))
                if j < 3:
                    mm.then_inc(chunk_used, 1)
                else:
                    mm.then_inc(aux_done, 1)

            def x_turns(key, src, ready):
                pe.wait_ge(*ready)
                for k in range(KT):
                    turn((key, k), [src[:, t, 128 * k:128 * k + 128] for t in range(TT)])

            x_turns("x", xrow, (xn_done, TT))

            def ssm_kernels(q):
                pe.wait_ge(cl_done, q + 1)
                if q == 0:
                    pe.wait_ge(prep_y, 1)
                for a in range(2):
                    ps = begin_aux(("k", q, a))
                    for b in range(4):
                        g = 4 * a + b
                        mm = pe.matmul(ps[0:GC, 128 * b:128 * b + 128], Y1[:, QG * q + g, :],
                                       CL[:, g, 0:L, :].rearrange("p a b -> p (a b)"), start=True, stop=True)
                    mm.then_inc(aux_done, 1)
                pe.wait_ge(zt_done, q + 1)
                for a in range(2):
                    turn(("z", q, a), [Zt[:, 4 * a + b, :, :].rearrange("p a b -> p (a b)") for b in range(4)])

            def ssm_chunks(q):
                pe.wait_ge(U_in, 16 * L)
                aux_out(pe, ("z", q, 0))
                aux_out(pe, ("z", q, 1))
                ps = begin_aux(("v", q))
                for g in range(QG):
                    mm = pe.matmul(ps[:, NCH * g:NCH * g + NCH], Wn[:, g, :], U[:, QG * q + g, :],
                                   start=True, stop=True)
                mm.then_inc(aux_done, 1)

            def ssm_out(q):
                pe.wait_ge(t_in, 16 * L * (q + 1))
                pe.wait_ge(s_done, q + 1)
                ps = begin_aux(("y", q))
                for g in range(QG):
                    pe.matmul(ps[:, NCH * g:NCH * g + NCH], Tm[:, g, :], U[:, QG * q + g, :],
                              start=True, stop=False)
                    mm = pe.matmul(ps[:, NCH * g + 1:NCH * g + NCH],
                                   CL[:, g, 1:L + 1, :].rearrange("p a b -> p (a b)"), Vb[:, g, 0:NCH - 1],
                                   start=False, stop=True)
                mm.then_inc(aux_done, 1)

            for k in range(KT):
                aux_out(pe, ("x", k))
            proj_cols("u", "u", hT)
            ssm_kernels(0)
            proj_cols("qi", "qi", hT)
            ssm_chunks(0)
            w = weights(pe, "ki")
            ps = begin_proj("ki")
            for k in range(KT):
                mm = pe.matmul(ps[:, :], w[:, k, 0:128], hT[:, k, :], start=(k == 0), stop=(k == KT - 1))
            mm.then_inc(proj_done, 1)
            ps = begin_proj("wi")
            for t in range(TT):
                for k in range(KT):
                    mm = pe.matmul(ps[:, 8 * t:8 * t + 8], hT[:, k, 128 * t:128 * t + 128], w[:, k, 128:136],
                                   start=(k == 0), stop=(k == KT - 1))
            mm.then_inc(proj_done, 1)
            ssm_out(0)
            proj_out(pe, ("qi", 3))
            proj_out(pe, ("qi", 2))
            proj_out(pe, ("qi", 1))
            proj_out(pe, ("qi", 0))
            proj_out(pe, "ki")
            for i in range(1, TT):
                for h in range(8):
                    r = 64 * (h % 2)
                    n = 128 * (i + 1)
                    pe.matmul(begin_aux(("rel", i, h))[:, 0:n], qiT[r:r + 64, h // 2, 128 * i:128 * i + 128],
                              kiT[r:r + 64, 0:n], start=True, stop=True).then_inc(aux_done, 1)
            ssm_kernels(1)
            proj_rows("k", "k", hT)
            ssm_chunks(1)
            pe.wait_ge(knorm_done, TT)
            for m in range(4):
                turn(("kt", m), [row[:, t, 128 * m:128 * m + 128] for t in range(TT)])
            ssm_out(1)
            proj_rows("q", "q", hT)
            ssm_kernels(2)
            pe.wait_ge(qnorm_done, TT)
            for m in range(4):
                turn(("qt", m), [row[:, t, 128 * m:128 * m + 128] for t in range(TT)])
            ssm_chunks(2)
            proj_rows("v", "v", hT)
            ssm_out(2)
            ssm_kernels(3)
            proj_cols("z", "z", hT)
            ssm_chunks(3)
            proj_rows("az", "az", hT)
            ssm_out(3)
            pe.wait_ge(silb_done, 1)
            for j in range(2):
                w = weights(pe, ("gate", j))
                ps = begin_proj(f"gate{j}")
                for k in range(KT):
                    mm = pe.matmul(ps[:, :], silb[:, k, :], w[:, k, :], start=(k == 0), stop=(k == KT - 1))
                mm.then_inc(proj_done, 1)

            pe.wait_ge(bias_in, 32)
            for h in range(8):
                pe.matmul(begin_aux(("flip", h))[:, :], gt[:, 0, 0:128], biasR[:, h, :],
                          start=True, stop=True).then_inc(aux_done, 1)
            for m in range(4):
                aux_out(pe, ("kt", m))
                aux_out(pe, ("qt", m))
                proj_out(pe, ("v", m))
            for n in range(NU1 + 2):
                if n < NU1:
                    i, h = UNITS1[n]
                    r = 64 * (h % 2)
                    pe.matmul(begin_aux(("qk", n))[:, 0:128 * (i + 1)],
                              qT[r:r + 64, h // 2, 128 * i:128 * i + 128],
                              kT[r:r + 64, h // 2, 0:128 * (i + 1)], start=True, stop=True).then_inc(aux_done, 1)
                if 0 <= n - 1 < NU1:
                    i, h = UNITS1[n - 1]
                    pe.wait_ge(exp_done, n)
                    turn(("pt", n - 1), [pr[:, (n - 1) % 2, 128 * b:128 * b + 128] for b in range(i + 1)])
                if 0 <= n - 2 < NU1:
                    i, h = UNITS1[n - 2]
                    aux_out(pe, ("pt", n - 2))
                    ps = begin_aux(("pv", n - 2))
                    for b in range(i + 1):
                        mm = pe.matmul(ps[:, 0:64], pT[:, (n - 2) % 2, 128 * b:128 * b + 128],
                                       v1[:, b, 64 * h:64 * h + 64], start=(b == 0), stop=(b == i))
                    mm.then_inc(aux_done, 1)
            pe.wait_ge(z_done, TT)
            proj_cols("glu", "glu", zz)
            pe.wait_ge(o_done, NU1)
            for m in range(4):
                turn(("ot", m), [orow[:, t, 128 * m:128 * m + 128] for t in range(TT)])
            pe.wait_ge(ys_done, TT)
            for m in range(4):
                aux_out(pe, ("ot", m))
            for j in range(2):
                w = weights(pe, ("out", j))
                for t in range(TT):
                    ps = begin_proj((f"out{j}", t))
                    for k in range(KT):
                        a = yT[:, k, :] if k < 4 else oT[:, k - 4, :]
                        mm = pe.matmul(ps[:, :], a[:, 128 * t:128 * t + 128], w[:, k, :],
                                       start=(k == 0), stop=(k == KT - 1))
                    mm.then_inc(proj_done, 1)

            x_turns("h2", xn2, (xn_done, 2 * TT))
            pe.wait_ge(small_in, 16 * 4)
            turn("pos", [posr[0:64, :]])
            for k in range(KT):
                aux_out(pe, ("h2", k))
            proj_cols("up", "up", hT)
            proj_rows("kv1", "kv1", hT)
            proj_rows("kv2", "kv2", hT, 304)
            proj_rows("q2a", "q2a", hT)
            pe.wait_ge(kdup_done, TT)
            for n in range(4):
                turn(("ks", n), [kdup[:, t, 128 * n:128 * n + 128] for t in range(TT)])
            turn(("kc", 0), [kvr[:, t, 0:128] for t in range(TT)])
            turn(("kc", 1), [kvr[:, t, 128:256] for t in range(TT)])
            aux_out(pe, "pos")
            for a in range(2):
                w = weights(pe, ("c1", a))
                aux_out(pe, ("kc", a))
                for g in range(2):
                    r = slice(64 * g, 64 * g + 64)
                    ps = begin_aux(("hid", a, g))
                    for l in range(32):
                        mm = pe.matmul(ps[:, 0:NCMP], w[r, l, :], kcT[r, a, l:l + 16 * (NCMP - 1) + 1:16],
                                       start=(l == 0), stop=(l == 31))
                    if g == 0:
                        for l in range(32):
                            mm = pe.matmul(ps[:, 31:32], w[r, l, :], posT[r, a, l:l + 1],
                                           start=(l == 0), stop=(l == 31))
                    mm.then_inc(aux_done, 1)
            proj_rows("q2b", "q2b", hT)
            pe.wait_ge(qrope_done, TT)
            for m in range(4):
                turn(("qt2", m), [row2[:, t, 128 * m:128 * m + 128] for t in range(TT)])
            pe.wait_ge(hid_done, 2)
            ps = begin_aux("kcm")
            for g in range(2):
                mm = pe.matmul(ps[:, 32 * g:32 * g + NCMP], w2s[:, 0:128], hid[:, 0, 32 * g:32 * g + NCMP],
                               start=True, stop=True)
            mm.then_inc(aux_done, 1)
            ps = begin_aux("vcm")
            for r in range(4):
                for g in range(2):
                    mm = pe.matmul(ps[32 * r:32 * r + NCMP, 64 * g:64 * g + 64], hid[:, 1, 32 * g:32 * g + NCMP],
                                   w2s[:, 128:192], start=True, stop=True)
            mm.then_inc(aux_done, 1)
            proj_rows("m00", "m00", hT)
            pe.wait_ge(qrope_done, 2 * TT)
            for m in range(4):
                turn(("qt2", 4 + m), [q2b[:, t, 128 * m:128 * m + 128] for t in range(TT)])
            pe.wait_ge(pooled_done, 4)
            pe.wait_ge(pw_in, 16)
            for j in range(4):
                pe.matmul(begin_proj(("ypm", j))[:, :], pwS[:, j, :], plT[:, j, :], start=True, stop=True)\
                    .then_inc(proj_done, 1)
            for j in range(4):
                proj_out(pe, ("ypm", j))
            proj_rows("yp0", "yp0", ypT)
            proj_rows("m01", "m01", hT)
            proj_rows("yp1", "yp1", ypT)
            for m in range(8):
                aux_out(pe, ("qt2", m))
            for n in range(4):
                aux_out(pe, ("ks", n))
            aux_out(pe, "kcm")
            aux_out(pe, "vcm")
            for i in range(TT + 1):
                if i < TT:
                    for odd in range(2):
                        r = slice(64 * odd, 64 * odd + 64)
                        ps = begin_aux(("cq", i, odd))
                        for h in range(odd, 16, 2):
                            mm = pe.matmul(ps[:, 16 * (h - odd):16 * (h - odd) + NCMP],
                                           qT2[r, h // 2, 128 * i:128 * i + 128], kcmp[r, h // 8, 0:NCMP],
                                           start=True, stop=True)
                        mm.then_inc(aux_done, 1)
                if i >= 1:
                    pe.wait_ge(cexp_done, i)
                    turn(("cp", i - 1), [pc[:, (i - 1) % 2, 128 * b:128 * b + 128] for b in range(4)])
                    aux_out(pe, ("cp", i - 1))
                    for a in range(2):
                        ps = begin_aux(("cv", i - 1, a))
                        for b in range(2):
                            mm = pe.matmul(ps[:, 256 * b:256 * b + 256], pTc[:, 128 * (2 * a + b):128 * (2 * a + b) + 128],
                                           vbd[:, a, :], start=True, stop=True)
                        mm.then_inc(aux_done, 1)
            for n in range(NU2 + 2):
                if n < NU2:
                    i, h = UNITS2[n]
                    r = slice(64 * (h % 2), 64 * (h % 2) + 64)
                    for b, key in enumerate(("qs", "qw")):
                        pe.matmul(begin_aux((key, n))[:, 0:128 * (i + 1)], qT2[r, h // 2, 128 * i:128 * i + 128],
                                  ksT[r, 2 * b + h // 8, 0:128 * (i + 1)], start=True, stop=True).then_inc(aux_done, 1)
                if 0 <= n - 1 < NU2:
                    i, h = UNITS2[n - 1]
                    for b, key in enumerate(("ps", "pw")):
                        pe.wait_ge(exp2_done, 2 * (n - 1) + b + 1)
                        turn((key, n - 1), [pr2[:, (n - 1) % 2, b, 128 * m:128 * m + 128] for m in range(i + 1)])
                if 0 <= n - 2 < NU2:
                    i, h = UNITS2[n - 2]
                    aux_out(pe, ("ps", n - 2))
                    aux_out(pe, ("pw", n - 2))
                    ps = begin_aux(("pv2", n - 2))
                    for b in range(2):
                        for m in range(i + 1):
                            mm = pe.matmul(ps[:, 64 * b:64 * b + 64], pT2[:, (n - 2) % 2, b, 128 * m:128 * m + 128],
                                           vs2[:, b, m, 64 * (h // 8):64 * (h // 8) + 64],
                                           start=(m == 0), stop=(m == i))
                    mm.then_inc(aux_done, 1)
            proj_rows("m10", "m10", hT)
            pe.wait_ge(o2_done, NU2)
            for m in range(8):
                turn(("o2", m), [ob[:, t, 128 * m:128 * m + 128] for t in range(TT)])
            for m in range(8):
                aux_out(pe, ("o2", m))
            proj_rows("ya0", "ya0", oT2)
            proj_rows("m11", "m11", hT)
            proj_rows("ya1", "ya1", oT2)
            pe.wait_ge(mg_done, 2 * TT)
            for m in range(8):
                turn(("mt", m), [mg[:, t, 128 * m:128 * m + 128] for t in range(TT)])
            for m in range(8):
                aux_out(pe, ("mt", m))
            proj_rows("wo0", "wo0", mT)
            proj_rows("wo1", "wo1", mT)

            pe.wait_ge(conv_in, 16 * 16)
            for a in range(2):
                turn(("cvt", a), [cvr[0:88, a, :]])
            x_turns("h3", xn3, (xn_done, 3 * TT))
            for k in range(KT):
                aux_out(pe, ("h3", k))
            for j in range(FT):
                w = weights(pe, ("f", j // 2))
                m = 128 if j < FT - 1 else 64
                for a, key in enumerate(("fg", "fv")):
                    c0 = 256 * a + 128 * (j % 2)
                    ps = begin_proj((key, j))
                    for k in range(KT):
                        mm = pe.matmul(ps[0:m, :], w[:, k, c0:c0 + m], hT[:, k, :], start=(k == 0), stop=(k == KT - 1))
                    mm.then_inc(proj_done, 1)
            pe.wait_ge(act_done, FT)
            for a in range(2):
                banks = [begin_proj((f"dn{a}", t)) for t in range(TT)]
                for b in range(3):
                    w = weights(pe, ("d", a, b))
                    for t in range(TT):
                        for k in range(8 * b, min(8 * b + 8, FT)):
                            m = 128 if k < FT - 1 else 64
                            mm = pe.matmul(banks[t][:, :], aT[0:m, k, 128 * t:128 * t + 128], w[0:m, k - 8 * b, :],
                                           start=(k == 0), stop=(k == FT - 1))
                        if b == 2:
                            mm.then_inc(proj_done, 1)
                    if b < 2:
                        mm.then_inc(chunk_used, 1)

        @block.scalar
        def _(act):
            step = Steps(act, act_step)
            act.dma_start(ident, k_ident).then_inc(consts_in, 16)
            for at, n, src in ROWS:
                act.dma_start(colr[at:at + n, :], src).then_inc(rows_in, 16)
            for a, src in ((0, a_re), (1, a_im)):
                for half in range(2):
                    act.dma_start(lraw[0:32, a, 64 * half:64 * half + 64], src[0]).then_inc(lam_in, 16)
            for a in range(2):
                for half in range(2):
                    src = (c_re, c_im)[(a + half) % 2]
                    act.dma_start(craw[:, a, :, 64 * half:64 * half + 64],
                                  src[0].rearrange("(m g) o p -> (g o) m p", g=8)).then_inc(craw_in, 16)
            for n in range(2):
                r = slice(64 * n, 64 * n + 64)
                act.dma_start(bre[r, :, :], b_re[0].rearrange("g p i -> p g i")).then_inc(b_in, 16)
                act.dma_start(bim[r, :, :], b_im[0].rearrange("g p i -> p g i")).then_inc(b_in, 16)

            aux_ready(act, "cols")
            act.wait_ge(vec_step, 1)
            act.activation(silc[:, 8:16], colv[:, CV_C:CV_C + 8], ACT.Tanh, scale=0.5).then_inc(act_tanhc, 1)

            act.wait_ge(mod_done, 1)
            for k in range(KT):
                aux_ready(act, ("x", k))
                act.activation(hT[:, k, :], abank(("x", k))[:, :], ACT.Identity, scale=modc[:, 8 + k:9 + k],
                               bias=modc[:, k:k + 1]).then_inc(afree(("x", k)), 1)

            def ssm_kernels(q):
                for a in range(2):
                    aux_ready(act, ("k", q, a))
                    if a == 0 and q == 0:
                        act.wait_ge(pool_ones, 1)
                    if a == 0 and q:
                        act.wait_ge(t_in, 16 * L * q)
                    act.activation(Kx[0:GC, 4 * a:4 * a + 4, 112:240],
                                   abank(("k", q, a))[0:GC, :].rearrange("p (a b) -> p a b", a=4),
                                   ACT.Copy).then_inc(afree(("k", q, a)), 1)
                for a in range(2):
                    aux_ready(act, ("z", q, a))
                    act.activation(Wn[:, 4 * a:4 * a + 4, :],
                                   abank(("z", q, a))[:, :].rearrange("p (a b) -> p a b", a=4),
                                   ACT.Copy).then_inc(afree(("z", q, a)), 1)

            def ssm_chunks(q):
                aux_ready(act, ("v", q))
                if q:
                    act.wait_ge(aux_done, AUX[("y", q - 1)] + 1)
                act.activation(Vb, abank(("v", q))[:, :].rearrange("p (a b) -> p a b", a=QG),
                               ACT.Copy).then_inc(afree(("v", q)), 1)

            def ssm_out(q):
                aux_ready(act, ("y", q))
                act.activation(Vs, abank(("y", q))[:, :].rearrange("p (a b) -> p a b", a=QG),
                               ACT.Copy).then_inc(afree(("y", q)), 1)

            for j in range(4):
                proj_ready(act, ("u", j))
                act.activation(u[:, j, :].rearrange("p (s c) -> p s c", s=L),
                               pbank(("u", j))[:, :].rearrange("p (c s) -> p s c", s=L),
                               ACT.Copy).then_inc(pfree(("u", j)), 1)
            ssm_kernels(0)
            for j in range(4):
                proj_ready(act, ("qi", j))
                act.activation(qiT[:, j, :], pbank(("qi", j))[:, :], ACT.Copy).then_inc(pfree(("qi", j)), 1)
            ssm_chunks(0)
            proj_ready(act, "ki")
            act.activation(kiT, pbank("ki")[:, :], ACT.Copy).then_inc(pfree("ki"), 1)
            proj_ready(act, "wi")
            act.activation(wi, pbank("wi")[:, 0:32].rearrange("p (a b) -> p a b", a=TT), ACT.Copy,
                           scale=8 ** -0.5).then_inc(pfree("wi"), 1)
            ssm_out(0)
            m = 0
            for i in range(1, TT):
                for h in range(8):
                    aux_ready(act, ("rel", i, h))
                    if m >= 2:
                        act.wait_ge(rel_used, m - 1)
                    n = 128 * (i + 1)
                    act.activation(reluq[:, m % 2, 0:n], abank(("rel", i, h))[:, 0:n], ACT.Relu)\
                       .then_inc(afree(("rel", i, h)), 1)
                    m += 1
            ssm_kernels(1)

            def rows_in_(name, dst):
                for t in range(TT):
                    proj_ready(act, (name, t))
                    act.activation(dst[:, t, :], pbank((name, t))[:, :], ACT.Copy)\
                       .then_inc(pfree((name, t)), 1)

            def columns_in(name, dst):
                for m in range(4):
                    aux_ready(act, (name, m))
                    act.activation(dst[:, m, :], abank((name, m))[:, :], ACT.Copy)\
                       .then_inc(afree((name, m)), 1)

            rows_in_("k", row)
            ssm_chunks(1)
            columns_in("kt", kT)
            ssm_out(1)
            aux_ready(act, ("kt", 3))
            rows_in_("q", row)
            ssm_kernels(2)
            act.wait_ge(rb_saved, 16)
            columns_in("qt", qT)
            ssm_chunks(2)
            rows_in_("v", v1)
            ssm_out(2)
            ssm_kernels(3)
            for j in range(4):
                proj_ready(act, ("z", j))
                act.activation(sz[:, j, :].rearrange("p (s c) -> p s c", s=L),
                               pbank(("z", j))[:, :].rearrange("p (c s) -> p s c", s=L),
                               ACT.Tanh, scale=0.5).then_inc(sz_tanh, 1)
            ssm_chunks(3)
            for t in range(TT):
                proj_ready(act, ("az", t))
                act.activation(az[:, t, :], pbank(("az", t))[:, :], ACT.Tanh, scale=0.5).then_inc(az_tanh, 1)
            ssm_out(3)
            for n in range(NU1 + 1):
                if n < NU1:
                    i, h = UNITS1[n]
                    act.wait_ge(lg_done, n + 1)
                    if n >= 2:
                        act.wait_ge(aux_done, AUX[("pt", n - 2)] + 1)
                        act.wait_ge(o_done, n - 1)
                    act.activation(pr[:, n % 2, 0:128 * (i + 1)], lg[:, n % 2, 0:128 * (i + 1)], ACT.Exp,
                                   scale=-1.0, bias=sml[:, n % 2:n % 2 + 1],
                                   accum_out=sml[:, 2 + n % 2:3 + n % 2]).then_inc(exp_done, 1)
                if n >= 1:
                    i, h = UNITS1[n - 1]
                    aux_ready(act, ("pt", n - 1))
                    if n >= 3:
                        act.wait_ge(aux_done, AUX[("pv", n - 3)] + 1)
                    act.activation(pT[:, (n - 1) % 2, 0:128 * (i + 1)], abank(("pt", n - 1))[:, 0:128 * (i + 1)],
                                   ACT.Copy).then_inc(afree(("pt", n - 1)), 1)
                if n % 8 == 7:
                    j = n // 8
                    act.wait_ge(y_skip, j + 1)
                    act.activation(gt[:, j % 2, :], gt[:, j % 2, :], ACT.Tanh, scale=SQ2PI).then_inc(y_tanh, 1)
            for j in range(4):
                proj_ready(act, ("glu", j))
                act.wait_ge(gbias_done, 1)
                if j >= 2:
                    act.wait_ge(ys_done, j - 1)
                act.activation(gt[:, j % 2, :], pbank(("glu", j))[:, :], ACT.Tanh, scale=0.25,
                               bias=colv[:, CV_BGLU + j:CV_BGLU + j + 1]).then_inc(pfree(("glu", j)), 1)
            columns_in("ot", oT)

            def scaled_columns_in(key, n, col):
                for k in range(n):
                    aux_ready(act, (key, k))
                    act.activation(hT[:, k, :], abank((key, k))[:, :], ACT.Copy,
                                   scale=colv[:, col + k:col + k + 1]).then_inc(afree((key, k)), 1)

            def many_columns_in(key, dst, ms, src=None):
                for m in ms:
                    aux_ready(act, (key, m))
                    act.activation(dst[:, m, :], abank((key, m))[:, :], ACT.Copy).then_inc(afree((key, m)), 1)

            act.wait_ge(x1_done, 2 * TT)
            act.dma_start(posr[0:64, :], cmp_pos_2[0].rearrange("a l d -> (a l) d")).then_inc(small_in, 16)
            for c0 in (0, 64):
                act.dma_start(w2s[:, c0:c0 + 64], cmp_w2_2[0, 0]).then_inc(small_in, 16)
            act.dma_start(w2s[:, 128:192], cmp_w2_2[0, 1]).then_inc(small_in, 16)
            scaled_columns_in("h2", KT, CV_G2)
            aux_ready(act, "pos")
            act.activation(posT[0:64, :, :], abank("pos")[0:64, 0:64].rearrange("p (a b) -> p a b", a=2), ACT.Copy)\
               .then_inc(afree("pos"), 1)
            for j in range(4):
                proj_ready(act, ("up", j))
                act.activation(upT[:, j, :], pbank(("up", j))[:, :], ACT.Copy).then_inc(pfree(("up", j)), 1)
            for t in range(TT):
                proj_ready(act, ("kv1", t))
                act.activation(kvr[:, t, 0:384], pbank(("kv1", t))[:, 0:384], ACT.Copy)
                act.activation(vs2[:, 0, t, :], pbank(("kv1", t))[:, 384:512], ACT.Copy)\
                   .then_inc(pfree(("kv1", t)), 1)
            for t in range(TT):
                proj_ready(act, ("kv2", t))
                act.activation(kvr[:, t, 384:512], pbank(("kv2", t))[:, 0:128], ACT.Copy)
                act.activation(vs2[:, 1, t, :], pbank(("kv2", t))[:, 128:256], ACT.Copy)
                act.activation(ngs[:, t, :], pbank(("kv2", t))[:, 256:304], ACT.Tanh, scale=0.5)\
                   .then_inc(pfree(("kv2", t)), 1)
            rows_in_("q2a", row2)
            many_columns_in("ks", ksT, range(4))
            many_columns_in("kc", kcT, range(2))
            act.wait_ge(hid_in, 1)
            act.activation(hid[:, 2:4, :].rearrange("p a b -> p (a b)")[:, 0:127],
                           hid[:, 2:4, :].rearrange("p a b -> p (a b)")[:, 0:127], ACT.Tanh, scale=SQ2PI)\
               .then_inc(hid_tanh, 1)
            rows_in_("q2b", q2b)
            many_columns_in("qt2", qT2, range(4))

            def tanh_rows(name, dst, c0, done):
                for t in range(TT):
                    proj_ready(act, (name, t))
                    act.activation(dst[:, t, c0:c0 + 512], pbank((name, t))[:, :], ACT.Tanh, scale=0.5)\
                       .then_inc(pfree((name, t)), 1)

            aux_ready(act, "kcm")
            act.activation(kcmp[:, :, 0:NCMP], abank("kcm")[:, 0:64].rearrange("p (a b) -> p a b", a=2)[:, :, 0:NCMP],
                           ACT.Copy).then_inc(afree("kcm"), 1)
            aux_ready(act, ("qt2", 7))
            many_columns_in("qt2", qT2, range(4, 8))
            tanh_rows("m00", mg, 0, None)
            for j in range(4):
                proj_ready(act, ("ypm", j))
                act.activation(ypT[:, j, :], pbank(("ypm", j))[:, :], ACT.Copy,
                               scale=colv[:, CV_PS + j:CV_PS + j + 1]).then_inc(pfree(("ypm", j)), 1)
            tanh_rows("m01", mg, 512, None)
            for i in range(TT + 1):
                if i < TT:
                    act.wait_ge(clg_done, i + 1)
                    pv_ = pc[:, i % 2, :].rearrange("p (a b) -> p a b", a=16)[:, :, 0:NCMP]
                    act.activation(pv_, pv_, ACT.Exp).then_inc(cexp_done, 1)
                if i >= 1:
                    aux_ready(act, ("cp", i - 1))
                    if i >= 2:
                        act.wait_ge(aux_done, AUX[("cv", i - 2, 1)] + 1)
                    act.activation(pTc, abank(("cp", i - 1))[:, :], ACT.Copy).then_inc(afree(("cp", i - 1)), 1)
            for n in range(NU2 + 1):
                if n < NU2:
                    i, h = UNITS2[n]
                    for b in range(2):
                        act.wait_ge(lg2_done, 2 * n + b + 1)
                        if n >= 2 and b == 0:
                            act.wait_ge(o2_done, n - 1)
                        buf = pr2[:, n % 2, b, 0:128 * (i + 1)]
                        act.activation(buf, buf, ACT.Exp, scale=-1.0, bias=sml[:, 16 + 2 * (n % 2) + b:17 + 2 * (n % 2) + b],
                                       accum_out=sml[:, 20 + 2 * (n % 2) + b:21 + 2 * (n % 2) + b]).then_inc(exp2_done, 1)
                if n >= 1:
                    i, h = UNITS2[n - 1]
                    if n >= 3:
                        act.wait_ge(aux_done, AUX[("pv2", n - 3)] + 1)
                    for b, key in enumerate(("ps", "pw")):
                        aux_ready(act, (key, n - 1))
                        act.activation(pT2[:, (n - 1) % 2, b, 0:128 * (i + 1)], abank((key, n - 1))[:, 0:128 * (i + 1)],
                                       ACT.Copy).then_inc(afree((key, n - 1)), 1)
            tanh_rows("m10", row2, 0, None)
            many_columns_in("o2", oT2, range(8))
            tanh_rows("m11", plT, 0, None)
            many_columns_in("mt", mT, range(8))
            scaled_columns_in("h3", KT, CV_GF)
            for j in range(FT):
                m = 128 if j < FT - 1 else 64
                for a, key in enumerate(("fg", "fv")):
                    proj_ready(act, (key, j))
                    if a == 0 and j == 0:
                        act.wait_ge(cvw_done, 2)
                    if a == 0 and j >= 2:
                        act.wait_ge(act_done, j - 1)
                    act.activation(fc[0:m, j % 2, a, :], pbank((key, j))[0:m, :], ACT.Identity,
                                   scale=cvw[0:m, a, 2, j:j + 1], bias=cvw[0:m, a, 3, j:j + 1]).then_inc(tap_done, 1)
                act.wait_ge(gatec_done, j + 1)
                act.activation(ft[0:m, j % 2, :], fc[0:m, j % 2, 0, :], ACT.Tanh, scale=0.5).then_inc(ftanh_done, 1)

        @block.gpsimd
        def _(pool):
            step = Steps(pool, pool_step)
            pool.dma_start(onehot[0:33, :], k_bucket).then_inc(onehot_in, 16)
            pool.dma_start(rb_in[0:32, :], rel_bias).then_inc(rb_in_s, 16)
            pool.memset(rb_in[32:33, :], 1.0).then_inc(rb_one, 1)
            pool.wait_ge(rb_one, 1)
            pool.dma_start(sp[:, 0, :], log_dt[0:1, :].partition_broadcast(128)).then_inc(ldt_in, 16)
            for a, src in enumerate(GAINS):
                pool.dma_start(gains[:, 64 * a:64 * a + 64], src.partition_broadcast(128)).then_inc(gains_in, 16)
            pool.dma_start(trim, k_tri).then_inc(consts_in2, 16)
            pool.dma_start(ropeT, k_rope).then_inc(consts_in2, 16)
            pool.dma_start(cmpmask, k_cmpmask).then_inc(consts_in2, 16)
            pool.dma_start(rowvalid, k_rowvalid).then_inc(consts_in2, 16)
            pool.dma_start(cnt, k_cnt).then_inc(consts_in2, 16)
            pool.wait_ge(consts_in2, 80)
            step(pool.memset(halves, -0.5))
            n_roots = [0]

            def root(cols):
                n_roots[0] += 1
                pool.wait_ge(ms_done, n_roots[0])
                n = cols.stop - cols.start
                pool.tensor_tensor(stat[:, cols], stat[:, cols], halves[:, 0:n], ALU.pow).then_inc(root_done, 1)

            root(slice(0, TT))
            pool.wait_ge(rbrow_done, 2)
            pool.dma_start(rb_dram, rb_row[0:8, :]).then_inc(rb_saved, 16)
            pool.wait_ge(proj_free[3], PROJ[("u", 3)] // 4 + 1)
            for j in range(3):
                proj_out(pool, ("u", j))
            pool.dma_start(u_dram.rearrange("(m g) o s c -> (g o) m (s c)", g=8), u).then_inc(u_saved, 16)
            pool.wait_ge(u_saved, 16)
            for s in range(L):
                pool.dma_start(U[GC * s:GC * s + GC, :, :], u_dram[:, :, s, :].rearrange("g o c -> o g c"))\
                    .then_inc(U_in, 16)
            TTM = ALU.mult

            def bc(a, *shape):
                return a.to_broadcast(list(shape)) if False else a

            for q in range(NQ):
                gs = slice(QG * q, QG * q + QG)
                Xa = [X_[:, gs, :].unsqueeze(2).broadcast_to((128, QG, 9, GC)) for X_ in (X1, X2)]
                Pa = [pw[:, a, :, gs].rearrange("p j g -> p g j").unsqueeze(3).broadcast_to((128, QG, 9, GC))
                      for a in range(2)]
                g1v = g1.rearrange("p (a b c) -> p a b c", a=QG, b=9)
                g2v = g2.rearrange("p (a b c) -> p a b c", a=QG, b=9)
                if q == 0:
                    pool.wait_ge(prep_x, 1)
                    pool.wait_ge(prep_y, 1)
                    step(pool.memset(Kx[0:GC, :, 0:112], 0.0))
                    pool.memset(r8[:, :, 0:1], 0.0).then_inc(pool_ones, 1)
                else:
                    aux_ready(pool, ("y", q - 1))
                pool.tensor_tensor(g1v, Xa[0], Pa[0], ALU.mult)
                step(pool.tensor_tensor(g2v, Xa[1], Pa[1], ALU.mult))
                step(pool.tensor_tensor(CL, g1v, g2v, ALU.add))
                pool.sem_inc(cl_done, 1)
                Ya = [Y_[:, gs, :].unsqueeze(2).broadcast_to((128, QG, L, GC)) for Y_ in (Y1, Y2)]
                Pa = [pw[:, a, 7::-1, gs].rearrange("p j g -> p g j").unsqueeze(3).broadcast_to((128, QG, L, GC))
                      for a in range(2)]
                g1v = g1[:, 0:1024].rearrange("p (a b c) -> p a b c", a=QG, b=L)
                g2v = g2[:, 0:1024].rearrange("p (a b c) -> p a b c", a=QG, b=L)
                pool.tensor_tensor(g1v, Ya[0], Pa[0], ALU.mult)
                step(pool.tensor_tensor(g2v, Ya[1], Pa[1], ALU.mult))
                step(pool.tensor_tensor(Zt, g1v, g2v, ALU.add))
                pool.sem_inc(zt_done, 1)
                for a in range(2):
                    aux_out(pool, ("k", q, a))
                for s in range(L):
                    pool.dma_start(Tm[GC * s:GC * s + GC, :, :],
                                   Kx[0:GC, :, (L - 1 - s) * GC:(L - 1 - s) * GC + 128]).then_inc(t_in, 16)
                pool.tensor_copy(r8[:, :, 1:NCH], sp[:, 12, gs].unsqueeze(2).broadcast_to((128, QG, NCH - 1)))
                pool.tensor_copy(E1[:, :, 0:1], sp[:, 10, gs].unsqueeze(2))
                step(pool.tensor_copy(E2[:, :, 0:1], sp[:, 11, gs].unsqueeze(2)))
                n = 1
                while n < NCH:
                    def lastb(E_):
                        return E_[:, :, n - 1:n].broadcast_to((128, QG, n))
                    t1 = g1[:, 0:QG * n].rearrange("p (a b) -> p a b", a=QG)
                    t2 = g2[:, 0:QG * n].rearrange("p (a b) -> p a b", a=QG)
                    t3 = g1[:, 512:512 + QG * n].rearrange("p (a b) -> p a b", a=QG)
                    t4 = g2[:, 512:512 + QG * n].rearrange("p (a b) -> p a b", a=QG)
                    pool.tensor_tensor(t1, E1[:, :, 0:n], lastb(E1), ALU.mult)
                    pool.tensor_tensor(t2, E2[:, :, 0:n], lastb(E2), ALU.mult)
                    pool.tensor_tensor(t3, E1[:, :, 0:n], lastb(E2), ALU.mult)
                    step(pool.tensor_tensor(t4, E2[:, :, 0:n], lastb(E1), ALU.mult))
                    pool.tensor_tensor(E1[:, :, n:2 * n], t1, t2, ALU.subtract)
                    step(pool.tensor_tensor(E2[:, :, n:2 * n], t3, t4, ALU.add))
                    n *= 2
                if q in (1, 2):
                    root(slice(16, 16 + 8 * TT))
                aux_out(pool, ("v", q))
                for n, (r, o) in enumerate(((0, 64), (64, 0))):
                    pool.dma_start(Vs[r:r + 64, :, :], Vb[o:o + 64, :, :]).then_inc(v_swapped, 16)
                w1 = g1[:, 0:512].rearrange("p (a b) -> p a b", a=QG)
                w2 = g2[:, 0:512].rearrange("p (a b) -> p a b", a=QG)
                pool.tensor_tensor(w1, Vb, E1, ALU.mult)
                pool.wait_ge(v_swapped, 32 * (q + 1))
                step(pool.tensor_tensor(w2, Vs, E2, ALU.mult))
                pool.tensor_tensor(Vb, w1, w2, ALU.add).then_inc(rot_done, 1)
                pool.wait_ge(scan_done, q + 1)
                for n, (r, o) in enumerate(((0, 64), (64, 0))):
                    pool.dma_start(Vs[r:r + 64, :, :], w1[o:o + 64, :, :]).then_inc(w_swapped, 16)
                pool.tensor_tensor(Vb, w1, E1, ALU.mult)
                pool.wait_ge(w_swapped, 32 * (q + 1))
                step(pool.tensor_tensor(w2, Vs, E2, ALU.mult))
                pool.tensor_tensor(Vb, Vb, w2, ALU.subtract).then_inc(s_done, 1)
                aux_out(pool, ("y", q))
                for s in range(L):
                    pool.dma_start(y_dram[gs, :, s, :].rearrange("g o c -> o g c"),
                                   Vs[GC * s:GC * s + GC, :, :]).then_inc(y_saved, 16)
                pool.wait_ge(y_saved, 16 * L * (q + 1))
                pool.dma_start(yT[:, q, :], y_dram[gs, :, :, :].rearrange("g o s c -> (g o) (s c)"))\
                    .then_inc(y_back, 16)
            pool.wait_ge(rb_saved, 16)
            pool.dma_start(biasR, bass.AP(rb_dram.tensor, 0, [[1, 128], [640, 8], [1, 512]])).then_inc(bias_in, 16)
            pool.dma_start(gt[:, 0, 0:128], k_flip).then_inc(bias_in, 16)
            pool.dma_start(badr, b_ada[0:1, 2048:3072].partition_broadcast(128)).then_inc(badr_in, 16)
            for h in range(8):
                aux_out(pool, ("flip", h))
            for n, (i, h) in enumerate(UNITS1):
                cols = 128 * (i + 1)
                if i and h == 0:
                    pool.wait_ge(topk_done, i)
                if i:
                    if n >= 2:
                        pool.wait_ge(lg_done, n - 1)
                    pool.tensor_tensor(mb[:, n % 2, 0:cols], biasT[:, h, 128 * (3 - i):512], score[:, i, 0:cols],
                                       ALU.add).then_inc(mb_done, 1)
            pool.wait_ge(o_done, NU1)
            pool.dma_start(xrow, x[0].rearrange("(t p) d -> p t d", p=128)).then_inc(x_again, 16)

            pool.wait_ge(x1_done, 2 * TT)
            pool.dma_start(pwS, pool_w_2[0].rearrange("g c d -> c g d")).then_inc(pw_in, 16)
            root(slice(0, TT))
            for j in range(4):
                proj_out(pool, ("up", j))
            for j, w in enumerate((2, 4, 8, 16)):
                src, m, flip = upT[:, j, :], 1, 0
                while m < w:
                    dst = (plT[:, j, :], tmp2[:, 0:512])[flip] if w in (2, 8) else (tmp2[:, 0:512], plT[:, j, :])[flip]
                    pool.tensor_tensor(dst[:, m:S], src[:, m:S], src[:, 0:S - m], ALU.add)
                    step(pool.tensor_copy(dst[:, 0:m], src[:, 0:m]))
                    src, m, flip = dst, 2 * m, 1 - flip
                p_ = plT[:, j, :]
                pool.tensor_scalar(p_[:, 16:S], p_[:, 16:S], 1.0 / w, None, ALU.mult)
                step(pool.tensor_tensor(p_[:, 0:16], p_[:, 0:16], cnt[:, j, :], ALU.mult))
                pool.tensor_tensor(p_, p_, upT[:, j, :], ALU.subtract).then_inc(pooled_done, 1)

            def rope(x_, cos, sin, shape):
                n = int(np.prod(shape[1:]))
                names = "abc"[:len(shape) - 1]
                t4 = [tmp2[:, 256 * m:256 * m + n].rearrange(f"p ({' '.join(names)}) -> p {' '.join(names)}",
                                                             **dict(zip(names, shape[1:]))) for m in range(4)]
                lo = x_[:, :, 0:32] if len(shape) == 3 else x_[:, :, :, 0:32]
                hi = x_[:, :, 32:64] if len(shape) == 3 else x_[:, :, :, 32:64]
                pool.tensor_tensor(t4[0], lo, cos, ALU.mult)
                pool.tensor_tensor(t4[1], hi, sin, ALU.mult)
                pool.tensor_tensor(t4[2], hi, cos, ALU.mult)
                step(pool.tensor_tensor(t4[3], lo, sin, ALU.mult))
                pool.tensor_tensor(lo, t4[0], t4[1], ALU.subtract)
                return pool.tensor_tensor(hi, t4[2], t4[3], ALU.add)

            root(slice(16, 40))
            for b, c0 in enumerate((0, 256, 384)):
                pool.wait_ge(kgain_done, b + 1)
                shape = (128, TT, 2, 32)
                rope(kvr[:, :, c0:c0 + 128].rearrange("p t (h d) -> p t h d", h=2),
                     ropeT[:, :, 0, :].unsqueeze(2).broadcast_to(shape), ropeT[:, :, 1, :].unsqueeze(2).broadcast_to(shape),
                     shape).then_inc(krope_done, 1)
                pool.wait_ge(krope_done, b + 1)
            for t in range(TT):
                pool.tensor_copy(kdup[:, t, :].rearrange("p (a b d) -> p a b d", a=4, b=2),
                                 kvr[:, t, 256:512].rearrange("p (a d) -> p a d", a=4).unsqueeze(2)
                                 .broadcast_to((128, 4, 2, 64))).then_inc(kdup_done, 1)
            for a, buf in enumerate((row2, q2b)):
                root(slice(16, 48))
                for t in range(TT):
                    pool.wait_ge(qgain_done, 4 * a + t + 1)
                    shape = (128, 8, 32)
                    rope(buf[:, t, :].rearrange("p (h d) -> p h d", h=8),
                         ropeT[:, t, 0:1, :].broadcast_to(shape), ropeT[:, t, 1:2, :].broadcast_to(shape),
                         shape).then_inc(qrope_done, 1)
                    pool.wait_ge(qrope_done, 4 * a + t + 1)
            pool.wait_ge(x2_done, 2 * TT)
            step(pool.memset(cvr, 0.0))
            for a in range(2):
                for tap in range(4):
                    src = conv_w_2[0, tap] if tap < 3 else conv_b_2[0]
                    src = src[DFF * a:DFF * a + DFF]
                    r0 = FT * tap
                    pool.dma_start(cvr[r0:r0 + FT - 1, a, :], src[0:128 * (FT - 1)].rearrange("(j p) -> j p", p=128))\
                        .then_inc(conv_in, 16)
                    pool.dma_start(cvr[r0 + FT - 1:r0 + FT, a, 0:64], src[128 * (FT - 1):DFF].rearrange("(j p) -> j p", p=64))\
                        .then_inc(conv_in, 16)
            root(slice(0, TT))

        @block.vector
        def _(v):
            step = Steps(v, vec_step)
            aux_ready(v, "cols")
            step(v.tensor_copy(colv[:, 0:62], abank("cols")[:, 0:62]))
            v.sem_inc(afree("cols"), 1)
            v.wait_ge(act_tanhc, 1)
            step(v.scalar_tensor_tensor(silc[:, 0:8], silc[:, 8:16], 1.0, colv[:, CV_C:CV_C + 8], ALU.add, ALU.mult))
            v.tensor_scalar(silc[:, 0:8], silc[:, 0:8], 0.5, None, ALU.mult).then_inc(silc_done, 1)
            v.tensor_scalar(colv[:, CV_BGLU:CV_BGLU + 4], colv[:, CV_BGLU:CV_BGLU + 4], 0.5, None, ALU.mult)\
                .then_inc(gbias_done, 1)

            roots = [0]

            def root(cols, scale):
                v.tensor_scalar(stat[:, cols], stat[:, cols], scale, EPS, ALU.mult, ALU.add).then_inc(ms_done, 1)
                roots[0] += 1
                v.wait_ge(root_done, roots[0])

            def row_norm(dst, scratch):
                for t in range(TT):
                    step(v.tensor_tensor_reduce(scratch, xrow[:, t, :], xrow[:, t, :], 1.0, 0.0, ALU.mult, ALU.add,
                                                stat[:, t:t + 1]))
                root(slice(0, TT), 1.0 / D)
                for t in range(TT):
                    v.tensor_scalar(dst[:, t, :], xrow[:, t, :], stat[:, t:t + 1], None, ALU.mult).then_inc(xn_done, 1)

            v.wait_ge(x_in, 16)
            row_norm(xrow, reluq.rearrange("p a b -> p (a b)"))

            LDT, DT, LR, LI, XR, TH, ER, COS, SIN = 0, 1, 2, 3, 4, 5, 6, 7, 8
            E8C, E8S, R8, SG = 10, 11, 12, 13

            def t_(n):
                return sp[:, n, :]

            def mul(o, a, b):
                step(v.tensor_tensor(o, a, b, ALU.mult))

            def exp_(o, a):
                k, r, p = t_(20), t_(21), t_(22)
                step(v.tensor_scalar(r, a, -88.0, 88.7, ALU.max, ALU.min))
                step(v.tensor_scalar(k, r, 1.4426950408889634, 12582912.0, ALU.mult, ALU.add))
                step(v.tensor_scalar(k, k, 12582912.0, None, ALU.subtract))
                step(v.scalar_tensor_tensor(r, k, -0.693359375, r, ALU.mult, ALU.add))
                step(v.scalar_tensor_tensor(r, k, 2.12194440e-4, r, ALU.mult, ALU.add))
                step(v.tensor_scalar(p, r, 1.0 / 5040, None, ALU.mult))
                for f in (720, 120, 24, 6, 2, 1):
                    step(v.scalar_tensor_tensor(p, p, 1.0 / f, r, ALU.add, ALU.mult))
                step(v.tensor_scalar(t_(23).bitcast(i32), k, 127.0, 8388608.0, ALU.add, ALU.mult))
                step(v.scalar_tensor_tensor(o, p, 1.0, t_(23), ALU.add, ALU.mult))

            aux_ready(v, "lam")
            v.tensor_copy(t_(LR), abank("lam")[:, 0:32])
            v.tensor_copy(t_(LI), abank("lam")[:, 32:64]).then_inc(afree("lam"), 1)
            aux_out(v, "lam")
            v.wait_ge(ldt_in, 16)
            exp_(t_(DT), t_(LDT))
            mul(t_(XR), t_(LR), t_(DT))
            mul(t_(TH), t_(LI), t_(DT))
            exp_(t_(ER), t_(XR))
            k, r, r2, p = t_(20), t_(21), t_(22), t_(23)
            step(v.tensor_scalar(k, t_(TH), 1.0 / (2 * math.pi), 12582912.0, ALU.mult, ALU.add))
            step(v.tensor_scalar(k, k, 12582912.0, None, ALU.subtract))
            step(v.scalar_tensor_tensor(r, k, -6.28125, t_(TH), ALU.mult, ALU.add))
            step(v.scalar_tensor_tensor(r, k, -1.934051513671875e-3, r, ALU.mult, ALU.add))
            step(v.scalar_tensor_tensor(r, k, -1.2556659146e-6, r, ALU.mult, ALU.add))
            mul(r2, r, r)
            step(v.tensor_scalar(p, r2, 1.0 / math.factorial(21), None, ALU.mult))
            for f in range(19, 1, -2):
                step(v.scalar_tensor_tensor(p, p, (-1) ** (f // 2) / math.factorial(f), r2, ALU.add, ALU.mult))
            step(v.scalar_tensor_tensor(t_(SIN), p, 1.0, r, ALU.add, ALU.mult))
            step(v.tensor_scalar(p, r2, 1.0 / math.factorial(20), None, ALU.mult))
            for f in range(18, 0, -2):
                step(v.scalar_tensor_tensor(p, p, (-1) ** (f // 2) / math.factorial(f), r2, ALU.add, ALU.mult))
            step(v.tensor_scalar(t_(COS), p, 1.0, None, ALU.add))

            def cmul(o_re, o_im, a_re_, a_im_, b_re_, b_im_, ta, tb, tc, td):
                v.tensor_tensor(ta, a_re_, b_re_, ALU.mult)
                v.tensor_tensor(tb, a_im_, b_im_, ALU.mult)
                v.tensor_tensor(tc, a_re_, b_im_, ALU.mult)
                step(v.tensor_tensor(td, a_im_, b_re_, ALU.mult))
                v.tensor_tensor(o_re, ta, tb, ALU.subtract)
                step(v.tensor_tensor(o_im, tc, td, ALU.add))

            v.memset(pw[:, 0, 0, :], 1.0)
            v.memset(pw[:, 1, 0, :], 0.0)
            mul(pw[:, 0, 1, :], t_(ER), t_(COS))
            mul(pw[:, 1, 1, :], t_(ER), t_(SIN))
            for n in (1, 2, 4):
                for m in range(1, n + 1):
                    cmul(pw[:, 0, n + m, :], pw[:, 1, n + m, :], pw[:, 0, n, :], pw[:, 1, n, :],
                         pw[:, 0, m, :], pw[:, 1, m, :], t_(20), t_(21), t_(22), t_(23))
            v.tensor_copy(t_(E8C), t_(COS))
            step(v.tensor_copy(t_(E8S), t_(SIN)))
            step(v.tensor_copy(t_(R8), t_(ER)))
            for n in range(3):
                cmul(t_(E8C), t_(E8S), t_(E8C), t_(E8S), t_(E8C), t_(E8S), t_(20), t_(21), t_(22), t_(23))
                mul(t_(R8), t_(R8), t_(R8))
            step(v.tensor_scalar(sp[64:128, E8S, :], sp[64:128, E8S, :], -1.0, None, ALU.mult))
            NR, DEN, FR, FI = 14, 15, 16, 17
            step(v.tensor_scalar(t_(NR), pw[:, 0, 1, :], -1.0, None, ALU.add))
            mul(t_(20), t_(LR), t_(LR))
            mul(t_(21), t_(LI), t_(LI))
            step(v.tensor_tensor(t_(DEN), t_(20), t_(21), ALU.add))
            step(v.reciprocal(t_(DEN), t_(DEN)))
            v.tensor_tensor(t_(20), t_(NR), t_(LR), ALU.mult)
            v.tensor_tensor(t_(21), pw[:, 1, 1, :], t_(LI), ALU.mult)
            v.tensor_tensor(t_(22), pw[:, 1, 1, :], t_(LR), ALU.mult)
            step(v.tensor_tensor(t_(23), t_(NR), t_(LI), ALU.mult))
            v.tensor_tensor(t_(20), t_(20), t_(21), ALU.add)
            step(v.tensor_tensor(t_(22), t_(22), t_(23), ALU.subtract))
            v.tensor_tensor(t_(FR), t_(20), t_(DEN), ALU.mult)
            step(v.tensor_tensor(t_(FI), t_(22), t_(DEN), ALU.mult))
            A1, A2, A3, A4 = 24, 25, 26, 27
            top, bot = slice(0, 64), slice(64, 128)
            for o, half, src, sgn in ((A1, top, FR, 1), (A1, bot, FI, 1), (A2, top, FI, -1), (A2, bot, FR, 1),
                                      (A3, top, FI, -1), (A3, bot, FR, 1), (A4, top, FR, -1), (A4, bot, FI, -1)):
                step(v.tensor_scalar(sp[half, o, :], sp[half, src, :], float(sgn), None, ALU.mult))
            v.wait_ge(b_in, 64)

            def gb(n):
                return t_(n).unsqueeze(2).broadcast_to((128, G, GC))

            v.tensor_tensor(Y1, bre, gb(A1), ALU.mult)
            v.tensor_tensor(Y2, bre, gb(A3), ALU.mult)
            v.tensor_tensor(X1, bim, gb(A2), ALU.mult)
            step(v.tensor_tensor(X2, bim, gb(A4), ALU.mult))
            v.tensor_tensor(Y1, Y1, X1, ALU.add)
            step(v.tensor_tensor(Y2, Y2, X2, ALU.add))
            def flat(a, rows=slice(0, 128)):
                return a[rows, :, :].rearrange("p a b -> p (a b)")
            aux_ready(v, "c1")
            v.tensor_copy(flat(X1, top), abank("c1")[top, :])
            v.tensor_scalar(flat(X1, bot), abank("c1")[bot, :], -1.0, None, ALU.mult).then_inc(afree("c1"), 1)
            aux_ready(v, "c2")
            v.tensor_scalar(flat(X2), abank("c2")[:, :], -1.0, None, ALU.mult).then_inc(afree("c2"), 1)
            aux_out(v, "c1")
            aux_out(v, "c2")
            v.sem_inc(prep_x, 1)
            v.sem_inc(prep_y, 1)
            for name, c0, n in (("rb", 0, 512), ("rb2", 512, 128)):
                aux_ready(v, name)
                v.tensor_copy(rb_row[0:8, c0:c0 + n], abank(name)[0:8, 0:n]).then_inc(rbtmp, 1)
            v.wait_ge(rbtmp, 2)
            v.sem_inc(afree("rb"), 1)
            v.sem_inc(afree("rb2"), 1)
            v.sem_inc(rbrow_done, 2)
            aux_ready(v, "mod")
            step(v.tensor_tensor(modc[:, 0:16], abank("mod")[:, 0:16], colv[:, CV_ADA:CV_ADA + 16], ALU.add))
            v.sem_inc(afree("mod"), 1)
            v.scalar_tensor_tensor(modc[:, 8:16], modc[:, 8:16], 1.0, colv[:, CV_G:CV_G + 8], ALU.add, ALU.mult)\
                .then_inc(mod_done, 1)

            def scan(q):
                v.wait_ge(rot_done, q + 1)
                v.tensor_tensor_scan(g1[:, 0:512], flat(r8), flat(Vb), 0.0, ALU.mult, ALU.add).then_inc(scan_done, 1)

            scan(0)
            v.wait_ge(consts_in2, 80)
            proj_out(v, "wi")

            def scores(i, m):
                n = 128 * (i + 1)
                for h in range(8):
                    aux_out(v, ("rel", i, h))
                    if h == 0:
                        ins = v.tensor_scalar(score[:, i, 0:n], reluq[:, m % 2, 0:n], wi[:, i, h:h + 1], None, ALU.mult)
                    else:
                        v.wait_ge(rel_used, m)
                        ins = v.scalar_tensor_tensor(score[:, i, 0:n], reluq[:, m % 2, 0:n], wi[:, i, h:h + 1],
                                                     score[:, i, 0:n], ALU.mult, ALU.add)
                    ins.then_inc(rel_used, 1)
                    m += 1
                v.wait_ge(rel_used, m)
                d = score[:, i, 128 * i:128 * i + 128]
                step(v.tensor_tensor(d, d, tri, ALU.add))

            def topk(i, rounds, end=False):
                s = score[:, i, 0:128 * (i + 1)]
                for _ in range(rounds):
                    step(v.max(sml[:, 8:16], s))
                    step(v.match_replace(s, sml[:, 8:16], s, TAKEN))
                if end:
                    v.tensor_scalar(s, s, TAKEN, NEG, ALU.not_equal, ALU.mult).then_inc(topk_done, 1)

            def head_norm(name, gain, done, buf, heads=8, sq=sqt):
                for t in range(TT):
                    proj_out(v, (name, t))
                    r_ = buf[:, t, 0:64 * heads]
                    step(v.tensor_tensor(sq[:, 0:64 * heads], r_, r_, ALU.mult))
                    step(v.tensor_reduce(stat[:, 16 + heads * t:16 + heads * (t + 1)],
                                         sq[:, 0:64 * heads].rearrange("p (a b) -> p a b", a=heads), X, ALU.add))
                root(slice(16, 16 + heads * TT), 1.0 / 64)
                for t in range(TT):
                    rv = buf[:, t, 0:64 * heads].rearrange("p (a b) -> p a b", a=heads)
                    ss = stat[:, 16 + heads * t:16 + heads * (t + 1)]
                    step(v.tensor_tensor(rv, rv, ss.unsqueeze(2).broadcast_to((128, heads, 64)), ALU.mult))
                    v.tensor_tensor(rv, rv, gain.unsqueeze(1).broadcast_to((128, heads, 64)), ALU.mult)\
                        .then_inc(done, 1)

            m = 0
            for i in range(1, TT):
                scores(i, 8 * (i - 1))
            v.wait_ge(gains_in, 16 * len(GAINS))
            step(v.tensor_scalar(gq1, gq1, 0.125, None, ALU.mult))
            head_norm("k", gk1, knorm_done, row)
            scan(1)
            topk(1, TOPK // 8, True)
            head_norm("q", gq1, qnorm_done, row)
            scan(2)
            topk(2, TOPK // 8, True)
            for j in range(4):
                v.wait_ge(sz_tanh, j + 1)
                v.scalar_tensor_tensor(sz[:, j, :].rearrange("p (s c) -> p s c", s=L),
                                       sz[:, j, :].rearrange("p (s c) -> p s c", s=L), 1.0,
                                       pbank(("z", j))[:, :].rearrange("p (c s) -> p s c", s=L),
                                       ALU.add, ALU.mult).then_inc(pfree(("z", j)), 1)
            scan(3)
            for t in range(TT):
                v.wait_ge(az_tanh, t + 1)
                v.scalar_tensor_tensor(az[:, t, :], az[:, t, :], 1.0, pbank(("az", t))[:, :], ALU.add, ALU.mult)\
                    .then_inc(pfree(("az", t)), 1)
            topk(3, TOPK // 8, True)
            v.wait_ge(aux_done, AUX[("y", 3)] + 1)
            v.wait_ge(y_back, 16 * NQ)
            v.tensor_copy(silb, silc[:, 0:8].unsqueeze(2).broadcast_to((128, KT, 128))).then_inc(silb_done, 1)
            v.wait_ge(badr_in, 16)
            for j in range(2):
                proj_ready(v, f"gate{j}")
                v.tensor_tensor(gate_b[:, 512 * j:512 * j + 512], pbank(f"gate{j}")[:, :],
                                badr[:, 512 * j:512 * j + 512], ALU.add).then_inc(pfree(f"gate{j}"), 1)

            def gelu_in(j):
                y = yT[:, j, :]
                if j >= 2:
                    v.wait_ge(z_done, j - 1)
                step(v.scalar_tensor_tensor(y, u[:, j, :], colv[:, CV_SKIP + j:CV_SKIP + j + 1], y, ALU.mult, ALU.add))
                step(v.tensor_tensor(gt[:, j % 2, :], y, y, ALU.mult))
                step(v.tensor_scalar(gt[:, j % 2, :], gt[:, j % 2, :], 0.044715, 1.0, ALU.mult, ALU.add))
                v.tensor_tensor(gt[:, j % 2, :], gt[:, j % 2, :], y, ALU.mult).then_inc(y_skip, 1)

            def gelu_out(j):
                v.wait_ge(y_tanh, j + 1)
                v.scalar_tensor_tensor(zz[:, j, :], gt[:, j % 2, :], 1.0, yT[:, j, :], ALU.add, ALU.mult)\
                    .then_inc(z_done, 1)

            for h in range(8):
                aux_ready(v, ("flip", h))
                v.tensor_copy(biasT[:, h, :], abank(("flip", h))[:, :]).then_inc(afree(("flip", h)), 1)
            for h in range(8):
                aux_out(v, ("flip", h))
            for n in range(NU1 + 2):
                if n < NU1:
                    i, h = UNITS1[n]
                    cols = 128 * (i + 1)
                    aux_ready(v, ("qk", n))
                    if i:
                        v.wait_ge(mb_done, n - 7)
                        bias = mb[:, n % 2, 0:cols]
                    else:
                        bias = biasT[:, h, 384:512]
                    if n >= 2:
                        v.wait_ge(exp_done, n - 1)
                    v.tensor_tensor_reduce(lg[:, n % 2, 0:cols], abank(("qk", n))[:, 0:cols], bias, -1.0, 3.0e38,
                                           ALU.add, ALU.min, sml[:, n % 2:n % 2 + 1]).then_inc(lg_done, 1)
                    v.wait_ge(lg_done, n + 1)
                    v.sem_inc(afree(("qk", n)), 1)
                if n % 8 == 2 and n < NU1:
                    gelu_in(n // 8)
                if n >= 2:
                    i, h = UNITS1[n - 2]
                    c0 = 4 + n % 2
                    v.wait_ge(exp_done, n - 1)
                    step(v.reciprocal(sml[:, c0:c0 + 1], sml[:, 2 + n % 2:3 + n % 2]))
                    step(v.tensor_scalar(sml[:, c0:c0 + 1], sml[:, c0:c0 + 1], 0.5, None, ALU.mult))
                    aux_ready(v, ("pv", n - 2))
                    v.scalar_tensor_tensor(orow[:, i, 64 * h:64 * h + 64], abank(("pv", n - 2))[:, 0:64],
                                           sml[:, c0:c0 + 1], az[:, i, 64 * h:64 * h + 64], ALU.mult, ALU.mult)\
                        .then_inc(o_done, 1)
                    v.wait_ge(o_done, n - 1)
                    v.sem_inc(afree(("pv", n - 2)), 1)
                if n % 8 == 1 and n > 8:
                    gelu_out(n // 8 - 1)
            for j in range(4):
                proj_out(v, ("glu", j))
                step(v.scalar_tensor_tensor(gt[:, j % 2, :], gt[:, j % 2, :], 1.0, zz[:, j, :], ALU.add, ALU.mult))
                v.scalar_tensor_tensor(yT[:, j, :].rearrange("p (c s) -> p s c", s=L),
                                       gt[:, j % 2, :].rearrange("p (s c) -> p s c", s=L), 0.125,
                                       sz[:, j, :].rearrange("p (s c) -> p s c", s=L), ALU.mult, ALU.mult)\
                    .then_inc(ys_done, 1)
            v.wait_ge(x_again, 16)
            for j in range(2):
                for t in range(TT):
                    proj_ready(v, (f"out{j}", t))
                    n = 4 * j + t
                    v.tensor_tensor(row[:, t, :], pbank((f"out{j}", t))[:, :], gate_b[:, 512 * j:512 * j + 512], ALU.mult)\
                        .then_inc(pfree((f"out{j}", t)), 1)
                    proj_out(v, (f"out{j}", t))
                    v.tensor_tensor(xrow[:, t, 512 * j:512 * j + 512], xrow[:, t, 512 * j:512 * j + 512],
                                    row[:, t, :], ALU.add).then_inc(x1_done, 1)

            v.wait_ge(x1_done, 2 * TT)
            row_norm(xn2, tmp2)
            for t in range(TT):
                proj_out(v, ("kv1", t))
                proj_out(v, ("kv2", t))
            sq2 = pT2[:, 0, 0, :]
            for b, c0 in enumerate((0, 256, 384)):
                kv = kvr[:, :, c0:c0 + 128]
                step(v.tensor_tensor(sq2.rearrange("p (t c) -> p t c", t=TT), kv, kv, ALU.mult))
                step(v.tensor_reduce(stat[:, 16 + 8 * b:24 + 8 * b], sq2.rearrange("p (t d) -> p t d", d=64), X, ALU.add))
            root(slice(16, 40), 1.0 / 64)
            for b, c0 in enumerate((0, 256, 384)):
                kv = kvr[:, :, c0:c0 + 128].rearrange("p t (h d) -> p t h d", h=2)
                rs = stat[:, 16 + 8 * b:24 + 8 * b].rearrange("p (t h) -> p t h", h=2).unsqueeze(3).broadcast_to((128, TT, 2, 64))
                step(v.tensor_tensor(kv, kv, rs, ALU.mult))
                gb_ = gains[:, 192 + 64 * b:256 + 64 * b].unsqueeze(1).unsqueeze(1).broadcast_to((128, TT, 2, 64))
                v.tensor_tensor(kv, kv, gb_, ALU.mult).then_inc(kgain_done, 1)
            v.tensor_scalar(ngs, ngs, 1.0, 0.5, ALU.add, ALU.mult).then_inc(ngs_done, 1)
            gq2 = gains[:, 128:192]
            step(v.tensor_scalar(gq2, gq2, 0.125, None, ALU.mult))
            head_norm("q2a", gq2, qgain_done, row2, sq=sq2)
            step(v.memset(hid, 0.0))
            for a in range(2):
                for g in range(2):
                    aux_ready(v, ("hid", a, g))
                step(v.tensor_tensor(sml[:, 24 + a:25 + a], abank(("hid", a, 0))[:, 31:32], colv[:, CV_B1 + a:CV_B1 + a + 1],
                                     ALU.add))
                for g in range(2):
                    v.tensor_scalar(hid[:, a, 32 * g:32 * g + NCMP], abank(("hid", a, g))[:, 0:NCMP], sml[:, 24 + a:25 + a],
                                    None, ALU.add).then_inc(afree(("hid", a, g)), 1)
                    aux_out(v, ("hid", a, g))
            hx = hid[:, 0:2, :].rearrange("p a b -> p (a b)")[:, 0:127]
            ht = hid[:, 2:4, :].rearrange("p a b -> p (a b)")[:, 0:127]
            step(v.tensor_tensor(ht, hx, hx, ALU.mult))
            step(v.tensor_scalar(ht, ht, 0.044715, 1.0, ALU.mult, ALU.add))
            v.tensor_tensor(ht, ht, hx, ALU.mult).then_inc(hid_in, 1)
            v.wait_ge(hid_tanh, 1)
            step(v.scalar_tensor_tensor(hx, ht, 1.0, hx, ALU.add, ALU.mult))
            step(v.tensor_scalar(hx, hx, 0.5, None, ALU.mult))
            v.sem_inc(hid_done, 2)
            head_norm("q2b", gq2, qgain_done, q2b, sq=sq2)
            step(v.memset(vbd, 0.0))
            aux_ready(v, ("qt2", 3))
            step(v.memset(pc, 0.0))
            aux_ready(v, "vcm")
            for r in range(4):
                for g in range(2):
                    ins = v.tensor_copy(vbd[32 * r:32 * r + NCMP, g, 64 * r:64 * r + 64],
                                        abank("vcm")[32 * r:32 * r + NCMP, 64 * g:64 * g + 64])
            ins.then_inc(afree("vcm"), 1)

            def gated(name, c0):
                for t in range(TT):
                    proj_ready(v, (name, t))
                    d = mg[:, t, c0:c0 + 512]
                    v.scalar_tensor_tensor(d, d, 1.0, pbank((name, t))[:, :], ALU.add, ALU.mult)\
                        .then_inc(pfree((name, t)), 1)

            for t in range(TT):
                proj_out(v, ("m00", t))
            gated("yp0", 0)
            for t in range(TT):
                proj_out(v, ("m01", t))
            gated("yp1", 512)
            v.wait_ge(ngs_done, 1)

            def compressed_scores(i):
                if i >= 2:
                    v.wait_ge(aux_done, AUX[("cp", i - 2)] + 1)
                for odd in range(2):
                    aux_ready(v, ("cq", i, odd))
                    dst = pc[:, i % 2, :].rearrange("p (a o b) -> p a o b", a=8, o=2)[:, :, odd, 0:NCMP]
                    ps = abank(("cq", i, odd))[:, 0:256].rearrange("p (a b) -> p a b", a=8)[:, :, 0:NCMP]
                    v.tensor_tensor(dst, ps, cmpmask[:, i:i + 1, 0:NCMP].broadcast_to((128, 8, NCMP)), ALU.add)\
                        .then_inc(afree(("cq", i, odd)), 1)
                    aux_out(v, ("cq", i, odd))
                p_ = pc[:, i % 2, :].rearrange("p (a b) -> p a b", a=16)[:, :, 0:NCMP]
                step(v.tensor_reduce(stat[:, 64:80], p_, X, ALU.max))
                v.tensor_tensor(p_, p_, stat[:, 64:80].unsqueeze(2).broadcast_to((128, 16, NCMP)), ALU.subtract)\
                    .then_inc(clg_done, 1)

            def compressed_out(i):
                v.wait_ge(cexp_done, i + 1)
                p_ = pc[:, i % 2, :].rearrange("p (a b) -> p a b", a=16)[:, :, 0:NCMP]
                step(v.tensor_reduce(stat[:, 80:96], p_, X, ALU.add))
                step(v.reciprocal(stat[:, 80:96], stat[:, 80:96]))
                step(v.tensor_tensor(stat[:, 80:96], stat[:, 80:96],
                                     ngs[:, i, :].rearrange("p (a b) -> p a b", a=16)[:, :, 0], ALU.mult))
                step(v.tensor_scalar(stat[:, 80:96], stat[:, 80:96], rowvalid[:, i:i + 1], None, ALU.mult))
                for a in range(2):
                    aux_ready(v, ("cv", i, a))
                    v.tensor_tensor(ob[:, i, 512 * a:512 * a + 512].rearrange("p (a b) -> p a b", a=8),
                                    abank(("cv", i, a))[:, :].rearrange("p (a b) -> p a b", a=8),
                                    stat[:, 80 + 8 * a:88 + 8 * a].unsqueeze(2).broadcast_to((128, 8, 64)), ALU.mult)\
                        .then_inc(afree(("cv", i, a)), 1)
                    aux_out(v, ("cv", i, a))

            for i in range(TT + 1):
                if i < TT:
                    compressed_scores(i)
                if i >= 1:
                    compressed_out(i - 1)
            for n in range(NU2 + 2):
                if n < NU2:
                    i, h = UNITS2[n]
                    cols = 128 * (i + 1)
                    if n >= 2:
                        v.wait_ge(aux_done, AUX[("pw", n - 2)] + 1)
                    for b, key in enumerate(("qs", "qw")):
                        aux_ready(v, (key, n))
                        v.tensor_tensor_reduce(pr2[:, n % 2, b, 0:cols], abank((key, n))[:, 0:cols], trim[:, 512 - cols:512],
                                               -1.0, 3.0e38, ALU.add, ALU.min,
                                               sml[:, 16 + 2 * (n % 2) + b:17 + 2 * (n % 2) + b]).then_inc(lg2_done, 1)
                        v.wait_ge(lg2_done, 2 * n + b + 1)
                        v.sem_inc(afree((key, n)), 1)
                if n >= 2:
                    i, h = UNITS2[n - 2]
                    c0 = 28 + 2 * (n % 2)
                    v.wait_ge(exp2_done, 2 * (n - 2) + 2)
                    step(v.reciprocal(sml[:, c0:c0 + 2], sml[:, 20 + 2 * (n % 2):22 + 2 * (n % 2)]))
                    step(v.tensor_tensor(sml[:, c0:c0 + 2], sml[:, c0:c0 + 2], ngs[:, i, 3 * h + 1:3 * h + 3], ALU.mult))
                    aux_ready(v, ("pv2", n - 2))
                    o_ = ob[:, i, 64 * h:64 * h + 64]
                    step(v.scalar_tensor_tensor(o_, abank(("pv2", n - 2))[:, 0:64], sml[:, c0:c0 + 1], o_, ALU.mult, ALU.add))
                    v.scalar_tensor_tensor(o_, abank(("pv2", n - 2))[:, 64:128], sml[:, c0 + 1:c0 + 2], o_, ALU.mult, ALU.add)\
                        .then_inc(o2_done, 1)
                    v.wait_ge(o2_done, n - 1)
                    v.sem_inc(afree(("pv2", n - 2)), 1)
            for j in range(2):
                for t in range(TT):
                    buf = (row2, plT)[j]
                    proj_out(v, (f"m1{j}", t))
                    proj_ready(v, (f"ya{j}", t))
                    v.scalar_tensor_tensor(buf[:, t, :], buf[:, t, :], 1.0, pbank((f"ya{j}", t))[:, :], ALU.add, ALU.mult)\
                        .then_inc(pfree((f"ya{j}", t)), 1)
                    proj_out(v, (f"ya{j}", t))
                    d = mg[:, t, 512 * j:512 * j + 512]
                    v.tensor_tensor(d, d, buf[:, t, :], ALU.add).then_inc(mg_done, 1)

            def half_added(name, done):
                for j in range(2):
                    for t in range(TT):
                        proj_ready(v, (f"{name}{j}", t))
                        d = xrow[:, t, 512 * j:512 * j + 512]
                        v.scalar_tensor_tensor(d, pbank((f"{name}{j}", t))[:, :], 0.5, d, ALU.mult, ALU.add)\
                            .then_inc(done, 1)
                        v.wait_ge(done, 4 * j + t + 1)
                        v.sem_inc(pfree((f"{name}{j}", t)), 1)

            half_added("wo", x2_done)
            row_norm(xn3, aT[:, 8:10, :].rearrange("p a b -> p (a b)"))
            for a in range(2):
                aux_ready(v, ("cvt", a))
                v.tensor_copy(cvw[:, a, :, :], abank(("cvt", a))[:, 0:88].rearrange("p (a b) -> p a b", a=4))\
                    .then_inc(cvw_done, 1)
                v.wait_ge(cvw_done, a + 1)
                v.sem_inc(afree(("cvt", a)), 1)
            for j in range(FT):
                m = 128 if j < FT - 1 else 64
                for a, key in enumerate(("fg", "fv")):
                    v.wait_ge(tap_done, 2 * j + a + 1)
                    f_, ps = fc[0:m, j % 2, a, :], pbank((key, j))
                    step(v.scalar_tensor_tensor(f_[:, 1:S], ps[0:m, 0:S - 1], cvw[0:m, a, 1, j:j + 1], f_[:, 1:S],
                                                ALU.mult, ALU.add))
                    step(v.scalar_tensor_tensor(f_[:, 2:S], ps[0:m, 0:S - 2], cvw[0:m, a, 0, j:j + 1], f_[:, 2:S],
                                                ALU.mult, ALU.add))
                    v.sem_inc(pfree((key, j)), 1)
                    if a == 0:
                        v.sem_inc(gatec_done, 1)
                v.wait_ge(ftanh_done, j + 1)
                step(v.scalar_tensor_tensor(ft[0:m, j % 2, :], ft[0:m, j % 2, :], 1.0, fc[0:m, j % 2, 0, :],
                                            ALU.add, ALU.mult))
                v.tensor_tensor(aT[0:m, j, :], ft[0:m, j % 2, :], fc[0:m, j % 2, 1, :], ALU.mult).then_inc(act_done, 1)
            half_added("dn", x3_done)


_INS = ["x", "c", "rel_bias", "norm_g", "w_ada", "b_ada", "w_in", "q_gain", "k_gain", "a_re", "a_im", "log_dt",
        "b_re", "b_im", "c_re", "c_im", "d_skip", "w_glu", "b_glu", "w_out", "attn_norm_w_2", "w_in_2",
        "pool_w_2", "pool_scale_2", "q_norm_w_2", "k_norm_w_2", "cmp_pos_2", "cmp_w1_2", "cmp_b1_2", "cmp_w2_2",
        "w_pool_br_2", "w_attn_br_2", "w_o_2", "ffn_norm_w_2", "w_up_2", "conv_w_2", "conv_b_2", "w_down_2"]


def shape_constants():
    f = np.float32
    ident = np.eye(128, dtype=f)
    bucket = np.zeros((33, 640), f)
    dist = np.arange(S, dtype=np.int32)
    large = 16 + (np.log(np.maximum(dist, 1).astype(f) / f(16)) / f(math.log(8)) * f(16)).astype(np.int32)
    b = np.where(dist < 16, dist, np.minimum(large, 31))
    bucket[b, S - 1 - dist] = 1.0
    bucket[32, S:] = NEG
    p = np.arange(128)
    tri = np.zeros((128, 512), f)
    tri[:, 384:] = np.where(p[None, :] <= p[:, None], 0.0, NEG)
    half = 32
    freqs = f(10000.0) ** (-np.arange(half, dtype=f) / f(half))
    ang = np.arange(S, dtype=f)[:, None] * freqs[None, :]
    rope = np.stack([np.cos(ang), np.sin(ang)], 1).astype(f)
    rope = np.ascontiguousarray(rope.reshape(TT, 128, 2, 32).transpose(1, 0, 2, 3))
    t = np.arange(S)
    ends = np.arange(32) * 16 + 31
    cm = np.where(ends[None, :] <= t[:, None], 0.0, NEG).astype(f)
    cm = np.ascontiguousarray(cm.reshape(TT, 128, 32).transpose(1, 0, 2))
    rv = np.ascontiguousarray((t >= 31).astype(f).reshape(TT, 128).T)
    cnt = np.ones((4, 16), f)
    for i, w in enumerate((2, 4, 8, 16)):
        cnt[i] = f(1) / np.minimum(np.arange(16) + 1, w).astype(f)
    cnt = np.ascontiguousarray(np.broadcast_to(cnt[None], (128, 4, 16)))
    return dict(k_ident=ident, k_bucket=bucket, k_tri=tri, k_rope=rope, k_cmpmask=cm, k_rowvalid=rv, k_cnt=cnt,
                k_flip=np.ascontiguousarray(ident[::-1]))


def kernel(**inputs):
    import concourse.bacc as _bacc
    from concourse.bass_utils import run_bass_kernel_spmd as _run

    nc = _bacc.Bacc("TRN2", target_bir_lowering=False, num_devices=1)
    arrays, args = {}, []
    named = [(name, np.ascontiguousarray(inputs[name])) for name in _INS] + list(shape_constants().items())
    for name, a in named:
        arrays[f"in_{name}"] = a
        args.append(nc.dram_tensor(f"in_{name}", a.shape, mybir.dt.from_np(a.dtype), kind="ExternalInput").ap())
    args.append(nc.dram_tensor("out_0", (1, S, D), mybir.dt.float32, kind="ExternalOutput").ap())
    program(nc, *args)
    r = _run(nc, [arrays], core_ids=[0])
    return r.results[0]["out_0"]
```

```python
import math
from contextlib import ExitStack

import numpy as np

import concourse.bass as bass
from concourse import mybir

S = 512
D = 1024
KT = D // 128
TT = S // 128
NEG = -1.0e30
SCORE_MASK = -1.0e30
TAKEN = -3.0e38
EPS = 1e-6
TOPK = min(256, S // 4)
G, GC, ST = 32, 16, 64
L = 8
NCH = S // L
QG = 8
NQ = G // QG
W_IN1 = 3656
W_IN2 = 4400
OFF_KV, OFF_NG, OFF_MG = 1536, 2304, 2352
NCMP = 31
DFF = 2752
FT = 22
SQ2PI = math.sqrt(2.0 / math.pi)


def program(nc, x, c, rel_bias, norm_g, w_ada, b_ada, w_in, q_gain, k_gain, a_re, a_im, log_dt,
            b_re, b_im, c_re, c_im, d_skip, w_glu, b_glu, w_out, attn_norm_w_2, w_in_2, pool_w_2,
            pool_scale_2, q_norm_w_2, k_norm_w_2, cmp_pos_2, cmp_w1_2, cmp_b1_2, cmp_w2_2,
            w_pool_br_2, w_attn_br_2, w_o_2, ffn_norm_w_2, w_up_2, conv_w_2, conv_b_2, w_down_2,
            k_ident, k_bucket, k_tri, k_rope, k_cmpmask, k_rowvalid, k_cnt, k_flip, out):
    f32 = mybir.dt.float32
    i32 = mybir.dt.int32
    ALU = mybir.AluOpType
    ACT = mybir.ActivationFunctionType
    X = mybir.AxisListType.X
    ctx = ExitStack()
    with ctx:
        def sem(name):
            return ctx.enter_context(nc.semaphore(name))

        ARENA = 53200
        arena = ctx.enter_context(nc.sbuf_tensor("arena", [128, ARENA], f32))
        bank = [ctx.enter_context(nc.psum_tensor(f"bank{i}", [128, 512], f32)) for i in range(8)]

        class Zone:
            def __init__(self, at, end=ARENA):
                self.at, self.end = at, end

            def take(self, words, *shape):
                a = arena[:, self.at:self.at + words]
                self.at += words
                assert self.at <= self.end, (self.at, self.end)
                if len(shape) > 1:
                    names = "abcd"[:len(shape)]
                    a = a.rearrange(f"p ({' '.join(names)}) -> p {' '.join(names)}",
                                    **{n: s for n, s in zip(names, shape)})
                return a

        z = Zone(0)
        slot = [z.take(4096) for _ in range(2)]
        XROW0 = z.at
        xrow = z.take(4096, TT, D)
        hT = z.take(4096, KT, S)
        ident = z.take(128)
        trim = z.take(512)
        tri = trim[:, 384:512]
        ropeT = z.take(TT * 64, TT, 2, 32)
        cmpmask = z.take(TT * 32, TT, 32)
        rowvalid = z.take(TT)
        cnt = z.take(64, 4, 16)
        colv = z.take(64)
        colr = z.take(128)
        modc = z.take(40)
        silc = z.take(16)
        stat = z.take(192)
        sml = z.take(64)
        halves = z.take(32)
        gains = z.take(384)
        BASE = z.at

        z = Zone(BASE)
        u = z.take(2048, TT, S)
        sz = z.take(2048, TT, S)
        yT = z.take(2048, TT, S)
        qiT = z.take(2048, TT, S)
        kiT = z.take(512)
        wi = z.take(32, TT, 8)
        score = z.take(2048, TT, S)
        reluq = z.take(1024, 2, S)
        row = z.take(2048, TT, 512)
        kT = z.take(2048, TT, S)
        qT = z.take(2048, TT, S)
        v1 = z.take(2048, TT, 512)
        sqt = reluq[:, 0, :]
        U = arena[:, XROW0:XROW0 + 2048].rearrange("p (a b) -> p a b", a=G)
        az = arena[:, XROW0 + 2048:XROW0 + 4096].rearrange("p (a b) -> p a b", a=TT)
        zq = Zone(z.at - 2048 - 2048)
        onehot, rb_row, rb_in = zq.take(640), zq.take(640), zq.take(8)
        SSM0 = z.at
        X1, X2 = z.take(512, G, GC), z.take(512, G, GC)
        Y1, Y2 = z.take(512, G, GC), z.take(512, G, GC)
        pw = z.take(2 * 9 * 32, 2, 9, 32)
        sp = z.take(32 * 32, 32, 32)
        CL = z.take(QG * 9 * GC, QG, 9, GC)
        Zt = z.take(1024, QG, L, GC)
        Tm = z.take(1024, QG, 128)
        Wn = z.take(1024, QG, 128)
        KX0 = z.at
        Kx = z.take(QG * 240, QG, 240)
        E1, E2 = z.take(512, QG, NCH), z.take(512, QG, NCH)
        Vb, Vs = z.take(512, QG, NCH), z.take(512, QG, NCH)
        r8 = z.take(512, QG, NCH)
        G0 = z.at
        g1, g2 = z.take(1152), z.take(1152)
        far = arena[:, BASE + 2048 + 1024:BASE + 2048 + 1536].rearrange("p (a n g) -> p a n g", a=2, n=8)
        near = arena[:, BASE + 2048 + 1536:BASE + 4096].rearrange("p (a n g) -> p a n g", a=2, n=8)
        zq = Zone(KX0)
        craw, lraw = zq.take(1024, 2, 4, 128), zq.take(256, 2, 128)
        zq = Zone(G0)
        bre, bim = zq.take(512, G, GC), zq.take(512, G, GC)
        END1 = z.at

        z = Zone(SSM0)
        biasT = z.take(4096, 8, 512)
        biasR = arena[:, z.at:z.at + 4096].rearrange("p (a b) -> p a b", a=8)
        mb = z.take(1024, 2, 512)
        lg = z.take(1024, 2, 512)
        pr = z.take(1024, 2, 512)
        pT = z.take(1024, 2, 512)
        zz = z.take(2048, TT, S)
        gt = z.take(1024, 2, 512)
        gate_b = z.take(1024)
        badr = z.take(1024)
        silb = z.take(1024, KT, 128)
        orow, oT = row, qiT

        z = Zone(BASE)
        upT = z.take(2048, 4, S)
        plT = z.take(2048, 4, S)
        ypT = z.take(2048, 4, S)
        pwS = z.take(512, 4, 128)
        row2 = z.take(2048, TT, 512)
        tmp2 = z.take(1024)
        qT2 = z.take(4096, 8, S)
        ksT = z.take(2048, 4, S)
        kcT = z.take(1024, 2, S)
        vs2 = z.take(1024, 2, TT, 128)
        ngs = z.take(TT * 48, TT, 48)
        posr, posT = z.take(64), z.take(64, 2, 32)
        w2s = z.take(192)
        hid = z.take(256, 4, 64)
        kcmp = z.take(64, 2, 32)
        vbd = z.take(512, 2, 256)
        pc = row2[:, 0:2, :]
        pTc = row2[:, 2, :]
        pr2 = z.take(2048, 2, 2, 512)
        pT2 = z.take(2048, 2, 2, 512)
        OB0 = z.at
        ob = z.take(4096, TT, D)
        mg = z.take(4096, TT, D)
        END2 = z.at
        oT2 = qT2
        xn2 = ob
        kvr = arena[:, OB0:OB0 + 2048].rearrange("p (a b) -> p a b", a=TT)
        kdup = arena[:, OB0 + 2048:OB0 + 4096].rearrange("p (a b) -> p a b", a=TT)
        q2b = arena[:, OB0 + 4096:OB0 + 6144].rearrange("p (a b) -> p a b", a=TT)
        mT = hT

        z = Zone(BASE)
        aT = z.take(FT * 512, FT, S)
        cvw = z.take(2 * 88, 2, 4, FT)
        cvr = z.take(2 * 128, 2, 128)
        fc = z.take(4 * 512, 2, 2, 512)
        ft = z.take(2 * 512, 2, 512)
        xn3 = arena[:, BASE:BASE + 4096].rearrange("p (a b) -> p a b", a=TT)


        PROJ, AUX = {}, {}

        def name_proj(*names):
            for n in names:
                PROJ[n] = len(PROJ)

        def name_aux(*names):
            for n in names:
                AUX[n] = len(AUX)

        def four(name):
            return [(name, t) for t in range(TT)]

        def ssm_names(q):
            return [("k", q, 0), ("k", q, 1), ("z", q, 0), ("z", q, 1)]

        def rel_names(i):
            return [("rel", i, h) for h in range(8)]

        name_aux("cols", "lam", "c1", "c2", "rb", "rb2", "mod", *[("x", k) for k in range(KT)])
        name_proj(*four("u"), *four("qi"), "ki", "wi", *four("k"), *four("q"), *four("v"))
        name_aux(*ssm_names(0), ("v", 0), ("y", 0), *rel_names(1), *ssm_names(1), *rel_names(2), ("v", 1),
                 *rel_names(3), ("y", 1), *ssm_names(2), ("v", 2), *four("kt"), ("y", 2), *ssm_names(3), ("v", 3),
                 *four("qt"), ("y", 3), *[("flip", h) for h in range(8)])
        name_proj(("az", 0))
        FILL1 = {0: ("az", 1), 2: ("az", 2), 4: ("az", 3), 6: ("z", 0), 8: ("z", 1), 10: ("z", 2), 12: ("z", 3),
                 14: "gate0", 16: "gate1", 20: ("glu", 0), 23: ("glu", 1), 26: ("glu", 2), 29: ("glu", 3)}
        UNITS1 = [(i, h) for i in range(TT) for h in range(8)]
        NU1 = len(UNITS1)
        for n in range(NU1 + 2):
            if n < NU1:
                name_proj(("qk", n))
            if 0 <= n - 1 < NU1:
                name_aux(("pt", n - 1))
            if 0 <= n - 2 < NU1:
                name_aux(("pv", n - 2))
            if n in FILL1:
                name_proj(FILL1[n])
        name_aux(*four("ot"))
        name_proj(*[(f"out{j}", t) for t in range(TT) for j in range(2)])
        name_aux(*[("h2", k) for k in range(KT)], "pos")
        name_proj(*four("up"), *four("kv1"), *four("kv2"), *four("q2a"))
        name_aux(*[("ks", n) for n in range(4)], ("kc", 0), ("kc", 1))
        name_aux(*[("hid", a, g) for a in range(2) for g in range(2)])
        name_proj(*four("q2b"))
        name_aux(*[("qt2", m) for m in range(4)], "kcm", "vcm")
        name_proj(*four("m00"))
        name_aux(*[("qt2", m) for m in range(4, 8)])
        name_proj(*four("ypm"))
        FILLC = {i: ("yp0", i) for i in range(TT)}
        FILL2 = {1 + 3 * n: name for n, name in enumerate(four("m01") + four("yp1") + four("m10") + four("m11"))}
        for i in range(TT + 1):
            if i < TT:
                name_aux(("cq", i, 0), ("cq", i, 1))
            if i >= 1:
                name_aux(("cp", i - 1), ("cv", i - 1, 0), ("cv", i - 1, 1))
            if i in FILLC:
                name_proj(FILLC[i])
        UNITS2 = [(i, h) for i in range(TT) for h in range(16)]
        NU2 = len(UNITS2)
        for n in range(NU2 + 2):
            if n < NU2:
                name_proj(("qs", n), ("qw", n))
            if 0 <= n - 1 < NU2:
                name_aux(("ps", n - 1), ("pw", n - 1))
            if 0 <= n - 2 < NU2:
                name_aux(("pv2", n - 2))
            if n in FILL2:
                name_proj(FILL2[n])
        name_aux(*[("o2", m) for m in range(8)])
        name_proj(*four("ya0"), *four("ya1"))
        name_aux(*[("mt", m) for m in range(8)])
        name_proj(*four("wo0"), *four("wo1"))
        name_aux(("cvt", 0), ("cvt", 1), *[("h3", k) for k in range(KT)])
        for j in range(FT):
            name_proj(("fg", j), ("fv", j))
        for a in range(2):
            name_proj(*four(f"dn{a}"))

        proj_done, aux_done = sem("proj_done"), sem("aux_done")
        proj_free = [sem(f"proj_free{b}") for b in range(4)]
        aux_free = [sem(f"aux_free{b}") for b in range(4)]

        def pbank(name):
            return bank[PROJ[name] % 4]

        def abank(name):
            return bank[4 + AUX[name] % 4]

        def proj_ready(eng, name):
            eng.wait_ge(proj_done, PROJ[name] + 1)

        def aux_ready(eng, name):
            eng.wait_ge(aux_done, AUX[name] + 1)

        def proj_out(eng, name):
            eng.wait_ge(proj_free[PROJ[name] % 4], PROJ[name] // 4 + 1)

        def aux_out(eng, name):
            eng.wait_ge(aux_free[AUX[name] % 4], AUX[name] // 4 + 1)

        def pfree(name):
            return proj_free[PROJ[name] % 4]

        def afree(name):
            return aux_free[AUX[name] % 4]

        def cols_of(w, k0, k1, c0, c1):
            return w[0, k0 * 128:k1 * 128, c0:c1].rearrange("(k p) n -> p k n", p=128)

        def slot_view(s, kt, n):
            return slot[s][:, 0:kt * n].rearrange("p (k n) -> p k n", k=kt)

        CHUNKS = []

        def chunk(name, last, kt, n, parts):
            CHUNKS.append((name, last, kt, n, parts))

        for j in range(4):
            chunk(("ada", j), ("used", j + 1) if j < 3 else ("aux", "mod"), KT, 512, [(0, 512, lambda j=j: cols_of(w_ada, 0, KT, 512 * j, 512 * j + 512))])

        def w1chunk(name, last, c0):
            chunk(name, ("proj", last), KT, 512, [(0, 512, lambda: cols_of(w_in, 0, KT, c0, c0 + 512))])

        w1chunk("u", ("u", 3), 0)
        w1chunk("qi", ("qi", 3), 3072)
        chunk("ki", ("proj", "wi"), KT, 136,
              [(0, 64, lambda: cols_of(w_in, 0, KT, 3584, 3648)),
               (64, 136, lambda: cols_of(w_in, 0, KT, 3584, 3656))])
        for name, c0 in (("k", 1536), ("q", 1024), ("v", 2048), ("az", 2560), ("z", 512)):
            w1chunk(name, (name, 3), c0)
        for j in range(2):
            chunk(("gate", j), ("proj", f"gate{j}"), KT, 512,
                  [(0, 512, lambda j=j: cols_of(w_ada, 0, KT, 2048 + 512 * j, 2560 + 512 * j))])
        chunk("glu", ("proj", ("glu", 3)), 4, 512, [(0, 512, lambda: cols_of(w_glu, 0, 4, 0, 512))])
        for j in range(2):
            chunk(("out", j), ("proj", (f"out{j}", 3)), KT, 512,
                  [(0, 512, lambda j=j: cols_of(w_out, 0, KT, 512 * j, 512 * j + 512))])
        def wchunk(name, last, w, kt, c0, n=512):
            chunk(name, ("proj", last), kt, n, [(0, n, lambda: cols_of(w, 0, kt, c0, c0 + n))])

        wchunk("up", ("up", 3), w_in_2, KT, 0)
        wchunk("kv1", ("kv1", 3), w_in_2, KT, OFF_KV)
        wchunk("kv2", ("kv2", 3), w_in_2, KT, OFF_KV + 512, 304)
        wchunk("q2a", ("q2a", 3), w_in_2, KT, 512)
        for a in range(2):
            src = cmp_w1_2[0, a].rearrange("(l d) n -> d l n", d=64)
            chunk(("c1", a), ("aux", ("hid", a, 1)), 32, 128,
                  [(None, slice(0, 64), lambda src=src: src), (None, slice(64, 128), lambda src=src: src)])
        wchunk("q2b", ("q2b", 3), w_in_2, KT, 1024)
        wchunk("m00", ("m00", 3), w_in_2, KT, OFF_MG)
        wchunk("yp0", ("yp0", 3), w_pool_br_2, 4, 0)
        wchunk("m01", ("m01", 3), w_in_2, KT, OFF_MG + 512)
        wchunk("yp1", ("yp1", 3), w_pool_br_2, 4, 512)
        wchunk("m10", ("m10", 3), w_in_2, KT, OFF_MG + 1024)
        wchunk("m11", ("m11", 3), w_in_2, KT, OFF_MG + 1536)
        wchunk("ya0", ("ya0", 3), w_attn_br_2, KT, 0)
        wchunk("ya1", ("ya1", 3), w_attn_br_2, KT, 512)
        wchunk("wo0", ("wo0", 3), w_o_2, KT, 0)
        wchunk("wo1", ("wo1", 3), w_o_2, KT, 512)
        for J in range(FT // 2):
            n = 256 if J < FT // 2 - 1 else 192
            chunk(("f", J), ("proj", ("fv", 2 * J + 1)), KT, 512,
                  [(0, n, lambda J=J, n=n: cols_of(w_up_2, 0, KT, 256 * J, 256 * J + n)),
                   (256, 256 + n, lambda J=J, n=n: cols_of(w_up_2, 0, KT, DFF + 256 * J, DFF + 256 * J + n))])
        for a in range(2):
            for b in range(3):
                last = ("used", 4 + 2 * a + b) if b < 2 else ("proj", (f"dn{a}", 3))
                if b < 2:
                    parts = [(0, 512, lambda a=a, b=b: cols_of(w_down_2, 8 * b, 8 * b + 8, 512 * a, 512 * a + 512))]
                else:
                    parts = [("down", a, None)]
                chunk(("d", a, b), last, 8 if b < 2 else 6, 512, parts)
        slot_full = [sem("slot0_full"), sem("slot1_full")]
        CH, count = {}, [0, 0]
        for n, (name, last, kt, cols, parts) in enumerate(CHUNKS):
            count[n % 2] += 16 * (2 if parts[0][0] == "down" else len(parts))
            CH[name] = (n % 2, count[n % 2], kt, cols)

        def weights(eng, name):
            s, full, kt, n = CH[name]
            eng.wait_ge(slot_full[s], full)
            return slot_view(s, kt, n)

        u_dram = nc.dram_tensor("u_dram", (G, GC, L, NCH), f32).ap()
        y_dram = nc.dram_tensor("y_dram", (G, GC, L, NCH), f32).ap()
        rb_dram = nc.dram_tensor("rb_dram", (8, 640), f32).ap()

        names = """x_in consts_in rows_in lam_in craw_in b_in ldt_in gains_in rb_in_s onehot_in
            vec_step act_step pool_step silc_done mod_done rows_done xn_done
            prep_x prep_y pool_ones u_ready u_saved U_in cl_done zt_done t_in v_swapped
            rot_done scan_done w_swapped s_done y_saved y_back b_in2 rb_saved bias_in
            rel_used topk_done knorm_done qnorm_done lg_done exp_done mb_done mb_used
            o_done x_again z_done silb_done y_skip y_tanh gbias_done ys_done out_tanh badr_in x1_done
            az_tanh sz_tanh ms_done root_done rb_one""".split()
        S_ = {n: sem(n) for n in names}
        (x_in, consts_in, rows_in, lam_in, craw_in, b_in, ldt_in, gains_in, rb_in_s, onehot_in,
         vec_step, act_step, pool_step, silc_done, mod_done, rows_done, xn_done,
         prep_x, prep_y, pool_ones, u_ready, u_saved, U_in, cl_done, zt_done, t_in, v_swapped,
         rot_done, scan_done, w_swapped, s_done, y_saved, y_back, b_in2, rb_saved, bias_in,
         rel_used, topk_done, knorm_done, qnorm_done, lg_done, exp_done, mb_done, mb_used,
         o_done, x_again, z_done, silb_done, y_skip, y_tanh, gbias_done, ys_done, out_tanh, badr_in,
         x1_done, az_tanh, sz_tanh, ms_done, root_done, rb_one) = [S_[n] for n in names]

        class Steps:
            def __init__(self, eng, s):
                self.eng, self.s, self.n = eng, s, 0

            def __call__(self, ins):
                self.n += 1
                ins.then_inc(self.s, 1)
                self.eng.wait_ge(self.s, self.n)

        act_tanhc, consts_in2, chunk_used, rbtmp, out_done = [
            sem(n) for n in ("act_tanhc", "consts_in2", "chunk_used", "rbtmp", "out_done")]
        (small_in, krope_done, qrope_done, hid_done, pooled_done, cexp_done, exp2_done, o2_done, mg_done, conv_in,
         act_done, hid_in, hid_tanh, clg_done, lg2_done, cvw_done, tap_done, gatec_done, ftanh_done, pw_in, x2_done,
         x3_done, kgain_done, qgain_done, ngs_done, kdup_done) = [sem(n) for n in """small_in krope_done qrope_done hid_done
            pooled_done cexp_done exp2_done o2_done mg_done conv_in act_done hid_in hid_tanh clg_done lg2_done cvw_done
            tap_done gatec_done ftanh_done pw_in x2_done x3_done kgain_done qgain_done ngs_done kdup_done""".split()]

        def by_rows(a):
            return a.rearrange("a (n p) -> (a n) p", p=128)

        ROWS = [(0, 8, by_rows(c)), (8, 8, by_rows(norm_g)), (16, 16, by_rows(b_ada[:, 0:2048])),
                (32, 8, by_rows(attn_norm_w_2)), (40, 8, by_rows(ffn_norm_w_2)), (48, 4, by_rows(d_skip)),
                (52, 4, by_rows(b_glu)), (56, 4, by_rows(pool_scale_2)), (60, 2, cmp_b1_2[0])]
        NROWS = len(ROWS)
        GAINS = [q_gain[0:1, :], k_gain[0:1, :], q_norm_w_2[0:1, :], k_norm_w_2[0, 0:1, :],
                 k_norm_w_2[0, 1:2, :], k_norm_w_2[0, 2:3, :]]

        block = ctx.enter_context(nc.Block())

        CV_C, CV_G, CV_ADA, CV_G2, CV_GF, CV_SKIP, CV_BGLU, CV_PS, CV_B1 = 0, 8, 16, 32, 40, 48, 52, 56, 60
        gq1, gk1 = gains[:, 0:64], gains[:, 64:128]

        @block.sync
        def _(sp_):
            sp_.dma_start(xrow, x[0].rearrange("(t p) d -> p t d", p=128)).then_inc(x_in, 16)
            def ssm_spread(q):
                for a in range(2):
                    aux_out(sp_, ("k", q, a))
                if q:
                    aux_ready(sp_, ("y", q - 1))
                for s in range(L):
                    sp_.dma_start(Tm[GC * s:GC * s + GC, :, :],
                                  Kx[0:GC, :, (L - 1 - s) * GC:(L - 1 - s) * GC + 128]).then_inc(t_in, 16)

            def ssm_swap(q):
                aux_out(sp_, ("v", q))
                for r, o in ((0, 64), (64, 0)):
                    sp_.dma_start(Vs[r:r + 64, :, :], Vb[o:o + 64, :, :]).then_inc(v_swapped, 16)
                sp_.wait_ge(scan_done, q + 1)
                w1 = g1[:, 0:512].rearrange("p (a b) -> p a b", a=QG)
                for r, o in ((0, 64), (64, 0)):
                    sp_.dma_start(Vs[r:r + 64, :, :], w1[o:o + 64, :, :]).then_inc(w_swapped, 16)

            def ssm_back(q):
                gs = slice(QG * q, QG * q + QG)
                aux_out(sp_, ("y", q))
                for s in range(L):
                    sp_.dma_start(y_dram[gs, :, s, :].rearrange("g o c -> o g c"),
                                  Vs[GC * s:GC * s + GC, :, :]).then_inc(y_saved, 16)
                sp_.wait_ge(y_saved, 16 * L * (q + 1))
                sp_.dma_start(yT[:, q, :], y_dram[gs, :, :, :].rearrange("g o s c -> (g o) (s c)"))\
                    .then_inc(y_back, 16)

            for n, (name, last, kt, cols, parts) in enumerate(CHUNKS):
                if name == "k":
                    for j in range(4):
                        proj_out(sp_, ("u", j))
                    sp_.dma_start(u_dram.rearrange("(m g) o s c -> (g o) m (s c)", g=8), u).then_inc(u_saved, 16)
                    sp_.wait_ge(u_saved, 16)
                    for s in range(L):
                        sp_.dma_start(U[GC * s:GC * s + GC, :, :], u_dram[:, :, s, :].rearrange("g o c -> o g c"))\
                            .then_inc(U_in, 16)
                    ssm_spread(0)
                    ssm_swap(0)
                if name == "q":
                    ssm_back(0)
                if name == "v":
                    ssm_spread(1)
                    ssm_swap(1)
                    ssm_back(1)
                    ssm_spread(2)
                if name == "az":
                    ssm_swap(2)
                    ssm_back(2)
                    ssm_spread(3)
                if name == "z":
                    ssm_swap(3)
                    ssm_back(3)
                if n >= 2:
                    kind, res = CHUNKS[n - 2][1]
                    if kind == "used":
                        sp_.wait_ge(chunk_used, res)
                    elif kind == "aux":
                        sp_.wait_ge(aux_done, AUX[res] + 1)
                    else:
                        sp_.wait_ge(proj_done, PROJ[res] + 1)
                w = slot_view(n % 2, kt, cols)
                for c0, c1, src in parts:
                    if c0 is None:
                        sp_.dma_start(w[c1, :, :], src()).then_inc(slot_full[n % 2], 16)
                    elif c0 == "down":
                        wd = w_down_2[0, 2048:DFF, 512 * c1:512 * c1 + 512]
                        sp_.dma_start(w[:, 0:5, :], wd[0:640, :].rearrange("(k p) n -> p k n", p=128))\
                           .then_inc(slot_full[n % 2], 16)
                        sp_.dma_start(w[0:64, 5, :], wd[640:704, :]).then_inc(slot_full[n % 2], 16)
                    else:
                        sp_.dma_start(w[:, :, c0:c1], src()).then_inc(slot_full[n % 2], 16)
            for n in range(8):
                a, t = n // 4, n % 4
                sp_.wait_ge(x3_done, n + 1)
                sp_.dma_start(out[0, 128 * t:128 * t + 128, 512 * a:512 * a + 512],
                              xrow[:, t, 512 * a:512 * a + 512]).then_inc(out_done, 16)
            sp_.wait_ge(out_done, 128)

        @block.tensor
        def _(pe):
            seen = [0, 0]

            def begin_aux(name):
                a = AUX[name]
                assert a == seen[0], (name, a, seen)
                seen[0] += 1
                if a >= 4:
                    pe.wait_ge(aux_free[a % 4], a // 4)
                return bank[4 + a % 4]

            def begin_proj(name):
                p = PROJ[name]
                assert p == seen[1], (name, p, seen)
                seen[1] += 1
                if p >= 4:
                    pe.wait_ge(proj_free[p % 4], p // 4)
                return bank[p % 4]

            def proj_rows(name, chunk_name, act, n=512):
                w = weights(pe, chunk_name)
                kt = w.shape[1]
                for t in range(TT):
                    ps = begin_proj((name, t))
                    for k in range(kt):
                        mm = pe.matmul(ps[:, 0:n], act[:, k, 128 * t:128 * t + 128], w[:, k, 0:n],
                                       start=(k == 0), stop=(k == kt - 1))
                    mm.then_inc(proj_done, 1)

            def proj_cols(name, chunk_name, act):
                w = weights(pe, chunk_name)
                kt = w.shape[1]
                for j in range(4):
                    ps = begin_proj((name, j))
                    for k in range(kt):
                        mm = pe.matmul(ps[:, :], w[:, k, 128 * j:128 * j + 128], act[:, k, :],
                                       start=(k == 0), stop=(k == kt - 1))
                    mm.then_inc(proj_done, 1)

            def turn(name, blocks):
                ps = begin_aux(name)
                at = 0
                for b in blocks:
                    p, f = b.shape[0], int(np.prod(b.shape[1:]))
                    mm = pe.transpose(ps[0:f, at:at + p], b, ident[0:p, 0:p])
                    at += p
                mm.then_inc(aux_done, 1)

            pe.wait_ge(consts_in, 16)
            pe.wait_ge(rows_in, 16 * NROWS)
            turn("cols", [colr[0:62, :]])
            pe.wait_ge(lam_in, 64)
            turn("lam", [lraw[0:32, 0, :], lraw[0:32, 1, :]])
            pe.wait_ge(craw_in, 64)
            for a in range(2):
                turn(f"c{a + 1}", [craw[:, a, m, :] for m in range(4)])
            pe.wait_ge(rb_in_s, 16)
            pe.wait_ge(rb_one, 1)
            pe.wait_ge(onehot_in, 16)
            for name, c0, n in (("rb", 0, 512), ("rb2", 512, 128)):
                pe.matmul(begin_aux(name)[0:8, 0:n], rb_in[0:33, :], onehot[0:33, c0:c0 + n],
                          start=True, stop=True).then_inc(aux_done, 1)
            pe.wait_ge(silc_done, 1)
            ps = begin_aux("mod")
            for j in range(4):
                w = weights(pe, ("ada", j))
                for m in range(4):
                    for k in range(KT):
                        mm = pe.matmul(ps[:, 4 * j + m:4 * j + m + 1], w[:, k, 128 * m:128 * m + 128],
                                       silc[:, k:k + 1], start=(k == 0), stop=(k == KT - 1))
                if j < 3:
                    mm.then_inc(chunk_used, 1)
                else:
                    mm.then_inc(aux_done, 1)

            def x_turns(key, src, ready):
                pe.wait_ge(*ready)
                for k in range(KT):
                    turn((key, k), [src[:, t, 128 * k:128 * k + 128] for t in range(TT)])

            x_turns("x", xrow, (xn_done, TT))

            def ssm_kernels(q):
                pe.wait_ge(cl_done, q + 1)
                if q == 0:
                    pe.wait_ge(prep_y, 1)
                for a in range(2):
                    ps = begin_aux(("k", q, a))
                    for b in range(4):
                        g = 4 * a + b
                        mm = pe.matmul(ps[0:GC, 128 * b:128 * b + 128], Y1[:, QG * q + g, :],
                                       CL[:, g, 0:L, :].rearrange("p a b -> p (a b)"), start=True, stop=True)
                    mm.then_inc(aux_done, 1)
                pe.wait_ge(zt_done, q + 1)
                for a in range(2):
                    turn(("z", q, a), [Zt[:, 4 * a + b, :, :].rearrange("p a b -> p (a b)") for b in range(4)])

            def ssm_chunks(q):
                pe.wait_ge(U_in, 16 * L)
                aux_out(pe, ("z", q, 0))
                aux_out(pe, ("z", q, 1))
                ps = begin_aux(("v", q))
                for g in range(QG):
                    mm = pe.matmul(ps[:, NCH * g:NCH * g + NCH], Wn[:, g, :], U[:, QG * q + g, :],
                                   start=True, stop=True)
                mm.then_inc(aux_done, 1)

            def ssm_out(q):
                pe.wait_ge(t_in, 16 * L * (q + 1))
                pe.wait_ge(s_done, q + 1)
                ps = begin_aux(("y", q))
                for g in range(QG):
                    pe.matmul(ps[:, NCH * g:NCH * g + NCH], Tm[:, g, :], U[:, QG * q + g, :],
                              start=True, stop=False)
                    mm = pe.matmul(ps[:, NCH * g + 1:NCH * g + NCH],
                                   CL[:, g, 1:L + 1, :].rearrange("p a b -> p (a b)"), Vb[:, g, 0:NCH - 1],
                                   start=False, stop=True)
                mm.then_inc(aux_done, 1)

            def one_rows(name, t, chunk_name, act, n=512):
                w = weights(pe, chunk_name)
                kt = w.shape[1]
                ps = begin_proj((name, t))
                for k in range(kt):
                    mm = pe.matmul(ps[:, 0:n], act[:, k, 128 * t:128 * t + 128], w[:, k, 0:n],
                                   start=(k == 0), stop=(k == kt - 1))
                mm.then_inc(proj_done, 1)

            def one_cols(name, j, chunk_name, act):
                w = weights(pe, chunk_name)
                kt = w.shape[1]
                ps = begin_proj((name, j))
                for k in range(kt):
                    mm = pe.matmul(ps[:, :], w[:, k, 128 * j:128 * j + 128], act[:, k, :],
                                   start=(k == 0), stop=(k == kt - 1))
                mm.then_inc(proj_done, 1)

            for k in range(KT):
                aux_out(pe, ("x", k))
            proj_cols("u", "u", hT)
            ssm_kernels(0)
            one_cols("qi", 0, "qi", hT)
            one_cols("qi", 1, "qi", hT)
            one_cols("qi", 2, "qi", hT)
            ssm_chunks(0)
            one_cols("qi", 3, "qi", hT)
            w = weights(pe, "ki")
            ps = begin_proj("ki")
            for k in range(KT):
                mm = pe.matmul(ps[:, :], w[:, k, 0:128], hT[:, k, :], start=(k == 0), stop=(k == KT - 1))
            mm.then_inc(proj_done, 1)
            ps = begin_proj("wi")
            for t in range(TT):
                for k in range(KT):
                    mm = pe.matmul(ps[:, 8 * t:8 * t + 8], hT[:, k, 128 * t:128 * t + 128], w[:, k, 128:136],
                                   start=(k == 0), stop=(k == KT - 1))
            mm.then_inc(proj_done, 1)
            ssm_out(0)
            proj_out(pe, ("qi", 3))
            proj_out(pe, ("qi", 2))
            proj_out(pe, ("qi", 1))
            proj_out(pe, ("qi", 0))
            proj_out(pe, "ki")
            for i in range(1, TT):
                for h in range(8):
                    r = 64 * (h % 2)
                    n = 128 * (i + 1)
                    pe.matmul(begin_aux(("rel", i, h))[:, 0:n], qiT[r:r + 64, h // 2, 128 * i:128 * i + 128],
                              kiT[r:r + 64, 0:n], start=True, stop=True).then_inc(aux_done, 1)
                if i == 1:
                    ssm_kernels(1)
                if i == 2:
                    ssm_chunks(1)
            ssm_out(1)
            one_rows("k", 0, "k", hT)
            one_rows("k", 1, "k", hT)
            ssm_kernels(2)
            one_rows("k", 2, "k", hT)
            one_rows("k", 3, "k", hT)
            ssm_chunks(2)
            one_rows("q", 0, "q", hT)
            one_rows("q", 1, "q", hT)
            pe.wait_ge(knorm_done, TT)
            for m in range(4):
                turn(("kt", m), [row[:, t, 128 * m:128 * m + 128] for t in range(TT)])
            ssm_out(2)
            one_rows("q", 2, "q", hT)
            ssm_kernels(3)
            one_rows("q", 3, "q", hT)
            one_rows("v", 0, "v", hT)
            ssm_chunks(3)
            one_rows("v", 1, "v", hT)
            pe.wait_ge(qnorm_done, TT)
            for m in range(4):
                turn(("qt", m), [row[:, t, 128 * m:128 * m + 128] for t in range(TT)])
            one_rows("v", 2, "v", hT)
            ssm_out(3)
            one_rows("v", 3, "v", hT)
            one_rows("az", 0, "az", hT)

            def fill1(name):
                if name in ("gate0", "gate1"):
                    pe.wait_ge(silb_done, 1)
                    w = weights(pe, ("gate", int(name[4])))
                    ps = begin_proj(name)
                    for k in range(KT):
                        mm = pe.matmul(ps[:, :], silb[:, k, :], w[:, k, :], start=(k == 0), stop=(k == KT - 1))
                    mm.then_inc(proj_done, 1)
                elif name[0] == "az":
                    one_rows("az", name[1], "az", hT)
                elif name[0] == "z":
                    one_cols("z", name[1], "z", hT)
                else:
                    pe.wait_ge(z_done, TT)
                    one_cols("glu", name[1], "glu", zz)


            pe.wait_ge(bias_in, 32)
            for h in range(8):
                pe.matmul(begin_aux(("flip", h))[:, :], gt[:, 0, 0:128], biasR[:, h, :],
                          start=True, stop=True).then_inc(aux_done, 1)
            for m in range(4):
                aux_out(pe, ("kt", m))
                aux_out(pe, ("qt", m))
                proj_out(pe, ("v", m))
            for n in range(NU1 + 2):
                if n < NU1:
                    i, h = UNITS1[n]
                    r = 64 * (h % 2)
                    pe.matmul(begin_proj(("qk", n))[:, 0:128 * (i + 1)],
                              qT[r:r + 64, h // 2, 128 * i:128 * i + 128],
                              kT[r:r + 64, h // 2, 0:128 * (i + 1)], start=True, stop=True).then_inc(proj_done, 1)
                if 0 <= n - 1 < NU1:
                    i, h = UNITS1[n - 1]
                    pe.wait_ge(exp_done, n)
                    turn(("pt", n - 1), [pr[:, (n - 1) % 2, 128 * b:128 * b + 128] for b in range(i + 1)])
                if 0 <= n - 2 < NU1:
                    i, h = UNITS1[n - 2]
                    aux_out(pe, ("pt", n - 2))
                    ps = begin_aux(("pv", n - 2))
                    for b in range(i + 1):
                        mm = pe.matmul(ps[:, 0:64], pT[:, (n - 2) % 2, 128 * b:128 * b + 128],
                                       v1[:, b, 64 * h:64 * h + 64], start=(b == 0), stop=(b == i))
                    mm.then_inc(aux_done, 1)
                if n in FILL1:
                    fill1(FILL1[n])
            pe.wait_ge(o_done, NU1)
            for m in range(4):
                turn(("ot", m), [orow[:, t, 128 * m:128 * m + 128] for t in range(TT)])
            pe.wait_ge(ys_done, TT)
            for m in range(4):
                aux_out(pe, ("ot", m))
            for t in range(TT):
                for j in range(2):
                    w = weights(pe, ("out", j))
                    ps = begin_proj((f"out{j}", t))
                    for k in range(KT):
                        a = yT[:, k, :] if k < 4 else oT[:, k - 4, :]
                        mm = pe.matmul(ps[:, :], a[:, 128 * t:128 * t + 128], w[:, k, :],
                                       start=(k == 0), stop=(k == KT - 1))
                    mm.then_inc(proj_done, 1)

            x_turns("h2", xn2, (xn_done, 2 * TT))
            pe.wait_ge(small_in, 16 * 4)
            turn("pos", [posr[0:64, :]])
            for k in range(KT):
                aux_out(pe, ("h2", k))
            proj_cols("up", "up", hT)
            proj_rows("kv1", "kv1", hT)
            proj_rows("kv2", "kv2", hT, 304)
            proj_rows("q2a", "q2a", hT)
            pe.wait_ge(kdup_done, TT)
            for n in range(4):
                turn(("ks", n), [kdup[:, t, 128 * n:128 * n + 128] for t in range(TT)])
            turn(("kc", 0), [kvr[:, t, 0:128] for t in range(TT)])
            turn(("kc", 1), [kvr[:, t, 128:256] for t in range(TT)])
            aux_out(pe, "pos")
            for a in range(2):
                w = weights(pe, ("c1", a))
                aux_out(pe, ("kc", a))
                for g in range(2):
                    r = slice(64 * g, 64 * g + 64)
                    ps = begin_aux(("hid", a, g))
                    for l in range(32):
                        mm = pe.matmul(ps[:, 0:NCMP], w[r, l, :], kcT[r, a, l:l + 16 * (NCMP - 1) + 1:16],
                                       start=(l == 0), stop=(l == 31))
                    if g == 0:
                        for l in range(32):
                            mm = pe.matmul(ps[:, 31:32], w[r, l, :], posT[r, a, l:l + 1],
                                           start=(l == 0), stop=(l == 31))
                    mm.then_inc(aux_done, 1)
            proj_rows("q2b", "q2b", hT)
            pe.wait_ge(qrope_done, TT)
            for m in range(4):
                turn(("qt2", m), [row2[:, t, 128 * m:128 * m + 128] for t in range(TT)])
            pe.wait_ge(hid_done, 2)
            ps = begin_aux("kcm")
            for g in range(2):
                mm = pe.matmul(ps[:, 32 * g:32 * g + NCMP], w2s[:, 0:128], hid[:, 0, 32 * g:32 * g + NCMP],
                               start=True, stop=True)
            mm.then_inc(aux_done, 1)
            ps = begin_aux("vcm")
            for r in range(4):
                for g in range(2):
                    mm = pe.matmul(ps[32 * r:32 * r + NCMP, 64 * g:64 * g + 64], hid[:, 1, 32 * g:32 * g + NCMP],
                                   w2s[:, 128:192], start=True, stop=True)
            mm.then_inc(aux_done, 1)
            proj_rows("m00", "m00", hT)
            pe.wait_ge(qrope_done, 2 * TT)
            for m in range(4):
                turn(("qt2", 4 + m), [q2b[:, t, 128 * m:128 * m + 128] for t in range(TT)])
            pe.wait_ge(pooled_done, 4)
            pe.wait_ge(pw_in, 16)
            for j in range(4):
                pe.matmul(begin_proj(("ypm", j))[:, :], pwS[:, j, :], plT[:, j, :], start=True, stop=True)\
                    .then_inc(proj_done, 1)
            for j in range(4):
                proj_out(pe, ("ypm", j))

            def fill2(name):
                key, t = name
                one_rows(key, t, key, ypT if key[0] == "y" else hT)

            for m in range(8):
                aux_out(pe, ("qt2", m))
            for n in range(4):
                aux_out(pe, ("ks", n))
            aux_out(pe, "kcm")
            aux_out(pe, "vcm")
            for i in range(TT + 1):
                if i < TT:
                    for odd in range(2):
                        r = slice(64 * odd, 64 * odd + 64)
                        ps = begin_aux(("cq", i, odd))
                        for h in range(odd, 16, 2):
                            mm = pe.matmul(ps[:, 16 * (h - odd):16 * (h - odd) + NCMP],
                                           qT2[r, h // 2, 128 * i:128 * i + 128], kcmp[r, h // 8, 0:NCMP],
                                           start=True, stop=True)
                        mm.then_inc(aux_done, 1)
                if i >= 1:
                    pe.wait_ge(cexp_done, i)
                    turn(("cp", i - 1), [pc[:, (i - 1) % 2, 128 * b:128 * b + 128] for b in range(4)])
                    aux_out(pe, ("cp", i - 1))
                    for a in range(2):
                        ps = begin_aux(("cv", i - 1, a))
                        for b in range(2):
                            mm = pe.matmul(ps[:, 256 * b:256 * b + 256], pTc[:, 128 * (2 * a + b):128 * (2 * a + b) + 128],
                                           vbd[:, a, :], start=True, stop=True)
                        mm.then_inc(aux_done, 1)
                if i in FILLC:
                    fill2(FILLC[i])
            for n in range(NU2 + 2):
                if n < NU2:
                    i, h = UNITS2[n]
                    r = slice(64 * (h % 2), 64 * (h % 2) + 64)
                    for b, key in enumerate(("qs", "qw")):
                        pe.matmul(begin_proj((key, n))[:, 0:128 * (i + 1)], qT2[r, h // 2, 128 * i:128 * i + 128],
                                  ksT[r, 2 * b + h // 8, 0:128 * (i + 1)], start=True, stop=True).then_inc(proj_done, 1)
                if 0 <= n - 1 < NU2:
                    i, h = UNITS2[n - 1]
                    for b, key in enumerate(("ps", "pw")):
                        pe.wait_ge(exp2_done, 2 * (n - 1) + b + 1)
                        turn((key, n - 1), [pr2[:, (n - 1) % 2, b, 128 * m:128 * m + 128] for m in range(i + 1)])
                if 0 <= n - 2 < NU2:
                    i, h = UNITS2[n - 2]
                    aux_out(pe, ("ps", n - 2))
                    aux_out(pe, ("pw", n - 2))
                    ps = begin_aux(("pv2", n - 2))
                    for b in range(2):
                        for m in range(i + 1):
                            mm = pe.matmul(ps[:, 64 * b:64 * b + 64], pT2[:, (n - 2) % 2, b, 128 * m:128 * m + 128],
                                           vs2[:, b, m, 64 * (h // 8):64 * (h // 8) + 64],
                                           start=(m == 0), stop=(m == i))
                    mm.then_inc(aux_done, 1)
                if n in FILL2:
                    fill2(FILL2[n])
            pe.wait_ge(o2_done, NU2)
            for m in range(8):
                turn(("o2", m), [ob[:, t, 128 * m:128 * m + 128] for t in range(TT)])
            for m in range(8):
                aux_out(pe, ("o2", m))
            proj_rows("ya0", "ya0", oT2)
            proj_rows("ya1", "ya1", oT2)
            pe.wait_ge(mg_done, 2 * TT)
            for m in range(8):
                turn(("mt", m), [mg[:, t, 128 * m:128 * m + 128] for t in range(TT)])
            for m in range(8):
                aux_out(pe, ("mt", m))
            proj_rows("wo0", "wo0", mT)
            proj_rows("wo1", "wo1", mT)

            pe.wait_ge(conv_in, 16 * 16)
            for a in range(2):
                turn(("cvt", a), [cvr[0:88, a, :]])
            x_turns("h3", xn3, (xn_done, 3 * TT))
            for k in range(KT):
                aux_out(pe, ("h3", k))
            for j in range(FT):
                w = weights(pe, ("f", j // 2))
                m = 128 if j < FT - 1 else 64
                for a, key in enumerate(("fg", "fv")):
                    c0 = 256 * a + 128 * (j % 2)
                    ps = begin_proj((key, j))
                    for k in range(KT):
                        mm = pe.matmul(ps[0:m, :], w[:, k, c0:c0 + m], hT[:, k, :], start=(k == 0), stop=(k == KT - 1))
                    mm.then_inc(proj_done, 1)
            pe.wait_ge(act_done, FT)
            for a in range(2):
                banks = [begin_proj((f"dn{a}", t)) for t in range(TT)]
                for b in range(3):
                    w = weights(pe, ("d", a, b))
                    for t in range(TT):
                        for k in range(8 * b, min(8 * b + 8, FT)):
                            m = 128 if k < FT - 1 else 64
                            mm = pe.matmul(banks[t][:, :], aT[0:m, k, 128 * t:128 * t + 128], w[0:m, k - 8 * b, :],
                                           start=(k == 0), stop=(k == FT - 1))
                        if b == 2:
                            mm.then_inc(proj_done, 1)
                    if b < 2:
                        mm.then_inc(chunk_used, 1)

        @block.scalar
        def _(act):
            step = Steps(act, act_step)
            act.dma_start(ident, k_ident).then_inc(consts_in, 16)
            for at, n, src in ROWS:
                act.dma_start(colr[at:at + n, :], src).then_inc(rows_in, 16)
            for a, src in ((0, a_re), (1, a_im)):
                for half in range(2):
                    act.dma_start(lraw[0:32, a, 64 * half:64 * half + 64], src[0]).then_inc(lam_in, 16)
            for a in range(2):
                for half in range(2):
                    src = (c_re, c_im)[(a + half) % 2]
                    act.dma_start(craw[:, a, :, 64 * half:64 * half + 64],
                                  src[0].rearrange("(m g) o p -> (g o) m p", g=8)).then_inc(craw_in, 16)
            act.dma_start(bre[0:64, :, :], b_re[0].rearrange("g p i -> p g i")).then_inc(b_in, 16)
            act.dma_start(bim[0:64, :, :], b_im[0].rearrange("g p i -> p g i")).then_inc(b_in, 16)
            aux_ready(act, "lam")
            act.activation(sp[:, 2:4, :], abank("lam")[:, 0:64].rearrange("p (a b) -> p a b", a=2), ACT.Copy)\
               .then_inc(afree("lam"), 1)
            for name, dst, top_scale in (("c1", X1, 1.0), ("c2", X2, -1.0)):
                aux_ready(act, name)
                for r, f in ((slice(0, 64), top_scale), (slice(64, 128), -1.0)):
                    ins = act.activation(dst[r, :, :].rearrange("p a b -> p (a b)"), abank(name)[r, :], ACT.Copy, scale=f)
                ins.then_inc(afree(name), 1)
            act.wait_ge(b_in, 32)
            for b_ in (bre, bim):
                act.dma_start(b_[64:128, :, :], b_[0:64, :, :]).then_inc(b_in2, 16)
            for name, c0, n in (("rb", 0, 512), ("rb2", 512, 128)):
                aux_ready(act, name)
                act.activation(rb_row[0:8, c0:c0 + n], abank(name)[0:8, 0:n], ACT.Copy).then_inc(afree(name), 1)

            aux_ready(act, "cols")
            act.wait_ge(vec_step, 1)
            act.activation(silc[:, 8:16], colv[:, CV_C:CV_C + 8], ACT.Tanh, scale=0.5).then_inc(act_tanhc, 1)

            act.wait_ge(mod_done, 1)
            for k in range(KT):
                aux_ready(act, ("x", k))
                act.activation(hT[:, k, :], abank(("x", k))[:, :], ACT.Identity, scale=modc[:, 8 + k:9 + k],
                               bias=modc[:, k:k + 1]).then_inc(afree(("x", k)), 1)

            def ssm_kernels(q):
                for a in range(2):
                    aux_ready(act, ("k", q, a))
                    if a == 0 and q == 0:
                        act.wait_ge(pool_ones, 1)
                    if a == 0 and q:
                        act.wait_ge(t_in, 16 * L * q)
                    act.activation(Kx[0:GC, 4 * a:4 * a + 4, 112:240],
                                   abank(("k", q, a))[0:GC, :].rearrange("p (a b) -> p a b", a=4),
                                   ACT.Copy).then_inc(afree(("k", q, a)), 1)
                for a in range(2):
                    aux_ready(act, ("z", q, a))
                    act.activation(Wn[:, 4 * a:4 * a + 4, :],
                                   abank(("z", q, a))[:, :].rearrange("p (a b) -> p a b", a=4),
                                   ACT.Copy).then_inc(afree(("z", q, a)), 1)

            def ssm_chunks(q):
                aux_ready(act, ("v", q))
                if q:
                    act.wait_ge(aux_done, AUX[("y", q - 1)] + 1)
                act.activation(Vb, abank(("v", q))[:, :].rearrange("p (a b) -> p a b", a=QG),
                               ACT.Copy).then_inc(afree(("v", q)), 1)

            def ssm_out(q):
                aux_ready(act, ("y", q))
                act.activation(Vs, abank(("y", q))[:, :].rearrange("p (a b) -> p a b", a=QG),
                               ACT.Copy).then_inc(afree(("y", q)), 1)

            for j in range(4):
                proj_ready(act, ("u", j))
                act.activation(u[:, j, :].rearrange("p (s c) -> p s c", s=L),
                               pbank(("u", j))[:, :].rearrange("p (c s) -> p s c", s=L),
                               ACT.Copy).then_inc(pfree(("u", j)), 1)
            ssm_kernels(0)
            for j in range(4):
                if j == 3:
                    ssm_chunks(0)
                proj_ready(act, ("qi", j))
                act.activation(qiT[:, j, :], pbank(("qi", j))[:, :], ACT.Copy).then_inc(pfree(("qi", j)), 1)
            proj_ready(act, "ki")
            act.activation(kiT, pbank("ki")[:, :], ACT.Copy).then_inc(pfree("ki"), 1)
            proj_ready(act, "wi")
            act.activation(wi, pbank("wi")[:, 0:32].rearrange("p (a b) -> p a b", a=TT), ACT.Copy,
                           scale=8 ** -0.5).then_inc(pfree("wi"), 1)
            ssm_out(0)
            m = 0
            for i in range(1, TT):
                for h in range(8):
                    aux_ready(act, ("rel", i, h))
                    if m >= 2:
                        act.wait_ge(rel_used, m - 1)
                    n = 128 * (i + 1)
                    act.activation(reluq[:, m % 2, 0:n], abank(("rel", i, h))[:, 0:n], ACT.Relu)\
                       .then_inc(afree(("rel", i, h)), 1)
                    m += 1
                if i == 1:
                    ssm_kernels(1)
                if i == 2:
                    ssm_chunks(1)
            ssm_out(1)

            def rows_in_(name, dst, ts=range(TT)):
                for t in ts:
                    proj_ready(act, (name, t))
                    act.activation(dst[:, t, :], pbank((name, t))[:, :], ACT.Copy)\
                       .then_inc(pfree((name, t)), 1)

            def columns_in(name, dst):
                for m in range(4):
                    aux_ready(act, (name, m))
                    act.activation(dst[:, m, :], abank((name, m))[:, :], ACT.Copy)\
                       .then_inc(afree((name, m)), 1)

            rows_in_("k", row, (0, 1))
            ssm_kernels(2)
            rows_in_("k", row, (2, 3))
            ssm_chunks(2)
            columns_in("kt", kT)
            aux_ready(act, ("kt", 3))
            rows_in_("q", row, (0, 1))
            ssm_out(2)
            rows_in_("q", row, (2,))
            ssm_kernels(3)
            rows_in_("q", row, (3,))
            rows_in_("v", v1, (0,))
            ssm_chunks(3)
            rows_in_("v", v1, (1,))
            act.wait_ge(rb_saved, 16)
            columns_in("qt", qT)
            rows_in_("v", v1, (2,))
            ssm_out(3)
            rows_in_("v", v1, (3,))

            def az_in(t):
                proj_ready(act, ("az", t))
                act.activation(az[:, t, :], pbank(("az", t))[:, :], ACT.Tanh, scale=0.5).then_inc(az_tanh, 1)

            def fill1(name):
                if name[0] == "az":
                    az_in(name[1])
                elif name[0] == "z":
                    j = name[1]
                    proj_ready(act, ("z", j))
                    act.activation(sz[:, j, :].rearrange("p (s c) -> p s c", s=L),
                                   pbank(("z", j))[:, :].rearrange("p (c s) -> p s c", s=L),
                                   ACT.Tanh, scale=0.5).then_inc(sz_tanh, 1)
                elif name[0] == "glu":
                    j = name[1]
                    proj_ready(act, ("glu", j))
                    act.wait_ge(gbias_done, 1)
                    if j >= 2:
                        act.wait_ge(ys_done, j - 1)
                    act.activation(gt[:, j % 2, :], pbank(("glu", j))[:, :], ACT.Tanh, scale=0.25,
                                   bias=colv[:, CV_BGLU + j:CV_BGLU + j + 1]).then_inc(pfree(("glu", j)), 1)

            az_in(0)
            for n in range(NU1 + 1):
                if n < NU1:
                    i, h = UNITS1[n]
                    act.wait_ge(lg_done, n + 1)
                    if n >= 2:
                        act.wait_ge(aux_done, AUX[("pt", n - 2)] + 1)
                        act.wait_ge(o_done, n - 1)
                    act.activation(pr[:, n % 2, 0:128 * (i + 1)], lg[:, n % 2, 0:128 * (i + 1)], ACT.Exp,
                                   scale=-1.0, bias=sml[:, n % 2:n % 2 + 1],
                                   accum_out=sml[:, 2 + n % 2:3 + n % 2]).then_inc(exp_done, 1)
                if n >= 1:
                    i, h = UNITS1[n - 1]
                    aux_ready(act, ("pt", n - 1))
                    if n >= 3:
                        act.wait_ge(aux_done, AUX[("pv", n - 3)] + 1)
                    act.activation(pT[:, (n - 1) % 2, 0:128 * (i + 1)], abank(("pt", n - 1))[:, 0:128 * (i + 1)],
                                   ACT.Copy).then_inc(afree(("pt", n - 1)), 1)
                if n in FILL1:
                    fill1(FILL1[n])
                if n in (3, 6, 9, 12):
                    j = n // 3 - 1
                    act.wait_ge(y_skip, j + 1)
                    act.activation(gt[:, j % 2, :], gt[:, j % 2, :], ACT.Tanh, scale=SQ2PI).then_inc(y_tanh, 1)
            columns_in("ot", oT)

            def scaled_columns_in(key, n, col):
                for k in range(n):
                    aux_ready(act, (key, k))
                    act.activation(hT[:, k, :], abank((key, k))[:, :], ACT.Copy,
                                   scale=colv[:, col + k:col + k + 1]).then_inc(afree((key, k)), 1)

            def many_columns_in(key, dst, ms, src=None):
                for m in ms:
                    aux_ready(act, (key, m))
                    act.activation(dst[:, m, :], abank((key, m))[:, :], ACT.Copy).then_inc(afree((key, m)), 1)

            act.wait_ge(x1_done, 2 * TT)
            act.dma_start(posr[0:64, :], cmp_pos_2[0].rearrange("a l d -> (a l) d")).then_inc(small_in, 16)
            for c0 in (0, 64):
                act.dma_start(w2s[:, c0:c0 + 64], cmp_w2_2[0, 0]).then_inc(small_in, 16)
            act.dma_start(w2s[:, 128:192], cmp_w2_2[0, 1]).then_inc(small_in, 16)
            scaled_columns_in("h2", KT, CV_G2)
            aux_ready(act, "pos")
            act.activation(posT[0:64, :, :], abank("pos")[0:64, 0:64].rearrange("p (a b) -> p a b", a=2), ACT.Copy)\
               .then_inc(afree("pos"), 1)
            for j in range(4):
                proj_ready(act, ("up", j))
                act.activation(upT[:, j, :], pbank(("up", j))[:, :], ACT.Copy).then_inc(pfree(("up", j)), 1)
            for t in range(TT):
                proj_ready(act, ("kv1", t))
                act.activation(kvr[:, t, 0:384], pbank(("kv1", t))[:, 0:384], ACT.Copy)
                act.activation(vs2[:, 0, t, :], pbank(("kv1", t))[:, 384:512], ACT.Copy)\
                   .then_inc(pfree(("kv1", t)), 1)
            for t in range(TT):
                proj_ready(act, ("kv2", t))
                act.activation(kvr[:, t, 384:512], pbank(("kv2", t))[:, 0:128], ACT.Copy)
                act.activation(vs2[:, 1, t, :], pbank(("kv2", t))[:, 128:256], ACT.Copy)
                act.activation(ngs[:, t, :], pbank(("kv2", t))[:, 256:304], ACT.Tanh, scale=0.5)\
                   .then_inc(pfree(("kv2", t)), 1)
            rows_in_("q2a", row2)
            many_columns_in("ks", ksT, range(4))
            many_columns_in("kc", kcT, range(2))
            act.wait_ge(hid_in, 1)
            act.activation(hid[:, 2:4, :].rearrange("p a b -> p (a b)")[:, 0:127],
                           hid[:, 2:4, :].rearrange("p a b -> p (a b)")[:, 0:127], ACT.Tanh, scale=SQ2PI)\
               .then_inc(hid_tanh, 1)
            rows_in_("q2b", q2b)
            many_columns_in("qt2", qT2, range(4))

            def tanh_rows(name, dst, c0, ts=range(TT)):
                for t in ts:
                    proj_ready(act, (name, t))
                    act.activation(dst[:, t, c0:c0 + 512], pbank((name, t))[:, :], ACT.Tanh, scale=0.5)\
                       .then_inc(pfree((name, t)), 1)

            aux_ready(act, "kcm")
            act.activation(kcmp[:, :, 0:NCMP], abank("kcm")[:, 0:64].rearrange("p (a b) -> p a b", a=2)[:, :, 0:NCMP],
                           ACT.Copy).then_inc(afree("kcm"), 1)
            aux_ready(act, ("qt2", 7))
            many_columns_in("qt2", qT2, range(4, 8))
            tanh_rows("m00", mg, 0)
            for j in range(4):
                proj_ready(act, ("ypm", j))
                act.activation(ypT[:, j, :], pbank(("ypm", j))[:, :], ACT.Copy,
                               scale=colv[:, CV_PS + j:CV_PS + j + 1]).then_inc(pfree(("ypm", j)), 1)
            for i in range(TT + 1):
                if i < TT:
                    act.wait_ge(clg_done, i + 1)
                    pv_ = pc[:, i % 2, :].rearrange("p (a b) -> p a b", a=16)[:, :, 0:NCMP]
                    act.activation(pv_, pv_, ACT.Exp).then_inc(cexp_done, 1)
                if i >= 1:
                    aux_ready(act, ("cp", i - 1))
                    if i >= 2:
                        act.wait_ge(aux_done, AUX[("cv", i - 2, 1)] + 1)
                    act.activation(pTc, abank(("cp", i - 1))[:, :], ACT.Copy).then_inc(afree(("cp", i - 1)), 1)
            for n in range(NU2 + 1):
                if n < NU2:
                    i, h = UNITS2[n]
                    for b in range(2):
                        act.wait_ge(lg2_done, 2 * n + b + 1)
                        if n >= 2 and b == 0:
                            act.wait_ge(o2_done, n - 1)
                        buf = pr2[:, n % 2, b, 0:128 * (i + 1)]
                        act.activation(buf, buf, ACT.Exp, scale=-1.0, bias=sml[:, 16 + 2 * (n % 2) + b:17 + 2 * (n % 2) + b],
                                       accum_out=sml[:, 20 + 2 * (n % 2) + b:21 + 2 * (n % 2) + b]).then_inc(exp2_done, 1)
                if n >= 1:
                    i, h = UNITS2[n - 1]
                    if n >= 3:
                        act.wait_ge(aux_done, AUX[("pv2", n - 3)] + 1)
                    for b, key in enumerate(("ps", "pw")):
                        aux_ready(act, (key, n - 1))
                        act.activation(pT2[:, (n - 1) % 2, b, 0:128 * (i + 1)], abank((key, n - 1))[:, 0:128 * (i + 1)],
                                       ACT.Copy).then_inc(afree((key, n - 1)), 1)
                if n in FILL2 and FILL2[n][0] != "yp1":
                    key, t = FILL2[n]
                    tanh_rows(key, {"m01": mg, "m10": row2, "m11": plT}[key], 512 * (key == "m01"), (t,))
            many_columns_in("o2", oT2, range(8))
            many_columns_in("mt", mT, range(8))
            scaled_columns_in("h3", KT, CV_GF)
            for j in range(FT):
                m = 128 if j < FT - 1 else 64
                for a, key in enumerate(("fg", "fv")):
                    proj_ready(act, (key, j))
                    if a == 0 and j == 0:
                        act.wait_ge(cvw_done, 2)
                    if a == 0 and j >= 2:
                        act.wait_ge(act_done, j - 1)
                    act.activation(fc[0:m, j % 2, a, :], pbank((key, j))[0:m, :], ACT.Identity,
                                   scale=cvw[0:m, a, 2, j:j + 1], bias=cvw[0:m, a, 3, j:j + 1]).then_inc(tap_done, 1)
                act.wait_ge(gatec_done, j + 1)
                act.activation(ft[0:m, j % 2, :], fc[0:m, j % 2, 0, :], ACT.Tanh, scale=0.5).then_inc(ftanh_done, 1)

        @block.gpsimd
        def _(pool):
            step = Steps(pool, pool_step)
            pool.dma_start(onehot[0:33, :], k_bucket).then_inc(onehot_in, 16)
            pool.dma_start(rb_in[0:32, :], rel_bias).then_inc(rb_in_s, 16)
            pool.memset(rb_in[32:33, :], 1.0).then_inc(rb_one, 1)
            pool.wait_ge(rb_one, 1)
            pool.dma_start(sp[:, 0, :], log_dt[0:1, :].partition_broadcast(128)).then_inc(ldt_in, 16)
            for a, src in enumerate(GAINS):
                pool.dma_start(gains[:, 64 * a:64 * a + 64], src.partition_broadcast(128)).then_inc(gains_in, 16)
            step(pool.memset(halves, -0.5))
            n_roots = [0]

            def root(cols):
                n_roots[0] += 1
                pool.wait_ge(ms_done, n_roots[0])
                n = cols.stop - cols.start
                pool.tensor_tensor(stat[:, cols], stat[:, cols], halves[:, 0:n], ALU.pow).then_inc(root_done, 1)

            root(slice(0, TT))
            pool.dma_start(trim, k_tri).then_inc(consts_in2, 16)
            pool.dma_start(ropeT, k_rope).then_inc(consts_in2, 16)
            pool.dma_start(cmpmask, k_cmpmask).then_inc(consts_in2, 16)
            pool.dma_start(rowvalid, k_rowvalid).then_inc(consts_in2, 16)
            pool.dma_start(cnt, k_cnt).then_inc(consts_in2, 16)
            pool.wait_ge(consts_in2, 80)
            aux_out(pool, "rb")
            aux_out(pool, "rb2")
            pool.dma_start(rb_dram, rb_row[0:8, :]).then_inc(rb_saved, 16)
            for q in range(NQ):
                gs = slice(QG * q, QG * q + QG)
                Xa = [X_[:, gs, :].unsqueeze(2).broadcast_to((128, QG, 9, GC)) for X_ in (X1, X2)]
                Pa = [pw[:, a, :, gs].rearrange("p j g -> p g j").unsqueeze(3).broadcast_to((128, QG, 9, GC))
                      for a in range(2)]
                g1v = g1.rearrange("p (a b c) -> p a b c", a=QG, b=9)
                g2v = g2.rearrange("p (a b c) -> p a b c", a=QG, b=9)
                if q == 0:
                    pool.wait_ge(prep_x, 1)
                    pool.wait_ge(prep_y, 1)
                    step(pool.memset(Kx[0:GC, :, 0:112], 0.0))
                    pool.memset(r8[:, :, 0:1], 0.0).then_inc(pool_ones, 1)
                else:
                    aux_ready(pool, ("y", q - 1))
                pool.tensor_tensor(g1v, Xa[0], Pa[0], ALU.mult)
                step(pool.tensor_tensor(g2v, Xa[1], Pa[1], ALU.mult))
                step(pool.tensor_tensor(CL, g1v, g2v, ALU.add))
                pool.sem_inc(cl_done, 1)
                Ya = [Y_[:, gs, :].unsqueeze(2).broadcast_to((128, QG, L, GC)) for Y_ in (Y1, Y2)]
                Pa = [pw[:, a, 7::-1, gs].rearrange("p j g -> p g j").unsqueeze(3).broadcast_to((128, QG, L, GC))
                      for a in range(2)]
                g1v = g1[:, 0:1024].rearrange("p (a b c) -> p a b c", a=QG, b=L)
                g2v = g2[:, 0:1024].rearrange("p (a b c) -> p a b c", a=QG, b=L)
                pool.tensor_tensor(g1v, Ya[0], Pa[0], ALU.mult)
                step(pool.tensor_tensor(g2v, Ya[1], Pa[1], ALU.mult))
                step(pool.tensor_tensor(Zt, g1v, g2v, ALU.add))
                pool.sem_inc(zt_done, 1)
                pool.tensor_copy(r8[:, :, 1:NCH], sp[:, 12, gs].unsqueeze(2).broadcast_to((128, QG, NCH - 1)))
                shape = (128, QG, 8, 8)
                fr, fi = [far[:, a, :, gs].rearrange("p n g -> p g n").unsqueeze(3).broadcast_to(shape) for a in range(2)]
                nr, ni = [near[:, a, :, gs].rearrange("p n g -> p g n").unsqueeze(2).broadcast_to(shape) for a in range(2)]
                t1, t2, t3, t4 = [g_[:, o:o + 512].rearrange("p (a b c) -> p a b c", a=QG, b=8)
                                  for g_, o in ((g1, 0), (g2, 0), (g1, 512), (g2, 512))]
                pool.tensor_tensor(t1, fr, nr, ALU.mult)
                pool.tensor_tensor(t2, fi, ni, ALU.mult)
                pool.tensor_tensor(t3, fr, ni, ALU.mult)
                step(pool.tensor_tensor(t4, fi, nr, ALU.mult))
                pool.tensor_tensor(E1.rearrange("p g (a b) -> p g a b", a=8), t1, t2, ALU.subtract)
                step(pool.tensor_tensor(E2.rearrange("p g (a b) -> p g a b", a=8), t3, t4, ALU.add))
                if q in (2, 3):
                    root(slice(16, 16 + 8 * TT))
                aux_out(pool, ("v", q))
                w1 = g1[:, 0:512].rearrange("p (a b) -> p a b", a=QG)
                w2 = g2[:, 0:512].rearrange("p (a b) -> p a b", a=QG)
                pool.tensor_tensor(w1, Vb, E1, ALU.mult)
                pool.wait_ge(v_swapped, 32 * (q + 1))
                step(pool.tensor_tensor(w2, Vs, E2, ALU.mult))
                pool.tensor_tensor(Vb, w1, w2, ALU.add).then_inc(rot_done, 1)
                pool.wait_ge(scan_done, q + 1)
                pool.tensor_tensor(Vb, w1, E1, ALU.mult)
                pool.wait_ge(w_swapped, 32 * (q + 1))
                step(pool.tensor_tensor(w2, Vs, E2, ALU.mult))
                pool.tensor_tensor(Vb, Vb, w2, ALU.subtract).then_inc(s_done, 1)
            aux_ready(pool, ("y", 3))
            pool.wait_ge(rb_saved, 16)
            pool.dma_start(biasR, bass.AP(rb_dram.tensor, 0, [[1, 128], [640, 8], [1, 512]])).then_inc(bias_in, 16)
            pool.dma_start(gt[:, 0, 0:128], k_flip).then_inc(bias_in, 16)
            pool.dma_start(badr, b_ada[0:1, 2048:3072].partition_broadcast(128)).then_inc(badr_in, 16)
            for h in range(8):
                aux_out(pool, ("flip", h))
            for n, (i, h) in enumerate(UNITS1):
                cols = 128 * (i + 1)
                if i and h == 0:
                    pool.wait_ge(topk_done, i)
                if i:
                    if n >= 2:
                        pool.wait_ge(lg_done, n - 1)
                    pool.tensor_tensor(mb[:, n % 2, 0:cols], biasT[:, h, 128 * (3 - i):512], score[:, i, 0:cols],
                                       ALU.add).then_inc(mb_done, 1)
            pool.wait_ge(o_done, NU1)
            pool.dma_start(xrow, x[0].rearrange("(t p) d -> p t d", p=128)).then_inc(x_again, 16)

            pool.wait_ge(x1_done, 2 * TT)
            pool.dma_start(pwS, pool_w_2[0].rearrange("g c d -> c g d")).then_inc(pw_in, 16)
            root(slice(0, TT))
            for j in range(4):
                proj_out(pool, ("up", j))
            for j, w in enumerate((2, 4, 8, 16)):
                src, m, flip = upT[:, j, :], 1, 0
                while m < w:
                    dst = (plT[:, j, :], tmp2[:, 0:512])[flip] if w in (2, 8) else (tmp2[:, 0:512], plT[:, j, :])[flip]
                    pool.tensor_tensor(dst[:, m:S], src[:, m:S], src[:, 0:S - m], ALU.add)
                    step(pool.tensor_copy(dst[:, 0:m], src[:, 0:m]))
                    src, m, flip = dst, 2 * m, 1 - flip
                p_ = plT[:, j, :]
                pool.tensor_scalar(p_[:, 16:S], p_[:, 16:S], 1.0 / w, None, ALU.mult)
                step(pool.tensor_tensor(p_[:, 0:16], p_[:, 0:16], cnt[:, j, :], ALU.mult))
                pool.tensor_tensor(p_, p_, upT[:, j, :], ALU.subtract).then_inc(pooled_done, 1)

            def rope(x_, cos, sin, shape):
                n = int(np.prod(shape[1:]))
                names = "abc"[:len(shape) - 1]
                t4 = [tmp2[:, 256 * m:256 * m + n].rearrange(f"p ({' '.join(names)}) -> p {' '.join(names)}",
                                                             **dict(zip(names, shape[1:]))) for m in range(4)]
                lo = x_[:, :, 0:32] if len(shape) == 3 else x_[:, :, :, 0:32]
                hi = x_[:, :, 32:64] if len(shape) == 3 else x_[:, :, :, 32:64]
                pool.tensor_tensor(t4[0], lo, cos, ALU.mult)
                pool.tensor_tensor(t4[1], hi, sin, ALU.mult)
                pool.tensor_tensor(t4[2], hi, cos, ALU.mult)
                step(pool.tensor_tensor(t4[3], lo, sin, ALU.mult))
                pool.tensor_tensor(lo, t4[0], t4[1], ALU.subtract)
                return pool.tensor_tensor(hi, t4[2], t4[3], ALU.add)

            root(slice(16, 40))
            for b, c0 in enumerate((0, 256, 384)):
                pool.wait_ge(kgain_done, b + 1)
                shape = (128, TT, 2, 32)
                rope(kvr[:, :, c0:c0 + 128].rearrange("p t (h d) -> p t h d", h=2),
                     ropeT[:, :, 0, :].unsqueeze(2).broadcast_to(shape), ropeT[:, :, 1, :].unsqueeze(2).broadcast_to(shape),
                     shape).then_inc(krope_done, 1)
                pool.wait_ge(krope_done, b + 1)
            for t in range(TT):
                pool.tensor_copy(kdup[:, t, :].rearrange("p (a b d) -> p a b d", a=4, b=2),
                                 kvr[:, t, 256:512].rearrange("p (a d) -> p a d", a=4).unsqueeze(2)
                                 .broadcast_to((128, 4, 2, 64))).then_inc(kdup_done, 1)
            for a, buf in enumerate((row2, q2b)):
                root(slice(16, 48))
                for t in range(TT):
                    pool.wait_ge(qgain_done, 4 * a + t + 1)
                    shape = (128, 8, 32)
                    rope(buf[:, t, :].rearrange("p (h d) -> p h d", h=8),
                         ropeT[:, t, 0:1, :].broadcast_to(shape), ropeT[:, t, 1:2, :].broadcast_to(shape),
                         shape).then_inc(qrope_done, 1)
                    pool.wait_ge(qrope_done, 4 * a + t + 1)
            pool.wait_ge(x2_done, 2 * TT)
            step(pool.memset(cvr, 0.0))
            for a in range(2):
                for tap in range(4):
                    src = conv_w_2[0, tap] if tap < 3 else conv_b_2[0]
                    src = src[DFF * a:DFF * a + DFF]
                    r0 = FT * tap
                    pool.dma_start(cvr[r0:r0 + FT - 1, a, :], src[0:128 * (FT - 1)].rearrange("(j p) -> j p", p=128))\
                        .then_inc(conv_in, 16)
                    pool.dma_start(cvr[r0 + FT - 1:r0 + FT, a, 0:64], src[128 * (FT - 1):DFF].rearrange("(j p) -> j p", p=64))\
                        .then_inc(conv_in, 16)
            root(slice(0, TT))

        @block.vector
        def _(v):
            step = Steps(v, vec_step)
            aux_ready(v, "cols")
            step(v.tensor_copy(colv[:, 0:62], abank("cols")[:, 0:62]))
            v.sem_inc(afree("cols"), 1)
            v.wait_ge(act_tanhc, 1)
            step(v.scalar_tensor_tensor(silc[:, 0:8], silc[:, 8:16], 1.0, colv[:, CV_C:CV_C + 8], ALU.add, ALU.mult))
            v.tensor_scalar(silc[:, 0:8], silc[:, 0:8], 0.5, None, ALU.mult).then_inc(silc_done, 1)
            v.tensor_scalar(colv[:, CV_BGLU:CV_BGLU + 4], colv[:, CV_BGLU:CV_BGLU + 4], 0.5, None, ALU.mult)\
                .then_inc(gbias_done, 1)

            roots = [0]

            def root(cols, scale):
                v.tensor_scalar(stat[:, cols], stat[:, cols], scale, EPS, ALU.mult, ALU.add).then_inc(ms_done, 1)
                roots[0] += 1
                v.wait_ge(root_done, roots[0])

            def row_norm(dst, scratch):
                for t in range(TT):
                    step(v.tensor_tensor_reduce(scratch, xrow[:, t, :], xrow[:, t, :], 1.0, 0.0, ALU.mult, ALU.add,
                                                stat[:, t:t + 1]))
                root(slice(0, TT), 1.0 / D)
                for t in range(TT):
                    v.tensor_scalar(dst[:, t, :], xrow[:, t, :], stat[:, t:t + 1], None, ALU.mult).then_inc(xn_done, 1)

            v.wait_ge(x_in, 16)
            row_norm(xrow, reluq.rearrange("p a b -> p (a b)"))

            LDT, DT, LR, LI, XR, TH, ER, COS, SIN = 0, 1, 2, 3, 4, 5, 6, 7, 8
            E8C, E8S, R8, SG = 10, 11, 12, 13

            def t_(n):
                return sp[:, n, :]

            def mul(o, a, b):
                step(v.tensor_tensor(o, a, b, ALU.mult))

            def exp_(o, a):
                k, r, p = t_(20), t_(21), t_(22)
                step(v.tensor_scalar(r, a, -88.0, 88.7, ALU.max, ALU.min))
                step(v.tensor_scalar(k, r, 1.4426950408889634, 12582912.0, ALU.mult, ALU.add))
                step(v.tensor_scalar(k, k, 12582912.0, None, ALU.subtract))
                step(v.scalar_tensor_tensor(r, k, -0.693359375, r, ALU.mult, ALU.add))
                step(v.scalar_tensor_tensor(r, k, 2.12194440e-4, r, ALU.mult, ALU.add))
                step(v.tensor_scalar(p, r, 1.0 / 5040, None, ALU.mult))
                for f in (720, 120, 24, 6, 2, 1):
                    step(v.scalar_tensor_tensor(p, p, 1.0 / f, r, ALU.add, ALU.mult))
                step(v.tensor_scalar(t_(23).bitcast(i32), k, 127.0, 8388608.0, ALU.add, ALU.mult))
                step(v.scalar_tensor_tensor(o, p, 1.0, t_(23), ALU.add, ALU.mult))

            aux_out(v, "lam")
            v.wait_ge(ldt_in, 16)
            exp_(t_(DT), t_(LDT))
            mul(t_(XR), t_(LR), t_(DT))
            mul(t_(TH), t_(LI), t_(DT))
            exp_(t_(ER), t_(XR))
            k, r, r2, p = t_(20), t_(21), t_(22), t_(23)
            step(v.tensor_scalar(k, t_(TH), 1.0 / (2 * math.pi), 12582912.0, ALU.mult, ALU.add))
            step(v.tensor_scalar(k, k, 12582912.0, None, ALU.subtract))
            step(v.scalar_tensor_tensor(r, k, -6.28125, t_(TH), ALU.mult, ALU.add))
            step(v.scalar_tensor_tensor(r, k, -1.934051513671875e-3, r, ALU.mult, ALU.add))
            step(v.scalar_tensor_tensor(r, k, -1.2556659146e-6, r, ALU.mult, ALU.add))
            mul(r2, r, r)
            step(v.tensor_scalar(p, r2, 1.0 / math.factorial(21), None, ALU.mult))
            for f in range(19, 1, -2):
                step(v.scalar_tensor_tensor(p, p, (-1) ** (f // 2) / math.factorial(f), r2, ALU.add, ALU.mult))
            step(v.scalar_tensor_tensor(t_(SIN), p, 1.0, r, ALU.add, ALU.mult))
            step(v.tensor_scalar(p, r2, 1.0 / math.factorial(20), None, ALU.mult))
            for f in range(18, 0, -2):
                step(v.scalar_tensor_tensor(p, p, (-1) ** (f // 2) / math.factorial(f), r2, ALU.add, ALU.mult))
            step(v.tensor_scalar(t_(COS), p, 1.0, None, ALU.add))
            aux_ready(v, "mod")
            step(v.tensor_tensor(modc[:, 0:16], abank("mod")[:, 0:16], colv[:, CV_ADA:CV_ADA + 16], ALU.add))
            v.sem_inc(afree("mod"), 1)
            v.scalar_tensor_tensor(modc[:, 8:16], modc[:, 8:16], 1.0, colv[:, CV_G:CV_G + 8], ALU.add, ALU.mult)\
                .then_inc(mod_done, 1)

            def cmul(o_re, o_im, a_re_, a_im_, b_re_, b_im_, ta, tb, tc, td):
                v.tensor_tensor(ta, a_re_, b_re_, ALU.mult)
                v.tensor_tensor(tb, a_im_, b_im_, ALU.mult)
                v.tensor_tensor(tc, a_re_, b_im_, ALU.mult)
                step(v.tensor_tensor(td, a_im_, b_re_, ALU.mult))
                v.tensor_tensor(o_re, ta, tb, ALU.subtract)
                step(v.tensor_tensor(o_im, tc, td, ALU.add))

            v.memset(pw[:, 0, 0, :], 1.0)
            v.memset(pw[:, 1, 0, :], 0.0)
            mul(pw[:, 0, 1, :], t_(ER), t_(COS))
            mul(pw[:, 1, 1, :], t_(ER), t_(SIN))
            for n in (1, 2, 4):
                for m in range(1, n + 1):
                    cmul(pw[:, 0, n + m, :], pw[:, 1, n + m, :], pw[:, 0, n, :], pw[:, 1, n, :],
                         pw[:, 0, m, :], pw[:, 1, m, :], t_(20), t_(21), t_(22), t_(23))
            v.tensor_copy(t_(E8C), t_(COS))
            step(v.tensor_copy(t_(E8S), t_(SIN)))
            step(v.tensor_copy(t_(R8), t_(ER)))
            for n in range(3):
                cmul(t_(E8C), t_(E8S), t_(E8C), t_(E8S), t_(E8C), t_(E8S), t_(20), t_(21), t_(22), t_(23))
                mul(t_(R8), t_(R8), t_(R8))
            v.memset(far[:, 0, 0, :], 1.0)
            v.memset(far[:, 1, 0, :], 0.0)
            v.tensor_copy(near[:, 0, 0, :], t_(E8C))
            step(v.tensor_copy(near[:, 1, 0, :], t_(E8S)))
            zt_flat = Zt.rearrange("p a b c -> p (a b c)")
            for n in (1, 2, 4):
                for m in range(n):
                    cmul(near[:, 0, n + m, :], near[:, 1, n + m, :], near[:, 0, n - 1, :], near[:, 1, n - 1, :],
                         near[:, 0, m, :], near[:, 1, m, :], t_(20), t_(21), t_(22), t_(23))
            for n in range(1, 8):
                cmul(far[:, 0, n, :], far[:, 1, n, :], far[:, 0, n - 1, :], far[:, 1, n - 1, :],
                     near[:, 0, 7, :], near[:, 1, 7, :], t_(20), t_(21), t_(22), t_(23))
            for tab in (near, far):
                step(v.tensor_scalar(tab[64:128, 1, :, :], tab[64:128, 1, :, :], -1.0, None, ALU.mult))
            NR, DEN, FR, FI = 14, 15, 16, 17
            step(v.tensor_scalar(t_(NR), pw[:, 0, 1, :], -1.0, None, ALU.add))
            mul(t_(20), t_(LR), t_(LR))
            mul(t_(21), t_(LI), t_(LI))
            step(v.tensor_tensor(t_(DEN), t_(20), t_(21), ALU.add))
            step(v.reciprocal(t_(DEN), t_(DEN)))
            v.tensor_tensor(t_(20), t_(NR), t_(LR), ALU.mult)
            v.tensor_tensor(t_(21), pw[:, 1, 1, :], t_(LI), ALU.mult)
            v.tensor_tensor(t_(22), pw[:, 1, 1, :], t_(LR), ALU.mult)
            step(v.tensor_tensor(t_(23), t_(NR), t_(LI), ALU.mult))
            v.tensor_tensor(t_(20), t_(20), t_(21), ALU.add)
            step(v.tensor_tensor(t_(22), t_(22), t_(23), ALU.subtract))
            v.tensor_tensor(t_(FR), t_(20), t_(DEN), ALU.mult)
            step(v.tensor_tensor(t_(FI), t_(22), t_(DEN), ALU.mult))
            A1, A2, A3, A4 = 24, 25, 26, 27
            top, bot = slice(0, 64), slice(64, 128)
            for o, half, src, sgn in ((A1, top, FR, 1), (A1, bot, FI, 1), (A2, top, FI, -1), (A2, bot, FR, 1),
                                      (A3, top, FI, -1), (A3, bot, FR, 1), (A4, top, FR, -1), (A4, bot, FI, -1)):
                step(v.tensor_scalar(sp[half, o, :], sp[half, src, :], float(sgn), None, ALU.mult))
            v.wait_ge(b_in, 32)
            v.wait_ge(b_in2, 32)

            def gb(n):
                return t_(n).unsqueeze(2).broadcast_to((128, G, GC))

            v.tensor_tensor(Y1, bre, gb(A1), ALU.mult)
            v.tensor_tensor(Y2, bre, gb(A3), ALU.mult)
            za, zb = [zt_flat[:, o:o + 512].rearrange("p (a b) -> p a b", a=G) for o in (0, 512)]
            v.tensor_tensor(za, bim, gb(A2), ALU.mult)
            step(v.tensor_tensor(zb, bim, gb(A4), ALU.mult))
            v.tensor_tensor(Y1, Y1, za, ALU.add)
            step(v.tensor_tensor(Y2, Y2, zb, ALU.add))

            def flat(a, rows=slice(0, 128)):
                return a[rows, :, :].rearrange("p a b -> p (a b)")
            aux_out(v, "c1")
            aux_out(v, "c2")
            v.sem_inc(prep_x, 1)
            v.sem_inc(prep_y, 1)
            def scan(q):
                v.wait_ge(rot_done, q + 1)
                v.tensor_tensor_scan(g1[:, 0:512], flat(r8), flat(Vb), 0.0, ALU.mult, ALU.add).then_inc(scan_done, 1)

            scan(0)
            v.wait_ge(consts_in2, 80)
            proj_out(v, "wi")

            def scores(i, m):
                n = 128 * (i + 1)
                for h in range(8):
                    aux_out(v, ("rel", i, h))
                    if h == 0:
                        ins = v.tensor_scalar(score[:, i, 0:n], reluq[:, m % 2, 0:n], wi[:, i, h:h + 1], None, ALU.mult)
                    else:
                        v.wait_ge(rel_used, m)
                        ins = v.scalar_tensor_tensor(score[:, i, 0:n], reluq[:, m % 2, 0:n], wi[:, i, h:h + 1],
                                                     score[:, i, 0:n], ALU.mult, ALU.add)
                    ins.then_inc(rel_used, 1)
                    m += 1
                v.wait_ge(rel_used, m)
                d = score[:, i, 128 * i:128 * i + 128]
                step(v.tensor_tensor(d, d, tri, ALU.add))

            def topk(i, rounds, end=False):
                s = score[:, i, 0:128 * (i + 1)]
                for _ in range(rounds):
                    step(v.max(sml[:, 8:16], s))
                    step(v.match_replace(s, sml[:, 8:16], s, TAKEN))
                if end:
                    v.tensor_scalar(s, s, TAKEN, NEG, ALU.not_equal, ALU.mult).then_inc(topk_done, 1)

            def head_norm(name, gain, done, buf, heads=8, sq=sqt):
                for t in range(TT):
                    proj_out(v, (name, t))
                    r_ = buf[:, t, 0:64 * heads]
                    step(v.tensor_tensor(sq[:, 0:64 * heads], r_, r_, ALU.mult))
                    step(v.tensor_reduce(stat[:, 16 + heads * t:16 + heads * (t + 1)],
                                         sq[:, 0:64 * heads].rearrange("p (a b) -> p a b", a=heads), X, ALU.add))
                root(slice(16, 16 + heads * TT), 1.0 / 64)
                for t in range(TT):
                    rv = buf[:, t, 0:64 * heads].rearrange("p (a b) -> p a b", a=heads)
                    ss = stat[:, 16 + heads * t:16 + heads * (t + 1)]
                    step(v.tensor_tensor(rv, rv, ss.unsqueeze(2).broadcast_to((128, heads, 64)), ALU.mult))
                    v.tensor_tensor(rv, rv, gain.unsqueeze(1).broadcast_to((128, heads, 64)), ALU.mult)\
                        .then_inc(done, 1)

            scores(1, 0)
            scores(2, 8)
            scan(1)
            scores(3, 16)
            topk(1, TOPK // 8, True)
            v.wait_ge(gains_in, 16 * len(GAINS))
            step(v.tensor_scalar(gq1, gq1, 0.125, None, ALU.mult))
            head_norm("k", gk1, knorm_done, row)
            scan(2)
            topk(2, 5)
            head_norm("q", gq1, qnorm_done, row)
            scan(3)
            topk(2, TOPK // 8 - 5, True)

            def az_in(t):
                v.wait_ge(az_tanh, t + 1)
                v.scalar_tensor_tensor(az[:, t, :], az[:, t, :], 1.0, pbank(("az", t))[:, :], ALU.add, ALU.mult)\
                    .then_inc(pfree(("az", t)), 1)

            def fill1(name):
                if name in ("gate0", "gate1"):
                    j = int(name[4])
                    v.wait_ge(badr_in, 16)
                    proj_ready(v, name)
                    v.tensor_tensor(gate_b[:, 512 * j:512 * j + 512], pbank(name)[:, :],
                                    badr[:, 512 * j:512 * j + 512], ALU.add).then_inc(pfree(name), 1)
                elif name[0] == "az":
                    az_in(name[1])
                elif name[0] == "z":
                    j = name[1]
                    v.wait_ge(sz_tanh, j + 1)
                    v.scalar_tensor_tensor(sz[:, j, :].rearrange("p (s c) -> p s c", s=L),
                                           sz[:, j, :].rearrange("p (s c) -> p s c", s=L), 1.0,
                                           pbank(("z", j))[:, :].rearrange("p (c s) -> p s c", s=L),
                                           ALU.add, ALU.mult).then_inc(pfree(("z", j)), 1)
                else:
                    j = name[1]
                    proj_out(v, ("glu", j))
                    step(v.scalar_tensor_tensor(gt[:, j % 2, :], gt[:, j % 2, :], 1.0, zz[:, j, :], ALU.add, ALU.mult))
                    v.scalar_tensor_tensor(yT[:, j, :].rearrange("p (c s) -> p s c", s=L),
                                           gt[:, j % 2, :].rearrange("p (s c) -> p s c", s=L), 0.125,
                                           sz[:, j, :].rearrange("p (s c) -> p s c", s=L), ALU.mult, ALU.mult)\
                        .then_inc(ys_done, 1)

            v.wait_ge(aux_done, AUX[("y", 3)] + 1)
            v.wait_ge(y_back, 16 * NQ)
            v.tensor_copy(silb, silc[:, 0:8].unsqueeze(2).broadcast_to((128, KT, 128))).then_inc(silb_done, 1)
            def gelu_in(j):
                y = yT[:, j, :]
                if j >= 2:
                    v.wait_ge(z_done, j - 1)
                step(v.scalar_tensor_tensor(y, u[:, j, :], colv[:, CV_SKIP + j:CV_SKIP + j + 1], y, ALU.mult, ALU.add))
                step(v.tensor_tensor(gt[:, j % 2, :], y, y, ALU.mult))
                step(v.tensor_scalar(gt[:, j % 2, :], gt[:, j % 2, :], 0.044715, 1.0, ALU.mult, ALU.add))
                v.tensor_tensor(gt[:, j % 2, :], gt[:, j % 2, :], y, ALU.mult).then_inc(y_skip, 1)

            def gelu_out(j):
                v.wait_ge(y_tanh, j + 1)
                v.scalar_tensor_tensor(zz[:, j, :], gt[:, j % 2, :], 1.0, yT[:, j, :], ALU.add, ALU.mult)\
                    .then_inc(z_done, 1)

            for h in range(8):
                aux_ready(v, ("flip", h))
                v.tensor_copy(biasT[:, h, :], abank(("flip", h))[:, :]).then_inc(afree(("flip", h)), 1)
            for h in range(8):
                aux_out(v, ("flip", h))
            az_in(0)
            for n in range(NU1 + 2):
                if n < NU1:
                    i, h = UNITS1[n]
                    cols = 128 * (i + 1)
                    proj_ready(v, ("qk", n))
                    if i:
                        v.wait_ge(mb_done, n - 7)
                        bias = mb[:, n % 2, 0:cols]
                    else:
                        bias = biasT[:, h, 384:512]
                    if n >= 2:
                        v.wait_ge(exp_done, n - 1)
                    v.tensor_tensor_reduce(lg[:, n % 2, 0:cols], pbank(("qk", n))[:, 0:cols], bias, -1.0, 3.0e38,
                                           ALU.add, ALU.min, sml[:, n % 2:n % 2 + 1]).then_inc(lg_done, 1)
                    v.wait_ge(lg_done, n + 1)
                    v.memset(stat[:, 187:188], 0.0).then_inc(pfree(("qk", n)), 1)
                if n < TOPK // 8:
                    topk(3, 1, n == TOPK // 8 - 1)
                if n in (2, 5, 8, 11):
                    gelu_in(n // 3)
                if n >= 2:
                    i, h = UNITS1[n - 2]
                    c0 = 4 + n % 2
                    v.wait_ge(exp_done, n - 1)
                    step(v.reciprocal(sml[:, c0:c0 + 1], sml[:, 2 + n % 2:3 + n % 2]))
                    step(v.tensor_scalar(sml[:, c0:c0 + 1], sml[:, c0:c0 + 1], 0.5, None, ALU.mult))
                    aux_ready(v, ("pv", n - 2))
                    v.scalar_tensor_tensor(orow[:, i, 64 * h:64 * h + 64], abank(("pv", n - 2))[:, 0:64],
                                           sml[:, c0:c0 + 1], az[:, i, 64 * h:64 * h + 64], ALU.mult, ALU.mult)\
                        .then_inc(o_done, 1)
                    v.wait_ge(o_done, n - 1)
                    v.sem_inc(afree(("pv", n - 2)), 1)
                if n in (4, 7, 10, 13):
                    gelu_out((n - 4) // 3)
                if n - 1 in FILL1:
                    fill1(FILL1[n - 1])
            v.wait_ge(x_again, 16)
            for t in range(TT):
                for j in range(2):
                    proj_ready(v, (f"out{j}", t))
                    part = (row, v1)[j][:, t, :]
                    v.tensor_tensor(part, pbank((f"out{j}", t))[:, :], gate_b[:, 512 * j:512 * j + 512], ALU.mult)\
                        .then_inc(pfree((f"out{j}", t)), 1)
                    proj_out(v, (f"out{j}", t))
                    v.tensor_tensor(xrow[:, t, 512 * j:512 * j + 512], xrow[:, t, 512 * j:512 * j + 512],
                                    part, ALU.add).then_inc(x1_done, 1)

            v.wait_ge(x1_done, 2 * TT)
            row_norm(xn2, tmp2)
            for t in range(TT):
                proj_out(v, ("kv1", t))
                proj_out(v, ("kv2", t))
            sq2 = pT2[:, 0, 0, :]
            for b, c0 in enumerate((0, 256, 384)):
                kv = kvr[:, :, c0:c0 + 128]
                step(v.tensor_tensor(sq2.rearrange("p (t c) -> p t c", t=TT), kv, kv, ALU.mult))
                step(v.tensor_reduce(stat[:, 16 + 8 * b:24 + 8 * b], sq2.rearrange("p (t d) -> p t d", d=64), X, ALU.add))
            root(slice(16, 40), 1.0 / 64)
            for b, c0 in enumerate((0, 256, 384)):
                kv = kvr[:, :, c0:c0 + 128].rearrange("p t (h d) -> p t h d", h=2)
                rs = stat[:, 16 + 8 * b:24 + 8 * b].rearrange("p (t h) -> p t h", h=2).unsqueeze(3).broadcast_to((128, TT, 2, 64))
                step(v.tensor_tensor(kv, kv, rs, ALU.mult))
                gb_ = gains[:, 192 + 64 * b:256 + 64 * b].unsqueeze(1).unsqueeze(1).broadcast_to((128, TT, 2, 64))
                v.tensor_tensor(kv, kv, gb_, ALU.mult).then_inc(kgain_done, 1)
            v.tensor_scalar(ngs, ngs, 1.0, 0.5, ALU.add, ALU.mult).then_inc(ngs_done, 1)
            gq2 = gains[:, 128:192]
            step(v.tensor_scalar(gq2, gq2, 0.125, None, ALU.mult))
            head_norm("q2a", gq2, qgain_done, row2, sq=sq2)
            step(v.memset(hid, 0.0))
            for a in range(2):
                for g in range(2):
                    aux_ready(v, ("hid", a, g))
                step(v.tensor_tensor(sml[:, 24 + a:25 + a], abank(("hid", a, 0))[:, 31:32], colv[:, CV_B1 + a:CV_B1 + a + 1],
                                     ALU.add))
                for g in range(2):
                    v.tensor_scalar(hid[:, a, 32 * g:32 * g + NCMP], abank(("hid", a, g))[:, 0:NCMP], sml[:, 24 + a:25 + a],
                                    None, ALU.add).then_inc(afree(("hid", a, g)), 1)
                    aux_out(v, ("hid", a, g))
            hx = hid[:, 0:2, :].rearrange("p a b -> p (a b)")[:, 0:127]
            ht = hid[:, 2:4, :].rearrange("p a b -> p (a b)")[:, 0:127]
            step(v.tensor_tensor(ht, hx, hx, ALU.mult))
            step(v.tensor_scalar(ht, ht, 0.044715, 1.0, ALU.mult, ALU.add))
            v.tensor_tensor(ht, ht, hx, ALU.mult).then_inc(hid_in, 1)
            v.wait_ge(hid_tanh, 1)
            step(v.scalar_tensor_tensor(hx, ht, 1.0, hx, ALU.add, ALU.mult))
            step(v.tensor_scalar(hx, hx, 0.5, None, ALU.mult))
            v.sem_inc(hid_done, 2)
            head_norm("q2b", gq2, qgain_done, q2b, sq=sq2)
            step(v.memset(vbd, 0.0))
            aux_ready(v, ("qt2", 3))
            step(v.memset(pc, 0.0))
            aux_ready(v, "vcm")
            for r in range(4):
                for g in range(2):
                    ins = v.tensor_copy(vbd[32 * r:32 * r + NCMP, g, 64 * r:64 * r + 64],
                                        abank("vcm")[32 * r:32 * r + NCMP, 64 * g:64 * g + 64])
            ins.then_inc(afree("vcm"), 1)

            def gated(name, gate, t, c0):
                proj_out(v, (gate, t))
                proj_ready(v, (name, t))
                d = mg[:, t, c0:c0 + 512]
                v.scalar_tensor_tensor(d, d, 1.0, pbank((name, t))[:, :], ALU.add, ALU.mult)\
                    .then_inc(pfree((name, t)), 1)

            v.wait_ge(ngs_done, 1)

            def compressed_scores(i):
                if i >= 2:
                    v.wait_ge(aux_done, AUX[("cp", i - 2)] + 1)
                for odd in range(2):
                    aux_ready(v, ("cq", i, odd))
                    dst = pc[:, i % 2, :].rearrange("p (a o b) -> p a o b", a=8, o=2)[:, :, odd, 0:NCMP]
                    ps = abank(("cq", i, odd))[:, 0:256].rearrange("p (a b) -> p a b", a=8)[:, :, 0:NCMP]
                    v.tensor_tensor(dst, ps, cmpmask[:, i:i + 1, 0:NCMP].broadcast_to((128, 8, NCMP)), ALU.add)\
                        .then_inc(afree(("cq", i, odd)), 1)
                    aux_out(v, ("cq", i, odd))
                p_ = pc[:, i % 2, :].rearrange("p (a b) -> p a b", a=16)[:, :, 0:NCMP]
                step(v.tensor_reduce(stat[:, 64:80], p_, X, ALU.max))
                v.tensor_tensor(p_, p_, stat[:, 64:80].unsqueeze(2).broadcast_to((128, 16, NCMP)), ALU.subtract)\
                    .then_inc(clg_done, 1)

            def compressed_out(i):
                v.wait_ge(cexp_done, i + 1)
                p_ = pc[:, i % 2, :].rearrange("p (a b) -> p a b", a=16)[:, :, 0:NCMP]
                step(v.tensor_reduce(stat[:, 80:96], p_, X, ALU.add))
                step(v.reciprocal(stat[:, 80:96], stat[:, 80:96]))
                step(v.tensor_tensor(stat[:, 80:96], stat[:, 80:96],
                                     ngs[:, i, :].rearrange("p (a b) -> p a b", a=16)[:, :, 0], ALU.mult))
                step(v.tensor_scalar(stat[:, 80:96], stat[:, 80:96], rowvalid[:, i:i + 1], None, ALU.mult))
                for a in range(2):
                    aux_ready(v, ("cv", i, a))
                    v.tensor_tensor(ob[:, i, 512 * a:512 * a + 512].rearrange("p (a b) -> p a b", a=8),
                                    abank(("cv", i, a))[:, :].rearrange("p (a b) -> p a b", a=8),
                                    stat[:, 80 + 8 * a:88 + 8 * a].unsqueeze(2).broadcast_to((128, 8, 64)), ALU.mult)\
                        .then_inc(afree(("cv", i, a)), 1)
                    aux_out(v, ("cv", i, a))

            for i in range(TT + 1):
                if i < TT:
                    compressed_scores(i)
                if i >= 1:
                    compressed_out(i - 1)
                if i in FILLC:
                    gated("yp0", "m00", i, 0)
            for n in range(NU2 + 2):
                if n < NU2:
                    i, h = UNITS2[n]
                    cols = 128 * (i + 1)
                    if n >= 2:
                        v.wait_ge(aux_done, AUX[("pw", n - 2)] + 1)
                    for b, key in enumerate(("qs", "qw")):
                        proj_ready(v, (key, n))
                        v.tensor_tensor_reduce(pr2[:, n % 2, b, 0:cols], pbank((key, n))[:, 0:cols], trim[:, 512 - cols:512],
                                               -1.0, 3.0e38, ALU.add, ALU.min,
                                               sml[:, 16 + 2 * (n % 2) + b:17 + 2 * (n % 2) + b]).then_inc(lg2_done, 1)
                        v.wait_ge(lg2_done, 2 * n + b + 1)
                        v.sem_inc(pfree((key, n)), 1)
                if n >= 2:
                    i, h = UNITS2[n - 2]
                    c0 = 28 + 2 * (n % 2)
                    v.wait_ge(exp2_done, 2 * (n - 2) + 2)
                    step(v.reciprocal(sml[:, c0:c0 + 2], sml[:, 20 + 2 * (n % 2):22 + 2 * (n % 2)]))
                    step(v.tensor_tensor(sml[:, c0:c0 + 2], sml[:, c0:c0 + 2], ngs[:, i, 3 * h + 1:3 * h + 3], ALU.mult))
                    aux_ready(v, ("pv2", n - 2))
                    o_ = ob[:, i, 64 * h:64 * h + 64]
                    step(v.scalar_tensor_tensor(o_, abank(("pv2", n - 2))[:, 0:64], sml[:, c0:c0 + 1], o_, ALU.mult, ALU.add))
                    v.scalar_tensor_tensor(o_, abank(("pv2", n - 2))[:, 64:128], sml[:, c0 + 1:c0 + 2], o_, ALU.mult, ALU.add)\
                        .then_inc(o2_done, 1)
                    v.wait_ge(o2_done, n - 1)
                    v.sem_inc(afree(("pv2", n - 2)), 1)
                if n in FILL2 and FILL2[n][0] == "yp1":
                    gated("yp1", "m01", FILL2[n][1], 512)
            for j in range(2):
                for t in range(TT):
                    buf = (row2, plT)[j]
                    proj_out(v, (f"m1{j}", t))
                    proj_ready(v, (f"ya{j}", t))
                    v.scalar_tensor_tensor(buf[:, t, :], buf[:, t, :], 1.0, pbank((f"ya{j}", t))[:, :], ALU.add, ALU.mult)\
                        .then_inc(pfree((f"ya{j}", t)), 1)
                    proj_out(v, (f"ya{j}", t))
                    d = mg[:, t, 512 * j:512 * j + 512]
                    v.tensor_tensor(d, d, buf[:, t, :], ALU.add).then_inc(mg_done, 1)

            def half_added(name, done):
                for j in range(2):
                    for t in range(TT):
                        proj_ready(v, (f"{name}{j}", t))
                        d = xrow[:, t, 512 * j:512 * j + 512]
                        v.scalar_tensor_tensor(d, pbank((f"{name}{j}", t))[:, :], 0.5, d, ALU.mult, ALU.add)\
                            .then_inc(done, 1)
                        v.wait_ge(done, 4 * j + t + 1)
                        v.sem_inc(pfree((f"{name}{j}", t)), 1)

            half_added("wo", x2_done)
            row_norm(xn3, aT[:, 8:10, :].rearrange("p a b -> p (a b)"))
            for a in range(2):
                aux_ready(v, ("cvt", a))
                v.tensor_copy(cvw[:, a, :, :], abank(("cvt", a))[:, 0:88].rearrange("p (a b) -> p a b", a=4))\
                    .then_inc(cvw_done, 1)
                v.wait_ge(cvw_done, a + 1)
                v.sem_inc(afree(("cvt", a)), 1)
            for j in range(FT):
                m = 128 if j < FT - 1 else 64
                for a, key in enumerate(("fg", "fv")):
                    v.wait_ge(tap_done, 2 * j + a + 1)
                    f_, ps = fc[0:m, j % 2, a, :], pbank((key, j))
                    step(v.scalar_tensor_tensor(f_[:, 1:S], ps[0:m, 0:S - 1], cvw[0:m, a, 1, j:j + 1], f_[:, 1:S],
                                                ALU.mult, ALU.add))
                    step(v.scalar_tensor_tensor(f_[:, 2:S], ps[0:m, 0:S - 2], cvw[0:m, a, 0, j:j + 1], f_[:, 2:S],
                                                ALU.mult, ALU.add))
                    v.sem_inc(pfree((key, j)), 1)
                    if a == 0:
                        v.sem_inc(gatec_done, 1)
                v.wait_ge(ftanh_done, j + 1)
                step(v.scalar_tensor_tensor(ft[0:m, j % 2, :], ft[0:m, j % 2, :], 1.0, fc[0:m, j % 2, 0, :],
                                            ALU.add, ALU.mult))
                v.tensor_tensor(aT[0:m, j, :], ft[0:m, j % 2, :], fc[0:m, j % 2, 1, :], ALU.mult).then_inc(act_done, 1)
            half_added("dn", x3_done)


_INS = ["x", "c", "rel_bias", "norm_g", "w_ada", "b_ada", "w_in", "q_gain", "k_gain", "a_re", "a_im", "log_dt",
        "b_re", "b_im", "c_re", "c_im", "d_skip", "w_glu", "b_glu", "w_out", "attn_norm_w_2", "w_in_2",
        "pool_w_2", "pool_scale_2", "q_norm_w_2", "k_norm_w_2", "cmp_pos_2", "cmp_w1_2", "cmp_b1_2", "cmp_w2_2",
        "w_pool_br_2", "w_attn_br_2", "w_o_2", "ffn_norm_w_2", "w_up_2", "conv_w_2", "conv_b_2", "w_down_2"]


def shape_constants():
    f = np.float32
    ident = np.eye(128, dtype=f)
    bucket = np.zeros((33, 640), f)
    dist = np.arange(S, dtype=np.int32)
    large = 16 + (np.log(np.maximum(dist, 1).astype(f) / f(16)) / f(math.log(8)) * f(16)).astype(np.int32)
    b = np.where(dist < 16, dist, np.minimum(large, 31))
    bucket[b, S - 1 - dist] = 1.0
    bucket[32, S:] = NEG
    p = np.arange(128)
    tri = np.zeros((128, 512), f)
    tri[:, 384:] = np.where(p[None, :] <= p[:, None], 0.0, NEG)
    half = 32
    freqs = f(10000.0) ** (-np.arange(half, dtype=f) / f(half))
    ang = np.arange(S, dtype=f)[:, None] * freqs[None, :]
    rope = np.stack([np.cos(ang), np.sin(ang)], 1).astype(f)
    rope = np.ascontiguousarray(rope.reshape(TT, 128, 2, 32).transpose(1, 0, 2, 3))
    t = np.arange(S)
    ends = np.arange(32) * 16 + 31
    cm = np.where(ends[None, :] <= t[:, None], 0.0, NEG).astype(f)
    cm = np.ascontiguousarray(cm.reshape(TT, 128, 32).transpose(1, 0, 2))
    rv = np.ascontiguousarray((t >= 31).astype(f).reshape(TT, 128).T)
    cnt = np.ones((4, 16), f)
    for i, w in enumerate((2, 4, 8, 16)):
        cnt[i] = f(1) / np.minimum(np.arange(16) + 1, w).astype(f)
    cnt = np.ascontiguousarray(np.broadcast_to(cnt[None], (128, 4, 16)))
    return dict(k_ident=ident, k_bucket=bucket, k_tri=tri, k_rope=rope, k_cmpmask=cm, k_rowvalid=rv, k_cnt=cnt,
                k_flip=np.ascontiguousarray(ident[::-1]))


def kernel(**inputs):
    import concourse.bacc as _bacc
    from concourse.bass_utils import run_bass_kernel_spmd as _run

    nc = _bacc.Bacc("TRN2", target_bir_lowering=False, num_devices=1)
    arrays, args = {}, []
    named = [(name, np.ascontiguousarray(inputs[name])) for name in _INS] + list(shape_constants().items())
    for name, a in named:
        arrays[f"in_{name}"] = a
        args.append(nc.dram_tensor(f"in_{name}", a.shape, mybir.dt.from_np(a.dtype), kind="ExternalInput").ap())
    args.append(nc.dram_tensor("out_0", (1, S, D), mybir.dt.float32, kind="ExternalOutput").ap())
    program(nc, *args)
    r = _run(nc, [arrays], core_ids=[0])
    return r.results[0]["out_0"]
```

```python
import math
from contextlib import ExitStack

import numpy as np

import concourse.bass as bass
from concourse import mybir

S = 512
D = 1024
KT = D // 128
TT = S // 128
NEG = -1.0e30
TAKEN = -3.0e38
EPS = 1e-6
TOPK = min(256, S // 4)
G, GC = 32, 16
L = 8
NCH = S // L
QG = 8
NQ = G // QG
OFF_KV, OFF_MG = 1536, 2352
NCMP = (S - 32) // 16 + 1
DFF = 2752
FT = -(-DFF // 128)
SQ2PI = math.sqrt(2.0 / math.pi)


def program(nc, x, c, rel_bias, norm_g, w_ada, b_ada, w_in, q_gain, k_gain, a_re, a_im, log_dt,
            b_re, b_im, c_re, c_im, d_skip, w_glu, b_glu, w_out, attn_norm_w_2, w_in_2, pool_w_2,
            pool_scale_2, q_norm_w_2, k_norm_w_2, cmp_pos_2, cmp_w1_2, cmp_b1_2, cmp_w2_2,
            w_pool_br_2, w_attn_br_2, w_o_2, ffn_norm_w_2, w_up_2, conv_w_2, conv_b_2, w_down_2,
            k_ident, k_bucket, k_tri, k_rope, k_cmpmask, k_rowvalid, k_cnt, k_flip, out):
    f32 = mybir.dt.float32
    i32 = mybir.dt.int32
    ALU = mybir.AluOpType
    ACT = mybir.ActivationFunctionType
    X = mybir.AxisListType.X
    ctx = ExitStack()
    with ctx:
        def sem(name):
            return ctx.enter_context(nc.semaphore(name))

        ARENA = 53200
        arena = ctx.enter_context(nc.sbuf_tensor("arena", [128, ARENA], f32))
        bank = [ctx.enter_context(nc.psum_tensor(f"bank{i}", [128, 512], f32)) for i in range(8)]

        class Zone:
            def __init__(self, at, end=ARENA):
                self.at, self.end = at, end

            def take(self, words, *shape):
                a = arena[:, self.at:self.at + words]
                self.at += words
                assert self.at <= self.end, (self.at, self.end)
                if len(shape) > 1:
                    names = "abcd"[:len(shape)]
                    a = a.rearrange(f"p ({' '.join(names)}) -> p {' '.join(names)}",
                                    **{n: s for n, s in zip(names, shape)})
                return a

        z = Zone(0)
        slot = [z.take(4096) for _ in range(2)]
        XROW0 = z.at
        xrow = z.take(4096, TT, D)
        hT = z.take(4096, KT, S)
        ident = z.take(128)
        trim = z.take(512)
        tri = trim[:, 384:512]
        ropeT = z.take(TT * 64, TT, 2, 32)
        cmpmask = z.take(TT * 32, TT, 32)
        rowvalid = z.take(TT)
        cnt = z.take(64, 4, 16)
        colv = z.take(64)
        colr = z.take(128)
        modc = z.take(40)
        silc = z.take(16)
        stat = z.take(192)
        sml = z.take(64)
        halves = z.take(32)
        gains = z.take(384)
        BASE = z.at

        modr = arena[0:1, BASE + 4096:BASE + 4096 + 2048]
        z = Zone(BASE)
        u = z.take(2048, TT, S)
        sz = z.take(2048, TT, S)
        yT = z.take(2048, TT, S)
        qiT = z.take(2048, TT, S)
        kiT = z.take(512)
        wi = z.take(32, TT, 8)
        score = z.take(2048, TT, S)
        reluq = z.take(1024, 2, S)
        row = z.take(2048, TT, 512)
        kT = z.take(2048, TT, S)
        qT = z.take(2048, TT, S)
        v1 = z.take(2048, TT, 512)
        wiT = row[64:72, 0, :]
        sqt = reluq[:, 0, :]
        U = arena[:, XROW0:XROW0 + 2048].rearrange("p (a b) -> p a b", a=G)
        az = arena[:, XROW0 + 2048:XROW0 + 4096].rearrange("p (a b) -> p a b", a=TT)
        zq = Zone(z.at - 2048 - 2048)
        onehot, rb_row, rb_in = zq.take(640), zq.take(640), zq.take(8)
        SSM0 = z.at
        X1, X2 = z.take(512, G, GC), z.take(512, G, GC)
        Y1, Y2 = z.take(512, G, GC), z.take(512, G, GC)
        pw = z.take(2 * 9 * 32, 2, 9, 32)
        sp = z.take(32 * 32, 32, 32)
        CL = z.take(QG * 9 * GC, QG, 9, GC)
        Zt = z.take(1024, QG, L, GC)
        Tm = z.take(1024, QG, 128)
        Wn = z.take(1024, QG, 128)
        KX0 = z.at
        Kx = z.take(QG * 240, QG, 240)
        E1, E2 = z.take(512, QG, NCH), z.take(512, QG, NCH)
        Vb, Vs = z.take(512, QG, NCH), z.take(512, QG, NCH)
        r8 = z.take(512, QG, NCH)
        G0 = z.at
        g1, g2 = z.take(1152), z.take(1152)
        far = arena[:, BASE + 2048 + 1024:BASE + 2048 + 1536].rearrange("p (a n g) -> p a n g", a=2, n=8)
        near = arena[:, BASE + 2048 + 1536:BASE + 4096].rearrange("p (a n g) -> p a n g", a=2, n=8)
        zq = Zone(KX0)
        craw, lraw = zq.take(1024, 2, 4, 128), zq.take(256, 2, 128)
        zq = Zone(G0)
        bre, bim = zq.take(512, G, GC), zq.take(512, G, GC)

        z = Zone(SSM0)
        biasT = z.take(4096, 8, 512)
        biasR = arena[:, z.at:z.at + 4096].rearrange("p (a b) -> p a b", a=8)
        mb = z.take(1024, 2, 512)
        lg = z.take(1024, 2, 512)
        pr = z.take(1024, 2, 512)
        pT = z.take(1024, 2, 512)
        zz = z.take(2048, TT, S)
        gt = z.take(1024, 2, 512)
        gate_b = z.take(1024)
        badr = z.take(1024)
        silb = z.take(1024, KT, 128)
        orow, oT = row, qiT

        z = Zone(BASE)
        upT = z.take(2048, 4, S)
        plT = z.take(2048, 4, S)
        ypT = z.take(2048, 4, S)
        pwS = z.take(512, 4, 128)
        row2 = z.take(2048, TT, 512)
        tmp2 = z.take(1024)
        qT2 = z.take(4096, 8, S)
        ksT = z.take(2048, 4, S)
        vs2 = z.take(1024, 2, TT, 128)
        ngs = z.take(TT * 48, TT, 48)
        posr = z.take(128)
        w2s = z.take(192)
        hid = z.take(256, 4, 64)
        kcmp = z.take(64, 2, 32)
        vbd = z.take(512, 2, 256)
        pc = row2[:, 0:2, :]
        pTc = row2[:, 2, :]
        pr2 = z.take(2048, 2, 2, 512)
        pT2 = z.take(2048, 2, 2, 512)
        OB0 = z.at
        ob = z.take(4096, TT, D)
        mg = z.take(4096, TT, D)
        cvw = z.take(2 * 88, 2, 4, FT)
        cvr = z.take(2 * 128, 2, 128)
        oT2 = qT2
        xn2 = ob
        kcT = arena[:, OB0 - 4096:OB0 - 4096 + 3072].rearrange("p (a g n) -> p a g n", a=2, g=3)
        kvr = arena[:, OB0:OB0 + 2048].rearrange("p (a b) -> p a b", a=TT)
        kdup = arena[:, OB0 + 2048:OB0 + 4096].rearrange("p (a b) -> p a b", a=TT)
        q2b = arena[:, OB0 + 4096:OB0 + 6144].rearrange("p (a b) -> p a b", a=TT)
        kcd = arena[:, OB0 + 6144:OB0 + 8192].rearrange("p (a b) -> p a b", a=TT)
        mT = hT

        z = Zone(BASE)
        aT = z.take(FT * 512, FT, S)
        fc = z.take(4 * 512, 2, 2, 512)
        ft = z.take(2 * 512, 2, 512)
        xn3 = arena[:, BASE:BASE + 4096].rearrange("p (a b) -> p a b", a=TT)


        PROJ, AUX = {}, {}

        def name_proj(*names):
            for n in names:
                PROJ[n] = len(PROJ)

        def name_aux(*names):
            for n in names:
                AUX[n] = len(AUX)

        def four(name):
            return [(name, t) for t in range(TT)]

        def ssm_names(q):
            return [("k", q, 0), ("k", q, 1), ("z", q, 0), ("z", q, 1)]

        def rel_names(i):
            return [("rel", i, h) for h in range(8)]

        name_aux("cols", "lam", "c1", "c2", "rb", "rb2", ("mod", 0), ("mod", 1),
                 *[("x", k) for k in range(KT)], ("mod", 2), ("mod", 3), "modt")
        name_proj(*four("u"), *four("qi"), "ki", *four("k"), *four("q"), *four("v"))
        name_aux(*ssm_names(0), ("v", 0), "wi", ("y", 0), *rel_names(1), *ssm_names(1), *rel_names(2), ("v", 1),
                 *rel_names(3), ("y", 1), *ssm_names(2), ("v", 2), *four("kt"), ("y", 2), *ssm_names(3), ("v", 3),
                 *four("qt"), ("y", 3), *[("flip", h) for h in range(8)])
        name_proj(("az", 0))
        FILL1 = {0: ("az", 1), 2: ("az", 2), 4: ("az", 3), 6: ("z", 0), 8: ("z", 1), 10: ("z", 2), 12: ("z", 3),
                 14: "gate0", 16: "gate1", 20: ("glu", 0), 23: ("glu", 1), 26: ("glu", 2), 29: ("glu", 3)}
        UNITS1 = [(i, h) for i in range(TT) for h in range(8)]
        NU1 = len(UNITS1)
        for n in range(NU1 + 2):
            if n < NU1:
                name_proj(("qk", n))
            if 0 <= n - 1 < NU1:
                name_aux(("pt", n - 1))
            if 0 <= n - 2 < NU1:
                name_aux(("pv", n - 2))
            if n in FILL1:
                name_proj(FILL1[n])
        name_aux(*four("ot"))
        name_proj(*[(f"out{j}", t) for t in range(TT) for j in range(2)])
        name_aux(*[("h2", k) for k in range(KT)], "pos", ("cvt", 0), ("cvt", 1))
        name_proj(*four("up"), *four("kv1"), *four("kv2"), *four("q2a"), *four("q2b"))
        name_aux(*[("ks", n) for n in range(4)], *[("kc", n) for n in range(4)])
        name_aux(("hid", 0), ("hid", 1))
        name_aux(*[("qt2", m) for m in range(8)], "kcm", "vcm")
        name_proj(*four("m00"))
        name_proj(*four("ypm"))
        FILL2 = {2 + 5 * n: name for n, name in enumerate(four("yp1") + four("m10") + four("m11"))}
        for i in range(TT + 1):
            if i < TT:
                name_aux(("cq", i, 0), ("cq", i, 1))
                name_proj(("m01", i))
            if i >= 1:
                name_aux(("cp", i - 1), ("cv", i - 1, 0), ("cv", i - 1, 1))
            if i < TT:
                name_proj(("yp0", i))
        UNITS2 = [(i, h) for i in range(TT) for h in range(16)]
        NU2 = len(UNITS2)
        for n in range(NU2 + 2):
            if n < NU2:
                name_proj(("qs", n), ("qw", n))
            if 0 <= n - 1 < NU2:
                name_aux(("ps", n - 1), ("pw", n - 1))
            if 0 <= n - 2 < NU2:
                name_aux(("pv2", n - 2))
            if n in FILL2:
                name_proj(FILL2[n])
        name_aux(*[("o2", m) for m in range(8)])
        name_proj(*four("ya0"), *four("ya1"))
        name_aux(*[("mt", m) for m in range(8)])
        name_proj(*[(f"wo{j}", t) for t in range(TT) for j in range(2)])
        name_aux(*[("h3", k) for k in range(KT)])
        for j in range(FT):
            name_proj(("fg", j), ("fv", j))
        for a in range(2):
            name_proj(*four(f"dn{a}"))

        proj_done, aux_done = sem("proj_done"), sem("aux_done")
        proj_free = [sem(f"proj_free{b}") for b in range(4)]
        aux_free = [sem(f"aux_free{b}") for b in range(4)]

        def pbank(name):
            return bank[PROJ[name] % 4]

        def abank(name):
            return bank[4 + AUX[name] % 4]

        def proj_ready(eng, name):
            eng.wait_ge(proj_done, PROJ[name] + 1)

        def aux_ready(eng, name):
            eng.wait_ge(aux_done, AUX[name] + 1)

        def proj_out(eng, name):
            eng.wait_ge(proj_free[PROJ[name] % 4], PROJ[name] // 4 + 1)

        def aux_out(eng, name):
            eng.wait_ge(aux_free[AUX[name] % 4], AUX[name] // 4 + 1)

        def pfree(name):
            return proj_free[PROJ[name] % 4]

        def afree(name):
            return aux_free[AUX[name] % 4]

        def cols_of(w, k0, k1, c0, c1):
            return w[0, k0 * 128:k1 * 128, c0:c1].rearrange("(k p) n -> p k n", p=128)

        def slot_view(s, kt, n):
            return slot[s][:, 0:kt * n].rearrange("p (k n) -> p k n", k=kt)

        CHUNKS = []

        def chunk(name, last, kt, n, parts):
            CHUNKS.append((name, last, kt, n, parts))

        for j in range(4):
            chunk(("ada", j), ("aux", ("mod", j)), KT, 512, [(0, 512, lambda j=j: cols_of(w_ada, 0, KT, 512 * j, 512 * j + 512))])

        def w1chunk(name, last, c0):
            chunk(name, ("proj", last), KT, 512, [(0, 512, lambda: cols_of(w_in, 0, KT, c0, c0 + 512))])

        w1chunk("u", ("u", 3), 0)
        w1chunk("qi", ("qi", 3), 3072)
        chunk("ki", ("proj", "ki"), KT, 72, [(0, 72, lambda: cols_of(w_in, 0, KT, 3584, 3656))])
        for name, c0 in (("k", 1536), ("q", 1024), ("v", 2048), ("az", 2560), ("z", 512)):
            w1chunk(name, (name, 3), c0)
        for j in range(2):
            chunk(("gate", j), ("proj", f"gate{j}"), KT, 512,
                  [(0, 512, lambda j=j: cols_of(w_ada, 0, KT, 2048 + 512 * j, 2560 + 512 * j))])
        chunk("glu", ("proj", ("glu", 3)), 4, 512, [(0, 512, lambda: cols_of(w_glu, 0, 4, 0, 512))])
        for j in range(2):
            chunk(("out", j), ("proj", (f"out{j}", 3)), KT, 512,
                  [(0, 512, lambda j=j: cols_of(w_out, 0, KT, 512 * j, 512 * j + 512))])
        def wchunk(name, last, w, kt, c0, n=512):
            chunk(name, ("proj", last), kt, n, [(0, n, lambda: cols_of(w, 0, kt, c0, c0 + n))])

        wchunk("up", ("up", 3), w_in_2, KT, 0)
        wchunk("kv1", ("kv1", 3), w_in_2, KT, OFF_KV)
        wchunk("kv2", ("kv2", 3), w_in_2, KT, OFF_KV + 512, 304)
        wchunk("q2a", ("q2a", 3), w_in_2, KT, 512)
        wchunk("q2b", ("q2b", 3), w_in_2, KT, 1024)
        chunk("c1", ("aux", ("hid", 1)), 32, 128,
              [(0, 128, lambda: cmp_w1_2[0].rearrange("a (k p) n -> p (a k) n", p=128))])
        wchunk("m00", ("m00", 3), w_in_2, KT, OFF_MG)
        wchunk("m01", ("m01", 3), w_in_2, KT, OFF_MG + 512)
        wchunk("yp0", ("yp0", 3), w_pool_br_2, 4, 0)
        wchunk("yp1", ("yp1", 3), w_pool_br_2, 4, 512)
        wchunk("m10", ("m10", 3), w_in_2, KT, OFF_MG + 1024)
        wchunk("m11", ("m11", 3), w_in_2, KT, OFF_MG + 1536)
        wchunk("ya0", ("ya0", 3), w_attn_br_2, KT, 0)
        wchunk("ya1", ("ya1", 3), w_attn_br_2, KT, 512)
        wchunk("wo0", ("wo0", 3), w_o_2, KT, 0)
        wchunk("wo1", ("wo1", 3), w_o_2, KT, 512)
        for J in range(FT // 2):
            n = 256 if J < FT // 2 - 1 else 192
            chunk(("f", J), ("proj", ("fv", 2 * J + 1)), KT, 512,
                  [(0, n, lambda J=J, n=n: cols_of(w_up_2, 0, KT, 256 * J, 256 * J + n)),
                   (256, 256 + n, lambda J=J, n=n: cols_of(w_up_2, 0, KT, DFF + 256 * J, DFF + 256 * J + n))])
        for a in range(2):
            for b in range(3):
                last = ("used", 1 + 2 * a + b) if b < 2 else ("proj", (f"dn{a}", 3))
                if b < 2:
                    parts = [(0, 512, lambda a=a, b=b: cols_of(w_down_2, 8 * b, 8 * b + 8, 512 * a, 512 * a + 512))]
                else:
                    parts = [("down", a, None)]
                chunk(("d", a, b), last, 8 if b < 2 else 6, 512, parts)
        slot_full = [sem("slot0_full"), sem("slot1_full")]
        CH, count = {}, [0, 0]
        for n, (name, last, kt, cols, parts) in enumerate(CHUNKS):
            count[n % 2] += 16 * (2 if parts[0][0] == "down" else len(parts))
            CH[name] = (n % 2, count[n % 2], kt, cols)

        def weights(eng, name):
            s, full, kt, n = CH[name]
            eng.wait_ge(slot_full[s], full)
            return slot_view(s, kt, n)

        u_dram = nc.dram_tensor("u_dram", (G, GC, L, NCH), f32).ap()
        y_dram = nc.dram_tensor("y_dram", (G, GC, L, NCH), f32).ap()
        rb_dram = nc.dram_tensor("rb_dram", (8, 640), f32).ap()

        x_in = sem("x_in")
        consts_in = sem("consts_in")
        rows_in = sem("rows_in")
        lam_in = sem("lam_in")
        craw_in = sem("craw_in")
        b_in = sem("b_in")
        b_in2 = sem("b_in2")
        ldt_in = sem("ldt_in")
        gains_in = sem("gains_in")
        rb_in_s = sem("rb_in_s")
        rb_one = sem("rb_one")
        onehot_in = sem("onehot_in")
        consts_in2 = sem("consts_in2")
        vec_step = sem("vec_step")
        act_step = sem("act_step")
        pool_step = sem("pool_step")
        act_tanhc = sem("act_tanhc")
        silc_done = sem("silc_done")
        mod_done = sem("mod_done")
        ms_done = sem("ms_done")
        root_done = sem("root_done")
        xn_done = sem("xn_done")
        h_ready = sem("h_ready")
        prep_done = sem("prep_done")
        pool_ones = sem("pool_ones")
        u_saved = sem("u_saved")
        U_in = sem("U_in")
        cl_done = sem("cl_done")
        zt_done = sem("zt_done")
        t_in = sem("t_in")
        v_swapped = sem("v_swapped")
        rot_done = sem("rot_done")
        scan_done = sem("scan_done")
        w_swapped = sem("w_swapped")
        s_done = sem("s_done")
        y_saved = sem("y_saved")
        y_back = sem("y_back")
        rb_saved = sem("rb_saved")
        bias_in = sem("bias_in")
        badr_in = sem("badr_in")
        ki_twice = sem("ki_twice")
        rel_used = sem("rel_used")
        topk_done = sem("topk_done")
        knorm_done = sem("knorm_done")
        qnorm_done = sem("qnorm_done")
        mb_done = sem("mb_done")
        lg_done = sem("lg_done")
        exp_done = sem("exp_done")
        o_done = sem("o_done")
        silb_done = sem("silb_done")
        gbias_done = sem("gbias_done")
        az_tanh = sem("az_tanh")
        sz_tanh = sem("sz_tanh")
        y_skip = sem("y_skip")
        y_tanh = sem("y_tanh")
        z_done = sem("z_done")
        ys_done = sem("ys_done")
        x_again = sem("x_again")
        x1_done = sem("x1_done")
        chunk_used = sem("chunk_used")
        small_in = sem("small_in")
        pw_in = sem("pw_in")
        conv_in = sem("conv_in")
        cvw_done = sem("cvw_done")
        kc_zero = sem("kc_zero")
        pooled_done = sem("pooled_done")
        kgain_done = sem("kgain_done")
        krope_done = sem("krope_done")
        kdup_done = sem("kdup_done")
        kcd_done = sem("kcd_done")
        qgain_done = sem("qgain_done")
        qrope_done = sem("qrope_done")
        ngs_done = sem("ngs_done")
        hid_in = sem("hid_in")
        hid_tanh = sem("hid_tanh")
        hid_done = sem("hid_done")
        clg_done = sem("clg_done")
        cexp_done = sem("cexp_done")
        lg2_done = sem("lg2_done")
        exp2_done = sem("exp2_done")
        o2_done = sem("o2_done")
        mg_done = sem("mg_done")
        x2_done = sem("x2_done")
        tap_done = sem("tap_done")
        gatec_done = sem("gatec_done")
        ftanh_done = sem("ftanh_done")
        act_done = sem("act_done")
        x3_done = sem("x3_done")
        out_done = sem("out_done")

        class Steps:
            def __init__(self, eng, s):
                self.eng, self.s, self.n = eng, s, 0

            def __call__(self, ins):
                self.n += 1
                ins.then_inc(self.s, 1)
                self.eng.wait_ge(self.s, self.n)

        def by_rows(a):
            return a.rearrange("a (n p) -> (a n) p", p=128)

        ROWS = [(0, 8, by_rows(c)), (8, 8, by_rows(norm_g)), (16, 16, by_rows(b_ada[:, 0:2048])),
                (32, 8, by_rows(attn_norm_w_2)), (40, 8, by_rows(ffn_norm_w_2)), (48, 4, by_rows(d_skip)),
                (52, 4, by_rows(b_glu)), (56, 4, by_rows(pool_scale_2)), (60, 2, cmp_b1_2[0])]
        NROWS = len(ROWS)
        GAINS = [q_gain[0:1, :], k_gain[0:1, :], q_norm_w_2[0:1, :], k_norm_w_2[0, 0:1, :],
                 k_norm_w_2[0, 1:2, :], k_norm_w_2[0, 2:3, :]]

        block = ctx.enter_context(nc.Block())

        CV_C, CV_G, CV_ADA, CV_G2, CV_GF, CV_SKIP, CV_BGLU, CV_PS, CV_B1 = 0, 8, 16, 32, 40, 48, 52, 56, 60
        gq1, gk1 = gains[:, 0:64], gains[:, 64:128]

        @block.sync
        def _(sp_):
            sp_.dma_start(xrow, x[0].rearrange("(t p) d -> p t d", p=128)).then_inc(x_in, 16)
            sp_.dma_start(ident, k_ident).then_inc(consts_in, 16)
            for at, n, src in ROWS:
                sp_.dma_start(colr[at:at + n, :], src).then_inc(rows_in, 16)

            def ssm_spread(q):
                for a in range(2):
                    aux_out(sp_, ("k", q, a))
                if q:
                    aux_ready(sp_, ("y", q - 1))
                for s in range(L):
                    sp_.dma_start(Tm[GC * s:GC * s + GC, :, :],
                                  Kx[0:GC, :, (L - 1 - s) * GC:(L - 1 - s) * GC + 128]).then_inc(t_in, 16)

            def ssm_swap(q):
                aux_out(sp_, ("v", q))
                for r, o in ((0, 64), (64, 0)):
                    sp_.dma_start(Vs[r:r + 64, :, :], Vb[o:o + 64, :, :]).then_inc(v_swapped, 16)
                sp_.wait_ge(scan_done, q + 1)
                w1 = g1[:, 0:512].rearrange("p (a b) -> p a b", a=QG)
                for r, o in ((0, 64), (64, 0)):
                    sp_.dma_start(Vs[r:r + 64, :, :], w1[o:o + 64, :, :]).then_inc(w_swapped, 16)

            def ssm_back(q):
                gs = slice(QG * q, QG * q + QG)
                aux_out(sp_, ("y", q))
                for s in range(L):
                    sp_.dma_start(y_dram[gs, :, s, :].rearrange("g o c -> o g c"),
                                  Vs[GC * s:GC * s + GC, :, :]).then_inc(y_saved, 16)
                sp_.wait_ge(y_saved, 16 * L * (q + 1))
                sp_.dma_start(yT[:, q, :], y_dram[gs, :, :, :].rearrange("g o s c -> (g o) (s c)"))\
                    .then_inc(y_back, 16)

            for n, (name, last, kt, cols, parts) in enumerate(CHUNKS):
                if name == "k":
                    for j in range(4):
                        proj_out(sp_, ("u", j))
                    sp_.dma_start(u_dram.rearrange("(m g) o s c -> (g o) m (s c)", g=8), u).then_inc(u_saved, 16)
                    sp_.wait_ge(u_saved, 16)
                    for s in range(L):
                        sp_.dma_start(U[GC * s:GC * s + GC, :, :], u_dram[:, :, s, :].rearrange("g o c -> o g c"))\
                            .then_inc(U_in, 16)
                    ssm_spread(0)
                    ssm_swap(0)
                if name == "q":
                    ssm_back(0)
                if name == "v":
                    ssm_spread(1)
                    ssm_swap(1)
                    ssm_back(1)
                    ssm_spread(2)
                if name == "az":
                    ssm_swap(2)
                    ssm_back(2)
                    ssm_spread(3)
                if name == "z":
                    ssm_swap(3)
                    ssm_back(3)
                if n >= 2:
                    kind, res = CHUNKS[n - 2][1]
                    if kind == "used":
                        sp_.wait_ge(chunk_used, res)
                    elif kind == "aux":
                        sp_.wait_ge(aux_done, AUX[res] + 1)
                    else:
                        sp_.wait_ge(proj_done, PROJ[res] + 1)
                w = slot_view(n % 2, kt, cols)
                for c0, c1, src in parts:
                    if c0 is None:
                        sp_.dma_start(w[c1, :, :], src()).then_inc(slot_full[n % 2], 16)
                    elif c0 == "down":
                        wd = w_down_2[0, 2048:DFF, 512 * c1:512 * c1 + 512]
                        sp_.dma_start(w[:, 0:5, :], wd[0:640, :].rearrange("(k p) n -> p k n", p=128))\
                           .then_inc(slot_full[n % 2], 16)
                        sp_.dma_start(w[0:64, 5, :], wd[640:704, :]).then_inc(slot_full[n % 2], 16)
                    else:
                        sp_.dma_start(w[:, :, c0:c1], src()).then_inc(slot_full[n % 2], 16)
            for n in range(8):
                a, t = n // 4, n % 4
                sp_.wait_ge(x3_done, n + 1)
                sp_.dma_start(out[0, 128 * t:128 * t + 128, 512 * a:512 * a + 512],
                              xrow[:, t, 512 * a:512 * a + 512]).then_inc(out_done, 16)
            sp_.wait_ge(out_done, 128)

        @block.tensor
        def _(pe):
            seen = [0, 0]

            def begin_aux(name):
                a = AUX[name]
                assert a == seen[0], (name, a, seen)
                seen[0] += 1
                if a >= 4:
                    pe.wait_ge(aux_free[a % 4], a // 4)
                return bank[4 + a % 4]

            def begin_proj(name):
                p = PROJ[name]
                assert p == seen[1], (name, p, seen)
                seen[1] += 1
                if p >= 4:
                    pe.wait_ge(proj_free[p % 4], p // 4)
                return bank[p % 4]

            def one_rows(name, t, chunk_name, act, n=512):
                w = weights(pe, chunk_name)
                kt = w.shape[1]
                ps = begin_proj((name, t))
                for k in range(kt):
                    mm = pe.matmul(ps[:, 0:n], act[:, k, 128 * t:128 * t + 128], w[:, k, 0:n],
                                   start=(k == 0), stop=(k == kt - 1))
                mm.then_inc(proj_done, 1)

            def one_cols(name, j, chunk_name, act):
                w = weights(pe, chunk_name)
                kt = w.shape[1]
                ps = begin_proj((name, j))
                for k in range(kt):
                    mm = pe.matmul(ps[:, :], w[:, k, 128 * j:128 * j + 128], act[:, k, :],
                                   start=(k == 0), stop=(k == kt - 1))
                mm.then_inc(proj_done, 1)

            def proj_rows(name, chunk_name, act, n=512):
                for t in range(TT):
                    one_rows(name, t, chunk_name, act, n)

            def proj_cols(name, chunk_name, act):
                for j in range(4):
                    one_cols(name, j, chunk_name, act)

            def turn(name, blocks, eye=None):
                ps = begin_aux(name)
                at = 0
                for b in blocks:
                    p, f = b.shape[0], int(np.prod(b.shape[1:]))
                    mm = pe.transpose(ps[0:f, at:at + p], b, ident[0:p, 0:p] if eye is None else eye)
                    at += p
                mm.then_inc(aux_done, 1)

            pe.wait_ge(consts_in, 16)
            pe.wait_ge(rows_in, 16 * NROWS)
            turn("cols", [colr[0:62, :]])
            pe.wait_ge(lam_in, 64)
            turn("lam", [lraw[0:32, 0, :], lraw[0:32, 1, :]])
            pe.wait_ge(craw_in, 64)
            for a in range(2):
                turn(f"c{a + 1}", [craw[:, a, m, :] for m in range(4)])
            pe.wait_ge(rb_in_s, 16)
            pe.wait_ge(rb_one, 1)
            pe.wait_ge(onehot_in, 16)
            for name, c0, n in (("rb", 0, 512), ("rb2", 512, 128)):
                pe.matmul(begin_aux(name)[0:8, 0:n], rb_in[0:33, :], onehot[0:33, c0:c0 + n],
                          start=True, stop=True).then_inc(aux_done, 1)
            def x_turns(key, src, ready):
                pe.wait_ge(*ready)
                for k in range(KT):
                    turn((key, k), [src[:, t, 128 * k:128 * k + 128] for t in range(TT)])

            pe.wait_ge(silc_done, 1)
            for j in range(4):
                if j == 2:
                    x_turns("x", xrow, (xn_done, TT))
                w = weights(pe, ("ada", j))
                ps = begin_aux(("mod", j))
                for k in range(KT):
                    mm = pe.matmul(ps[0:1, :], silc[:, k:k + 1], w[:, k, :], start=(k == 0), stop=(k == KT - 1))
                mm.then_inc(aux_done, 1)
            for j in range(4):
                aux_out(pe, ("mod", j))
            turn("modt", [modr[:, 128 * m:128 * m + 128] for m in range(16)])

            def ssm_taps(q):
                pe.wait_ge(cl_done, q + 1)
                if q == 0:
                    pe.wait_ge(prep_done, 1)
                for a in range(2):
                    ps = begin_aux(("k", q, a))
                    for b in range(4):
                        g = 4 * a + b
                        mm = pe.matmul(ps[0:GC, 128 * b:128 * b + 128], Y1[:, QG * q + g, :],
                                       CL[:, g, 0:L, :].rearrange("p a b -> p (a b)"), start=True, stop=True)
                    mm.then_inc(aux_done, 1)

            def ssm_inputs(q):
                pe.wait_ge(zt_done, q + 1)
                for a in range(2):
                    turn(("z", q, a), [Zt[:, 4 * a + b, :, :].rearrange("p a b -> p (a b)") for b in range(4)])

            def ssm_kernels(q):
                ssm_taps(q)
                ssm_inputs(q)

            def ssm_chunks(q):
                pe.wait_ge(U_in, 16 * L)
                aux_out(pe, ("z", q, 0))
                aux_out(pe, ("z", q, 1))
                ps = begin_aux(("v", q))
                for g in range(QG):
                    mm = pe.matmul(ps[:, NCH * g:NCH * g + NCH], Wn[:, g, :], U[:, QG * q + g, :],
                                   start=True, stop=True)
                mm.then_inc(aux_done, 1)

            def ssm_out(q):
                pe.wait_ge(t_in, 16 * L * (q + 1))
                pe.wait_ge(s_done, q + 1)
                ps = begin_aux(("y", q))
                for g in range(QG):
                    pe.matmul(ps[:, NCH * g:NCH * g + NCH], Tm[:, g, :], U[:, QG * q + g, :],
                              start=True, stop=False)
                    mm = pe.matmul(ps[:, NCH * g + 1:NCH * g + NCH],
                                   CL[:, g, 1:L + 1, :].rearrange("p a b -> p (a b)"), Vb[:, g, 0:NCH - 1],
                                   start=False, stop=True)
                mm.then_inc(aux_done, 1)

            pe.wait_ge(h_ready, KT)
            proj_cols("u", "u", hT)
            one_cols("qi", 0, "qi", hT)
            one_cols("qi", 1, "qi", hT)
            ssm_taps(0)
            one_cols("qi", 2, "qi", hT)
            ssm_inputs(0)
            one_cols("qi", 3, "qi", hT)
            ssm_chunks(0)
            w = weights(pe, "ki")
            ps = begin_proj("ki")
            for k in range(KT):
                mm = pe.matmul(ps[0:72, :], w[:, k, :], hT[:, k, :], start=(k == 0), stop=(k == KT - 1))
            mm.then_inc(proj_done, 1)
            proj_out(pe, "ki")
            turn("wi", [wiT[:, 128 * t:128 * t + 128] for t in range(TT)], ident[64:72, 64:72])
            ssm_out(0)
            proj_out(pe, ("qi", 3))
            proj_out(pe, ("qi", 2))
            proj_out(pe, ("qi", 1))
            proj_out(pe, ("qi", 0))
            pe.wait_ge(ki_twice, 16)
            for i in range(1, TT):
                for h in range(8):
                    r = 64 * (h % 2)
                    n = 128 * (i + 1)
                    pe.matmul(begin_aux(("rel", i, h))[:, 0:n], qiT[r:r + 64, h // 2, 128 * i:128 * i + 128],
                              kiT[r:r + 64, 0:n], start=True, stop=True).then_inc(aux_done, 1)
                if i == 1:
                    ssm_kernels(1)
                if i == 2:
                    ssm_chunks(1)
            ssm_out(1)
            one_rows("k", 0, "k", hT)
            one_rows("k", 1, "k", hT)
            ssm_kernels(2)
            one_rows("k", 2, "k", hT)
            one_rows("k", 3, "k", hT)
            ssm_chunks(2)
            one_rows("q", 0, "q", hT)
            one_rows("q", 1, "q", hT)
            pe.wait_ge(knorm_done, TT)
            for m in range(4):
                turn(("kt", m), [row[:, t, 128 * m:128 * m + 128] for t in range(TT)])
            ssm_out(2)
            one_rows("q", 2, "q", hT)
            ssm_kernels(3)
            one_rows("q", 3, "q", hT)
            one_rows("v", 0, "v", hT)
            ssm_chunks(3)
            one_rows("v", 1, "v", hT)
            pe.wait_ge(qnorm_done, TT)
            for m in range(4):
                turn(("qt", m), [row[:, t, 128 * m:128 * m + 128] for t in range(TT)])
            one_rows("v", 2, "v", hT)
            ssm_out(3)
            one_rows("v", 3, "v", hT)
            one_rows("az", 0, "az", hT)

            def fill1(name):
                if name in ("gate0", "gate1"):
                    pe.wait_ge(silb_done, 1)
                    w = weights(pe, ("gate", int(name[4])))
                    ps = begin_proj(name)
                    for k in range(KT):
                        mm = pe.matmul(ps[:, :], silb[:, k, :], w[:, k, :], start=(k == 0), stop=(k == KT - 1))
                    mm.then_inc(proj_done, 1)
                elif name[0] == "az":
                    one_rows("az", name[1], "az", hT)
                elif name[0] == "z":
                    one_cols("z", name[1], "z", hT)
                else:
                    pe.wait_ge(z_done, TT)
                    one_cols("glu", name[1], "glu", zz)

            pe.wait_ge(bias_in, 32)
            for h in range(8):
                pe.matmul(begin_aux(("flip", h))[:, :], gt[:, 0, 0:128], biasR[:, h, :],
                          start=True, stop=True).then_inc(aux_done, 1)
            for m in range(4):
                aux_out(pe, ("kt", m))
                aux_out(pe, ("qt", m))
                proj_out(pe, ("v", m))
            for n in range(NU1 + 2):
                if n < NU1:
                    i, h = UNITS1[n]
                    r = 64 * (h % 2)
                    pe.matmul(begin_proj(("qk", n))[:, 0:128 * (i + 1)],
                              qT[r:r + 64, h // 2, 128 * i:128 * i + 128],
                              kT[r:r + 64, h // 2, 0:128 * (i + 1)], start=True, stop=True).then_inc(proj_done, 1)
                if 0 <= n - 1 < NU1:
                    i, h = UNITS1[n - 1]
                    pe.wait_ge(exp_done, n)
                    turn(("pt", n - 1), [pr[:, (n - 1) % 2, 128 * b:128 * b + 128] for b in range(i + 1)])
                if 0 <= n - 2 < NU1:
                    i, h = UNITS1[n - 2]
                    aux_out(pe, ("pt", n - 2))
                    ps = begin_aux(("pv", n - 2))
                    for b in range(i + 1):
                        mm = pe.matmul(ps[:, 0:64], pT[:, (n - 2) % 2, 128 * b:128 * b + 128],
                                       v1[:, b, 64 * h:64 * h + 64], start=(b == 0), stop=(b == i))
                    mm.then_inc(aux_done, 1)
                if n in FILL1:
                    fill1(FILL1[n])
            pe.wait_ge(o_done, NU1)
            for m in range(4):
                turn(("ot", m), [orow[:, t, 128 * m:128 * m + 128] for t in range(TT)])
            pe.wait_ge(ys_done, TT)
            for m in range(4):
                aux_out(pe, ("ot", m))
            for t in range(TT):
                for j in range(2):
                    w = weights(pe, ("out", j))
                    ps = begin_proj((f"out{j}", t))
                    for k in range(KT):
                        a = yT[:, k, :] if k < 4 else oT[:, k - 4, :]
                        mm = pe.matmul(ps[:, :], a[:, 128 * t:128 * t + 128], w[:, k, :],
                                       start=(k == 0), stop=(k == KT - 1))
                    mm.then_inc(proj_done, 1)

            x_turns("h2", xn2, (xn_done, 2 * TT))
            pe.wait_ge(small_in, 16 * 4)
            turn("pos", [posr[0:32, :]])
            for k in range(KT):
                aux_out(pe, ("h2", k))
            proj_cols("up", "up", hT)
            pe.wait_ge(conv_in, 16 * 16)
            for a in range(2):
                turn(("cvt", a), [cvr[0:88, a, :]])
            proj_rows("kv1", "kv1", hT)
            proj_rows("kv2", "kv2", hT, 304)
            proj_rows("q2a", "q2a", hT)
            proj_rows("q2b", "q2b", hT)
            pe.wait_ge(kdup_done, TT)
            pe.wait_ge(kcd_done, TT)
            for n in range(4):
                turn(("ks", n), [kdup[:, t, 128 * n:128 * n + 128] for t in range(TT)])
            for n in range(4):
                turn(("kc", n), [kcd[:, t, 128 * n:128 * n + 128] for t in range(TT)])
            aux_out(pe, "pos")
            w = weights(pe, "c1")
            for n in range(4):
                aux_out(pe, ("kc", n))
            for a in range(2):
                ps = begin_aux(("hid", a))
                for k in range(16):
                    mm = pe.matmul(ps[:, 0:3 * NCMP], w[:, 16 * a + k, :],
                                   kcT[:, a, :, 2 * k:2 * k + 16 * (NCMP - 1) + 1:16],
                                   start=(k == 0), stop=(k == 15))
                mm.then_inc(aux_done, 1)
            pe.wait_ge(qrope_done, TT)
            for m in range(4):
                turn(("qt2", m), [row2[:, t, 128 * m:128 * m + 128] for t in range(TT)])
            pe.wait_ge(qrope_done, 2 * TT)
            for m in range(4):
                turn(("qt2", 4 + m), [q2b[:, t, 128 * m:128 * m + 128] for t in range(TT)])
            pe.wait_ge(hid_done, 2)
            ps = begin_aux("kcm")
            for g in range(2):
                mm = pe.matmul(ps[:, 32 * g:32 * g + NCMP], w2s[:, 0:128], hid[:, 0, 32 * g:32 * g + NCMP],
                               start=True, stop=True)
            mm.then_inc(aux_done, 1)
            ps = begin_aux("vcm")
            for r in range(4):
                for g in range(2):
                    mm = pe.matmul(ps[32 * r:32 * r + NCMP, 64 * g:64 * g + 64], hid[:, 1, 32 * g:32 * g + NCMP],
                                   w2s[:, 128:192], start=True, stop=True)
            mm.then_inc(aux_done, 1)
            proj_rows("m00", "m00", hT)
            pe.wait_ge(pooled_done, 4)
            pe.wait_ge(pw_in, 16)
            for j in range(4):
                pe.matmul(begin_proj(("ypm", j))[:, :], pwS[:, j, :], plT[:, j, :], start=True, stop=True)\
                    .then_inc(proj_done, 1)
            for j in range(4):
                proj_out(pe, ("ypm", j))

            def fill2(name):
                key, t = name
                one_rows(key, t, key, ypT if key[0] == "y" else hT)

            for m in range(8):
                aux_out(pe, ("qt2", m))
            for n in range(4):
                aux_out(pe, ("ks", n))
            aux_out(pe, "kcm")
            aux_out(pe, "vcm")
            for i in range(TT + 1):
                if i < TT:
                    for odd in range(2):
                        r = slice(64 * odd, 64 * odd + 64)
                        ps = begin_aux(("cq", i, odd))
                        for h in range(odd, 16, 2):
                            mm = pe.matmul(ps[:, 16 * (h - odd):16 * (h - odd) + NCMP],
                                           qT2[r, h // 2, 128 * i:128 * i + 128], kcmp[r, h // 8, 0:NCMP],
                                           start=True, stop=True)
                        mm.then_inc(aux_done, 1)
                    fill2(("m01", i))
                if i >= 1:
                    pe.wait_ge(cexp_done, i)
                    turn(("cp", i - 1), [pc[:, (i - 1) % 2, 128 * b:128 * b + 128] for b in range(4)])
                    aux_out(pe, ("cp", i - 1))
                    for a in range(2):
                        ps = begin_aux(("cv", i - 1, a))
                        for b in range(2):
                            mm = pe.matmul(ps[:, 256 * b:256 * b + 256], pTc[:, 128 * (2 * a + b):128 * (2 * a + b) + 128],
                                           vbd[:, a, :], start=True, stop=True)
                        mm.then_inc(aux_done, 1)
                if i < TT:
                    fill2(("yp0", i))
            for n in range(NU2 + 2):
                if n < NU2:
                    i, h = UNITS2[n]
                    r = slice(64 * (h % 2), 64 * (h % 2) + 64)
                    for b, key in enumerate(("qs", "qw")):
                        pe.matmul(begin_proj((key, n))[:, 0:128 * (i + 1)], qT2[r, h // 2, 128 * i:128 * i + 128],
                                  ksT[r, 2 * b + h // 8, 0:128 * (i + 1)], start=True, stop=True).then_inc(proj_done, 1)
                if 0 <= n - 1 < NU2:
                    i, h = UNITS2[n - 1]
                    for b, key in enumerate(("ps", "pw")):
                        pe.wait_ge(exp2_done, 2 * (n - 1) + b + 1)
                        turn((key, n - 1), [pr2[:, (n - 1) % 2, b, 128 * m:128 * m + 128] for m in range(i + 1)])
                if 0 <= n - 2 < NU2:
                    i, h = UNITS2[n - 2]
                    aux_out(pe, ("ps", n - 2))
                    aux_out(pe, ("pw", n - 2))
                    ps = begin_aux(("pv2", n - 2))
                    for b in range(2):
                        for m in range(i + 1):
                            mm = pe.matmul(ps[:, 64 * b:64 * b + 64], pT2[:, (n - 2) % 2, b, 128 * m:128 * m + 128],
                                           vs2[:, b, m, 64 * (h // 8):64 * (h // 8) + 64],
                                           start=(m == 0), stop=(m == i))
                    mm.then_inc(aux_done, 1)
                if n in FILL2:
                    fill2(FILL2[n])
            pe.wait_ge(o2_done, NU2)
            for m in range(8):
                turn(("o2", m), [ob[:, t, 128 * m:128 * m + 128] for t in range(TT)])
            for m in range(8):
                aux_out(pe, ("o2", m))
            proj_rows("ya0", "ya0", oT2)
            proj_rows("ya1", "ya1", oT2)
            pe.wait_ge(mg_done, 2 * TT)
            for m in range(8):
                turn(("mt", m), [mg[:, t, 128 * m:128 * m + 128] for t in range(TT)])
            for m in range(8):
                aux_out(pe, ("mt", m))
            for t in range(TT):
                for j in range(2):
                    one_rows(f"wo{j}", t, f"wo{j}", mT)

            x_turns("h3", xn3, (xn_done, 3 * TT))
            for k in range(KT):
                aux_out(pe, ("h3", k))
            for j in range(FT):
                w = weights(pe, ("f", j // 2))
                m = 128 if j < FT - 1 else 64
                for a, key in enumerate(("fg", "fv")):
                    c0 = 256 * a + 128 * (j % 2)
                    ps = begin_proj((key, j))
                    for k in range(KT):
                        mm = pe.matmul(ps[0:m, :], w[:, k, c0:c0 + m], hT[:, k, :], start=(k == 0), stop=(k == KT - 1))
                    mm.then_inc(proj_done, 1)
            pe.wait_ge(act_done, FT)
            for a in range(2):
                banks = [begin_proj((f"dn{a}", t)) for t in range(TT)]
                for b in range(3):
                    w = weights(pe, ("d", a, b))
                    for t in range(TT):
                        for k in range(8 * b, min(8 * b + 8, FT)):
                            m = 128 if k < FT - 1 else 64
                            mm = pe.matmul(banks[t][:, :], aT[0:m, k, 128 * t:128 * t + 128], w[0:m, k - 8 * b, :],
                                           start=(k == 0), stop=(k == FT - 1))
                        if b == 2:
                            mm.then_inc(proj_done, 1)
                    if b < 2:
                        mm.then_inc(chunk_used, 1)

        @block.scalar
        def _(act):
            step = Steps(act, act_step)
            for a, src in ((0, a_re), (1, a_im)):
                for half in range(2):
                    act.dma_start(lraw[0:32, a, 64 * half:64 * half + 64], src[0]).then_inc(lam_in, 16)
            for a in range(2):
                for half in range(2):
                    src = (c_re, c_im)[(a + half) % 2]
                    act.dma_start(craw[:, a, :, 64 * half:64 * half + 64],
                                  src[0].rearrange("(m g) o p -> (g o) m p", g=8)).then_inc(craw_in, 16)
            act.dma_start(bre[0:64, :, :], b_re[0].rearrange("g p i -> p g i")).then_inc(b_in, 16)
            act.dma_start(bim[0:64, :, :], b_im[0].rearrange("g p i -> p g i")).then_inc(b_in, 16)
            aux_ready(act, "lam")
            act.activation(sp[:, 2:4, :], abank("lam")[:, 0:64].rearrange("p (a b) -> p a b", a=2), ACT.Copy)\
               .then_inc(afree("lam"), 1)
            for name, dst, top_scale in (("c1", X1, 1.0), ("c2", X2, -1.0)):
                aux_ready(act, name)
                for r, f in ((slice(0, 64), top_scale), (slice(64, 128), -1.0)):
                    ins = act.activation(dst[r, :, :].rearrange("p a b -> p (a b)"), abank(name)[r, :], ACT.Copy, scale=f)
                ins.then_inc(afree(name), 1)
            act.wait_ge(b_in, 32)
            for b_ in (bre, bim):
                act.dma_start(b_[64:128, :, :], b_[0:64, :, :]).then_inc(b_in2, 16)
            for name, c0, n in (("rb", 0, 512), ("rb2", 512, 128)):
                aux_ready(act, name)
                act.activation(rb_row[0:8, c0:c0 + n], abank(name)[0:8, 0:n], ACT.Copy).then_inc(afree(name), 1)

            aux_ready(act, "cols")
            act.wait_ge(vec_step, 1)
            act.activation(silc[:, 8:16], colv[:, CV_C:CV_C + 8], ACT.Tanh, scale=0.5).then_inc(act_tanhc, 1)

            for j in range(4):
                if j == 2:
                    for k in range(KT):
                        aux_ready(act, ("x", k))
                        act.activation(hT[:, k, :], abank(("x", k))[:, :], ACT.Copy).then_inc(afree(("x", k)), 1)
                aux_ready(act, ("mod", j))
                act.activation(modr[:, 512 * j:512 * j + 512], abank(("mod", j))[0:1, :], ACT.Copy)\
                   .then_inc(afree(("mod", j)), 1)
            act.wait_ge(mod_done, 1)
            for k in range(0, KT, 2):
                aux_out(act, ("x", k))
                act.activation(hT[:, k, :], hT[:, k, :], ACT.Identity, scale=modc[:, 8 + k:9 + k],
                               bias=modc[:, k:k + 1]).then_inc(h_ready, 1)

            def ssm_taps(q):
                for a in range(2):
                    aux_ready(act, ("k", q, a))
                    if a == 0 and q == 0:
                        act.wait_ge(pool_ones, 1)
                    if a == 0 and q:
                        act.wait_ge(t_in, 16 * L * q)
                    act.activation(Kx[0:GC, 4 * a:4 * a + 4, 112:240],
                                   abank(("k", q, a))[0:GC, :].rearrange("p (a b) -> p a b", a=4),
                                   ACT.Copy).then_inc(afree(("k", q, a)), 1)

            def ssm_inputs(q):
                for a in range(2):
                    aux_ready(act, ("z", q, a))
                    act.activation(Wn[:, 4 * a:4 * a + 4, :],
                                   abank(("z", q, a))[:, :].rearrange("p (a b) -> p a b", a=4),
                                   ACT.Copy).then_inc(afree(("z", q, a)), 1)

            def ssm_kernels(q):
                ssm_taps(q)
                ssm_inputs(q)

            def ssm_chunks(q):
                aux_ready(act, ("v", q))
                if q:
                    act.wait_ge(aux_done, AUX[("y", q - 1)] + 1)
                act.activation(Vb, abank(("v", q))[:, :].rearrange("p (a b) -> p a b", a=QG),
                               ACT.Copy).then_inc(afree(("v", q)), 1)

            def ssm_out(q):
                aux_ready(act, ("y", q))
                act.activation(Vs, abank(("y", q))[:, :].rearrange("p (a b) -> p a b", a=QG),
                               ACT.Copy).then_inc(afree(("y", q)), 1)

            for j in range(4):
                proj_ready(act, ("u", j))
                act.activation(u[:, j, :].rearrange("p (s c) -> p s c", s=L),
                               pbank(("u", j))[:, :].rearrange("p (c s) -> p s c", s=L),
                               ACT.Copy).then_inc(pfree(("u", j)), 1)
            for j in range(4):
                if j == 2:
                    ssm_taps(0)
                if j == 3:
                    ssm_inputs(0)
                proj_ready(act, ("qi", j))
                act.activation(qiT[:, j, :], pbank(("qi", j))[:, :], ACT.Copy).then_inc(pfree(("qi", j)), 1)
            ssm_chunks(0)
            proj_ready(act, "ki")
            step(act.activation(kiT[0:64, :], pbank("ki")[0:64, :], ACT.Copy))
            act.dma_start(kiT[64:128, :], kiT[0:64, :]).then_inc(ki_twice, 16)
            act.activation(wiT, pbank("ki")[64:72, :], ACT.Copy).then_inc(pfree("ki"), 1)
            aux_ready(act, "wi")
            act.activation(wi, abank("wi")[:, 0:32].rearrange("p (a b) -> p a b", a=TT), ACT.Copy,
                           scale=8 ** -0.5).then_inc(afree("wi"), 1)
            ssm_out(0)
            m = 0
            for i in range(1, TT):
                for h in range(8):
                    aux_ready(act, ("rel", i, h))
                    if m >= 2:
                        act.wait_ge(rel_used, m - 1)
                    n = 128 * (i + 1)
                    act.activation(reluq[:, m % 2, 0:n], abank(("rel", i, h))[:, 0:n], ACT.Relu)\
                       .then_inc(afree(("rel", i, h)), 1)
                    m += 1
                if i == 1:
                    ssm_kernels(1)
                if i == 2:
                    ssm_chunks(1)
            ssm_out(1)

            def rows_in_(name, dst, ts=range(TT)):
                for t in ts:
                    proj_ready(act, (name, t))
                    act.activation(dst[:, t, :], pbank((name, t))[:, :], ACT.Copy)\
                       .then_inc(pfree((name, t)), 1)

            def columns_in(name, dst):
                for m in range(4):
                    aux_ready(act, (name, m))
                    act.activation(dst[:, m, :], abank((name, m))[:, :], ACT.Copy)\
                       .then_inc(afree((name, m)), 1)

            rows_in_("k", row, (0, 1))
            ssm_kernels(2)
            rows_in_("k", row, (2, 3))
            ssm_chunks(2)
            columns_in("kt", kT)
            aux_ready(act, ("kt", 3))
            rows_in_("q", row, (0, 1))
            ssm_out(2)
            rows_in_("q", row, (2,))
            ssm_kernels(3)
            rows_in_("q", row, (3,))
            rows_in_("v", v1, (0,))
            ssm_chunks(3)
            rows_in_("v", v1, (1,))
            act.wait_ge(rb_saved, 16)
            columns_in("qt", qT)
            rows_in_("v", v1, (2,))
            ssm_out(3)
            rows_in_("v", v1, (3,))

            def az_in(t):
                proj_ready(act, ("az", t))
                act.activation(az[:, t, :], pbank(("az", t))[:, :], ACT.Tanh, scale=0.5).then_inc(az_tanh, 1)

            def fill1(name):
                if name[0] == "az":
                    az_in(name[1])
                elif name[0] == "z":
                    j = name[1]
                    proj_ready(act, ("z", j))
                    act.activation(sz[:, j, :].rearrange("p (s c) -> p s c", s=L),
                                   pbank(("z", j))[:, :].rearrange("p (c s) -> p s c", s=L),
                                   ACT.Tanh, scale=0.5).then_inc(sz_tanh, 1)
                elif name[0] == "glu":
                    j = name[1]
                    proj_ready(act, ("glu", j))
                    act.wait_ge(gbias_done, 1)
                    if j >= 2:
                        act.wait_ge(ys_done, j - 1)
                    act.activation(gt[:, j % 2, :], pbank(("glu", j))[:, :], ACT.Tanh, scale=0.25,
                                   bias=colv[:, CV_BGLU + j:CV_BGLU + j + 1]).then_inc(pfree(("glu", j)), 1)

            az_in(0)
            for n in range(NU1 + 1):
                if n < NU1:
                    i, h = UNITS1[n]
                    act.wait_ge(lg_done, n + 1)
                    if n >= 2:
                        act.wait_ge(aux_done, AUX[("pt", n - 2)] + 1)
                    if n >= 4:
                        act.wait_ge(o_done, n - 3)
                    act.activation(pr[:, n % 2, 0:128 * (i + 1)], lg[:, n % 2, 0:128 * (i + 1)], ACT.Exp,
                                   scale=-1.0, bias=sml[:, n % 2:n % 2 + 1],
                                   accum_out=sml[:, 48 + n % 4:49 + n % 4]).then_inc(exp_done, 1)
                if n >= 1:
                    i, h = UNITS1[n - 1]
                    aux_ready(act, ("pt", n - 1))
                    if n >= 3:
                        act.wait_ge(aux_done, AUX[("pv", n - 3)] + 1)
                    act.activation(pT[:, (n - 1) % 2, 0:128 * (i + 1)], abank(("pt", n - 1))[:, 0:128 * (i + 1)],
                                   ACT.Copy).then_inc(afree(("pt", n - 1)), 1)
                if n in FILL1:
                    fill1(FILL1[n])
                if n in (3, 6, 9, 12):
                    j = n // 3 - 1
                    act.wait_ge(y_skip, j + 1)
                    act.activation(gt[:, j % 2, :], gt[:, j % 2, :], ACT.Tanh, scale=SQ2PI).then_inc(y_tanh, 1)
            columns_in("ot", oT)

            def scaled_columns_in(key, n, col):
                for k in range(n):
                    aux_ready(act, (key, k))
                    act.activation(hT[:, k, :], abank((key, k))[:, :], ACT.Copy,
                                   scale=colv[:, col + k:col + k + 1]).then_inc(afree((key, k)), 1)

            def many_columns_in(key, dst, ms, src=None):
                for m in ms:
                    aux_ready(act, (key, m))
                    act.activation(dst[:, m, :], abank((key, m))[:, :], ACT.Copy).then_inc(afree((key, m)), 1)

            act.wait_ge(x1_done, 2 * TT)
            act.dma_start(posr[0:32, :], cmp_pos_2[0].rearrange("a (k p) d -> (a k) (p d)", p=2)).then_inc(small_in, 16)
            for c0 in (0, 64):
                act.dma_start(w2s[:, c0:c0 + 64], cmp_w2_2[0, 0]).then_inc(small_in, 16)
            act.dma_start(w2s[:, 128:192], cmp_w2_2[0, 1]).then_inc(small_in, 16)
            scaled_columns_in("h2", KT, CV_G2)
            aux_ready(act, "pos")
            act.wait_ge(kc_zero, 1)
            act.activation(kcT[:, :, 2, 0:32:2], abank("pos")[:, 0:32].rearrange("p (a b) -> p a b", a=2), ACT.Copy)\
               .then_inc(afree("pos"), 1)
            for j in range(4):
                proj_ready(act, ("up", j))
                act.activation(upT[:, j, :], pbank(("up", j))[:, :], ACT.Copy).then_inc(pfree(("up", j)), 1)
            for t in range(TT):
                proj_ready(act, ("kv1", t))
                act.activation(kvr[:, t, 0:384], pbank(("kv1", t))[:, 0:384], ACT.Copy)
                act.activation(vs2[:, 0, t, :], pbank(("kv1", t))[:, 384:512], ACT.Copy)\
                   .then_inc(pfree(("kv1", t)), 1)
            for t in range(TT):
                proj_ready(act, ("kv2", t))
                act.activation(kvr[:, t, 384:512], pbank(("kv2", t))[:, 0:128], ACT.Copy)
                act.activation(vs2[:, 1, t, :], pbank(("kv2", t))[:, 128:256], ACT.Copy)
                act.activation(ngs[:, t, :], pbank(("kv2", t))[:, 256:304], ACT.Tanh, scale=0.5)\
                   .then_inc(pfree(("kv2", t)), 1)
            rows_in_("q2a", row2)
            rows_in_("q2b", q2b)
            many_columns_in("ks", ksT, range(4))
            for n in range(4):
                aux_ready(act, ("kc", n))
                act.activation(kcT[0:64, n // 2, n % 2, :], abank(("kc", n))[0:64, :], ACT.Copy)
                act.activation(kcT[64:128, n // 2, n % 2, 0:S - 1], abank(("kc", n))[64:128, 1:S], ACT.Copy)\
                   .then_inc(afree(("kc", n)), 1)
            many_columns_in("qt2", qT2, range(4))
            act.wait_ge(hid_in, 1)
            act.activation(hid[:, 2:4, :].rearrange("p a b -> p (a b)")[:, 0:127],
                           hid[:, 2:4, :].rearrange("p a b -> p (a b)")[:, 0:127], ACT.Tanh, scale=SQ2PI)\
               .then_inc(hid_tanh, 1)

            many_columns_in("qt2", qT2, range(4, 8))

            def tanh_rows(name, dst, c0, ts=range(TT)):
                for t in ts:
                    proj_ready(act, (name, t))
                    act.activation(dst[:, t, c0:c0 + 512], pbank((name, t))[:, :], ACT.Tanh, scale=0.5)\
                       .then_inc(pfree((name, t)), 1)

            aux_ready(act, "kcm")
            act.activation(kcmp[:, :, 0:NCMP], abank("kcm")[:, 0:64].rearrange("p (a b) -> p a b", a=2)[:, :, 0:NCMP],
                           ACT.Copy).then_inc(afree("kcm"), 1)
            tanh_rows("m00", mg, 0)
            for j in range(4):
                proj_ready(act, ("ypm", j))
                act.activation(ypT[:, j, :], pbank(("ypm", j))[:, :], ACT.Copy,
                               scale=colv[:, CV_PS + j:CV_PS + j + 1]).then_inc(pfree(("ypm", j)), 1)
            for i in range(TT + 1):
                if i < TT:
                    act.wait_ge(clg_done, i + 1)
                    pv_ = pc[:, i % 2, :].rearrange("p (a b) -> p a b", a=16)[:, :, 0:NCMP]
                    act.activation(pv_, pv_, ACT.Exp).then_inc(cexp_done, 1)
                    tanh_rows("m01", mg, 512, (i,))
                if i >= 1:
                    aux_ready(act, ("cp", i - 1))
                    if i >= 2:
                        act.wait_ge(aux_done, AUX[("cv", i - 2, 1)] + 1)
                    act.activation(pTc, abank(("cp", i - 1))[:, :], ACT.Copy).then_inc(afree(("cp", i - 1)), 1)
            for n in range(NU2 + 1):
                if n < NU2:
                    i, h = UNITS2[n]
                    for b in range(2):
                        act.wait_ge(lg2_done, 2 * n + b + 1)
                        if n >= 4 and b == 0:
                            act.wait_ge(o2_done, n - 3)
                        buf = pr2[:, n % 2, b, 0:128 * (i + 1)]
                        act.activation(buf, buf, ACT.Exp, scale=-1.0, bias=sml[:, 16 + 2 * (n % 2) + b:17 + 2 * (n % 2) + b],
                                       accum_out=sml[:, 40 + 2 * (n % 4) + b:41 + 2 * (n % 4) + b]).then_inc(exp2_done, 1)
                if n >= 1:
                    i, h = UNITS2[n - 1]
                    if n >= 3:
                        act.wait_ge(aux_done, AUX[("pv2", n - 3)] + 1)
                    for b, key in enumerate(("ps", "pw")):
                        aux_ready(act, (key, n - 1))
                        act.activation(pT2[:, (n - 1) % 2, b, 0:128 * (i + 1)], abank((key, n - 1))[:, 0:128 * (i + 1)],
                                       ACT.Copy).then_inc(afree((key, n - 1)), 1)
                if n in FILL2 and FILL2[n][0] != "yp1":
                    key, t = FILL2[n]
                    tanh_rows(key, {"m10": row2, "m11": plT}[key], 0, (t,))
            many_columns_in("o2", oT2, range(8))
            many_columns_in("mt", mT, range(8))
            scaled_columns_in("h3", KT, CV_GF)
            for j in range(FT):
                m = 128 if j < FT - 1 else 64
                for a, key in enumerate(("fg", "fv")):
                    proj_ready(act, (key, j))
                    if a == 0 and j == 0:
                        act.wait_ge(cvw_done, 2)
                    if a == 0 and j >= 2:
                        act.wait_ge(act_done, j - 1)
                    act.activation(fc[0:m, j % 2, a, :], pbank((key, j))[0:m, :], ACT.Identity,
                                   scale=cvw[0:m, a, 2, j:j + 1], bias=cvw[0:m, a, 3, j:j + 1]).then_inc(tap_done, 1)
                act.wait_ge(gatec_done, j + 1)
                act.activation(ft[0:m, j % 2, :], fc[0:m, j % 2, 0, :], ACT.Tanh, scale=0.5).then_inc(ftanh_done, 1)

        @block.gpsimd
        def _(pool):
            step = Steps(pool, pool_step)
            pool.dma_start(onehot[0:33, :], k_bucket).then_inc(onehot_in, 16)
            pool.dma_start(rb_in[0:32, :], rel_bias).then_inc(rb_in_s, 16)
            pool.memset(rb_in[32:33, :], 1.0).then_inc(rb_one, 1)
            pool.wait_ge(rb_one, 1)
            pool.dma_start(sp[:, 0, :], log_dt[0:1, :].partition_broadcast(128)).then_inc(ldt_in, 16)
            for a, src in enumerate(GAINS):
                pool.dma_start(gains[:, 64 * a:64 * a + 64], src.partition_broadcast(128)).then_inc(gains_in, 16)
            step(pool.memset(halves, -0.5))
            n_roots = [0]

            def root(cols):
                n_roots[0] += 1
                pool.wait_ge(ms_done, n_roots[0])
                n = cols.stop - cols.start
                pool.tensor_tensor(stat[:, cols], stat[:, cols], halves[:, 0:n], ALU.pow).then_inc(root_done, 1)

            def x_roots():
                for t in range(TT):
                    root(slice(t, t + 1))

            x_roots()
            pool.dma_start(trim, k_tri).then_inc(consts_in2, 16)
            pool.dma_start(ropeT, k_rope).then_inc(consts_in2, 16)
            pool.dma_start(cmpmask, k_cmpmask).then_inc(consts_in2, 16)
            pool.dma_start(rowvalid, k_rowvalid).then_inc(consts_in2, 16)
            pool.dma_start(cnt, k_cnt).then_inc(consts_in2, 16)
            pool.wait_ge(consts_in2, 80)
            aux_out(pool, "rb")
            aux_out(pool, "rb2")
            pool.dma_start(rb_dram, rb_row[0:8, :]).then_inc(rb_saved, 16)
            for q in range(NQ):
                gs = slice(QG * q, QG * q + QG)
                Xa = [X_[:, gs, :].unsqueeze(2).broadcast_to((128, QG, 9, GC)) for X_ in (X1, X2)]
                Pa = [pw[:, a, :, gs].rearrange("p j g -> p g j").unsqueeze(3).broadcast_to((128, QG, 9, GC))
                      for a in range(2)]
                g1v = g1.rearrange("p (a b c) -> p a b c", a=QG, b=9)
                g2v = g2.rearrange("p (a b c) -> p a b c", a=QG, b=9)
                if q == 0:
                    pool.wait_ge(prep_done, 1)
                    step(pool.memset(Kx[0:GC, :, 0:112], 0.0))
                    pool.memset(r8[:, :, 0:1], 0.0).then_inc(pool_ones, 1)
                else:
                    aux_ready(pool, ("y", q - 1))
                pool.tensor_tensor(g1v, Xa[0], Pa[0], ALU.mult)
                step(pool.tensor_tensor(g2v, Xa[1], Pa[1], ALU.mult))
                step(pool.tensor_tensor(CL, g1v, g2v, ALU.add))
                pool.sem_inc(cl_done, 1)
                Ya = [Y_[:, gs, :].unsqueeze(2).broadcast_to((128, QG, L, GC)) for Y_ in (Y1, Y2)]
                Pa = [pw[:, a, 7::-1, gs].rearrange("p j g -> p g j").unsqueeze(3).broadcast_to((128, QG, L, GC))
                      for a in range(2)]
                g1v = g1[:, 0:1024].rearrange("p (a b c) -> p a b c", a=QG, b=L)
                g2v = g2[:, 0:1024].rearrange("p (a b c) -> p a b c", a=QG, b=L)
                pool.tensor_tensor(g1v, Ya[0], Pa[0], ALU.mult)
                step(pool.tensor_tensor(g2v, Ya[1], Pa[1], ALU.mult))
                step(pool.tensor_tensor(Zt, g1v, g2v, ALU.add))
                pool.sem_inc(zt_done, 1)
                pool.tensor_copy(r8[:, :, 1:NCH], sp[:, 12, gs].unsqueeze(2).broadcast_to((128, QG, NCH - 1)))
                shape = (128, QG, 8, 8)
                fr, fi = [far[:, a, :, gs].rearrange("p n g -> p g n").unsqueeze(3).broadcast_to(shape) for a in range(2)]
                nr, ni = [near[:, a, :, gs].rearrange("p n g -> p g n").unsqueeze(2).broadcast_to(shape) for a in range(2)]
                t1, t2, t3, t4 = [g_[:, o:o + 512].rearrange("p (a b c) -> p a b c", a=QG, b=8)
                                  for g_, o in ((g1, 0), (g2, 0), (g1, 512), (g2, 512))]
                pool.tensor_tensor(t1, fr, nr, ALU.mult)
                pool.tensor_tensor(t2, fi, ni, ALU.mult)
                pool.tensor_tensor(t3, fr, ni, ALU.mult)
                step(pool.tensor_tensor(t4, fi, nr, ALU.mult))
                pool.tensor_tensor(E1.rearrange("p g (a b) -> p g a b", a=8), t1, t2, ALU.subtract)
                step(pool.tensor_tensor(E2.rearrange("p g (a b) -> p g a b", a=8), t3, t4, ALU.add))
                if q in (2, 3):
                    root(slice(16, 16 + 8 * TT))
                aux_out(pool, ("v", q))
                w1 = g1[:, 0:512].rearrange("p (a b) -> p a b", a=QG)
                w2 = g2[:, 0:512].rearrange("p (a b) -> p a b", a=QG)
                pool.tensor_tensor(w1, Vb, E1, ALU.mult)
                pool.wait_ge(v_swapped, 32 * (q + 1))
                step(pool.tensor_tensor(w2, Vs, E2, ALU.mult))
                pool.tensor_tensor(Vb, w1, w2, ALU.add).then_inc(rot_done, 1)
                pool.wait_ge(scan_done, q + 1)
                pool.tensor_tensor(Vb, w1, E1, ALU.mult)
                pool.wait_ge(w_swapped, 32 * (q + 1))
                step(pool.tensor_tensor(w2, Vs, E2, ALU.mult))
                pool.tensor_tensor(Vb, Vb, w2, ALU.subtract).then_inc(s_done, 1)
            aux_ready(pool, ("y", 3))
            pool.wait_ge(rb_saved, 16)
            pool.dma_start(biasR, bass.AP(rb_dram.tensor, 0, [[1, 128], [640, 8], [1, 512]])).then_inc(bias_in, 16)
            pool.dma_start(gt[:, 0, 0:128], k_flip).then_inc(bias_in, 16)
            pool.dma_start(badr, b_ada[0:1, 2048:3072].partition_broadcast(128)).then_inc(badr_in, 16)
            for h in range(8):
                aux_out(pool, ("flip", h))
            for n, (i, h) in enumerate(UNITS1):
                cols = 128 * (i + 1)
                if i and h == 0:
                    pool.wait_ge(topk_done, i)
                if i:
                    if n >= 2:
                        pool.wait_ge(lg_done, n - 1)
                    pool.tensor_tensor(mb[:, n % 2, 0:cols], biasT[:, h, 128 * (3 - i):512], score[:, i, 0:cols],
                                       ALU.add).then_inc(mb_done, 1)
            pool.wait_ge(o_done, NU1)
            pool.dma_start(xrow, x[0].rearrange("(t p) d -> p t d", p=128)).then_inc(x_again, 16)

            x_roots()
            pool.wait_ge(x1_done, 2 * TT)
            pool.dma_start(pwS, pool_w_2[0].rearrange("g c d -> c g d")).then_inc(pw_in, 16)
            pool.memset(kcT[:, :, 2, :], 0.0).then_inc(kc_zero, 1)
            step(pool.memset(cvr, 0.0))
            for a in range(2):
                for tap in range(4):
                    src = conv_w_2[0, tap] if tap < 3 else conv_b_2[0]
                    src = src[DFF * a:DFF * a + DFF]
                    r0 = FT * tap
                    pool.dma_start(cvr[r0:r0 + FT - 1, a, :], src[0:128 * (FT - 1)].rearrange("(j p) -> j p", p=128))\
                        .then_inc(conv_in, 16)
                    pool.dma_start(cvr[r0 + FT - 1:r0 + FT, a, 0:64], src[128 * (FT - 1):DFF].rearrange("(j p) -> j p", p=64))\
                        .then_inc(conv_in, 16)
            def pool_mix():
                for j in range(4):
                    proj_out(pool, ("up", j))
                for j, w in enumerate((2, 4, 8, 16)):
                    src, m, flip = upT[:, j, :], 1, 0
                    while m < w:
                        dst = (plT[:, j, :], tmp2[:, 0:512])[flip] if w in (2, 8) else (tmp2[:, 0:512], plT[:, j, :])[flip]
                        pool.tensor_tensor(dst[:, m:S], src[:, m:S], src[:, 0:S - m], ALU.add)
                        step(pool.tensor_copy(dst[:, 0:m], src[:, 0:m]))
                        src, m, flip = dst, 2 * m, 1 - flip
                    p_ = plT[:, j, :]
                    pool.tensor_scalar(p_[:, 16:S], p_[:, 16:S], 1.0 / w, None, ALU.mult)
                    step(pool.tensor_tensor(p_[:, 0:16], p_[:, 0:16], cnt[:, j, :], ALU.mult))
                    pool.tensor_tensor(p_, p_, upT[:, j, :], ALU.subtract).then_inc(pooled_done, 1)

            def rope(x_, cos, sin, shape):
                n = int(np.prod(shape[1:]))
                names = "abc"[:len(shape) - 1]
                t4 = [tmp2[:, 256 * m:256 * m + n].rearrange(f"p ({' '.join(names)}) -> p {' '.join(names)}",
                                                             **dict(zip(names, shape[1:]))) for m in range(4)]
                lo = x_[:, :, 0:32] if len(shape) == 3 else x_[:, :, :, 0:32]
                hi = x_[:, :, 32:64] if len(shape) == 3 else x_[:, :, :, 32:64]
                pool.tensor_tensor(t4[0], lo, cos, ALU.mult)
                pool.tensor_tensor(t4[1], hi, sin, ALU.mult)
                pool.tensor_tensor(t4[2], hi, cos, ALU.mult)
                step(pool.tensor_tensor(t4[3], lo, sin, ALU.mult))
                pool.tensor_tensor(lo, t4[0], t4[1], ALU.subtract)
                return pool.tensor_tensor(hi, t4[2], t4[3], ALU.add)

            pool_mix()
            root(slice(16, 40))
            for b, c0 in enumerate((0, 256, 384)):
                pool.wait_ge(kgain_done, b + 1)
                shape = (128, TT, 2, 32)
                rope(kvr[:, :, c0:c0 + 128].rearrange("p t (h d) -> p t h d", h=2),
                     ropeT[:, :, 0, :].unsqueeze(2).broadcast_to(shape), ropeT[:, :, 1, :].unsqueeze(2).broadcast_to(shape),
                     shape).then_inc(krope_done, 1)
                pool.wait_ge(krope_done, b + 1)
            for t in range(TT):
                pool.tensor_copy(kdup[:, t, :].rearrange("p (a b d) -> p a b d", a=4, b=2),
                                 kvr[:, t, 256:512].rearrange("p (a d) -> p a d", a=4).unsqueeze(2)
                                 .broadcast_to((128, 4, 2, 64))).then_inc(kdup_done, 1)
            for a, buf in enumerate((row2, q2b)):
                root(slice(16, 48))
                for t in range(TT):
                    pool.wait_ge(qgain_done, 4 * a + t + 1)
                    shape = (128, 8, 32)
                    rope(buf[:, t, :].rearrange("p (h d) -> p h d", h=8),
                         ropeT[:, t, 0:1, :].broadcast_to(shape), ropeT[:, t, 1:2, :].broadcast_to(shape),
                         shape).then_inc(qrope_done, 1)
                    pool.wait_ge(qrope_done, 4 * a + t + 1)
            x_roots()

        @block.vector
        def _(v):
            step = Steps(v, vec_step)
            aux_ready(v, "cols")
            step(v.tensor_copy(colv[:, 0:62], abank("cols")[:, 0:62]))
            v.sem_inc(afree("cols"), 1)
            v.wait_ge(act_tanhc, 1)
            step(v.scalar_tensor_tensor(silc[:, 0:8], silc[:, 8:16], 1.0, colv[:, CV_C:CV_C + 8], ALU.add, ALU.mult))
            v.tensor_scalar(silc[:, 0:8], silc[:, 0:8], 0.5, None, ALU.mult).then_inc(silc_done, 1)
            v.tensor_scalar(colv[:, CV_BGLU:CV_BGLU + 4], colv[:, CV_BGLU:CV_BGLU + 4], 0.5, None, ALU.mult)\
                .then_inc(gbias_done, 1)

            roots = [0]

            def root(cols, scale):
                v.tensor_scalar(stat[:, cols], stat[:, cols], scale, EPS, ALU.mult, ALU.add).then_inc(ms_done, 1)
                roots[0] += 1
                v.wait_ge(root_done, roots[0])

            def row_square(t, scratch):
                step(v.tensor_tensor_reduce(scratch, xrow[:, t, :], xrow[:, t, :], 1.0, 0.0, ALU.mult, ALU.add,
                                            stat[:, t:t + 1]))
                v.tensor_scalar(stat[:, t:t + 1], stat[:, t:t + 1], 1.0 / D, EPS, ALU.mult, ALU.add).then_inc(ms_done, 1)
                roots[0] += 1

            def row_scaled(dst):
                for t in range(TT):
                    v.wait_ge(root_done, roots[0] - TT + t + 1)
                    v.tensor_scalar(dst[:, t, :], xrow[:, t, :], stat[:, t:t + 1], None, ALU.mult).then_inc(xn_done, 1)

            v.wait_ge(x_in, 16)
            for t in range(TT):
                row_square(t, reluq.rearrange("p a b -> p (a b)"))
            row_scaled(xrow)

            LDT, DT, LR, LI, XR, TH, ER, COS, SIN = 0, 1, 2, 3, 4, 5, 6, 7, 8
            E8C, E8S, R8, SG = 10, 11, 12, 13

            def t_(n):
                return sp[:, n, :]

            def mul(o, a, b):
                step(v.tensor_tensor(o, a, b, ALU.mult))

            def exp_(o, a):
                k, r, p = t_(20), t_(21), t_(22)
                step(v.tensor_scalar(r, a, -88.0, 88.7, ALU.max, ALU.min))
                step(v.tensor_scalar(k, r, 1.4426950408889634, 12582912.0, ALU.mult, ALU.add))
                step(v.tensor_scalar(k, k, 12582912.0, None, ALU.subtract))
                step(v.scalar_tensor_tensor(r, k, -0.693359375, r, ALU.mult, ALU.add))
                step(v.scalar_tensor_tensor(r, k, 2.12194440e-4, r, ALU.mult, ALU.add))
                step(v.tensor_scalar(p, r, 1.0 / 5040, None, ALU.mult))
                for f in (720, 120, 24, 6, 2, 1):
                    step(v.scalar_tensor_tensor(p, p, 1.0 / f, r, ALU.add, ALU.mult))
                step(v.tensor_scalar(t_(23).bitcast(i32), k, 127.0, 8388608.0, ALU.add, ALU.mult))
                step(v.scalar_tensor_tensor(o, p, 1.0, t_(23), ALU.add, ALU.mult))

            aux_out(v, "lam")
            v.wait_ge(ldt_in, 16)
            exp_(t_(DT), t_(LDT))
            mul(t_(XR), t_(LR), t_(DT))
            mul(t_(TH), t_(LI), t_(DT))
            exp_(t_(ER), t_(XR))
            k, r, r2, p = t_(20), t_(21), t_(22), t_(23)
            step(v.tensor_scalar(k, t_(TH), 1.0 / (2 * math.pi), 12582912.0, ALU.mult, ALU.add))
            step(v.tensor_scalar(k, k, 12582912.0, None, ALU.subtract))
            step(v.scalar_tensor_tensor(r, k, -6.28125, t_(TH), ALU.mult, ALU.add))
            step(v.scalar_tensor_tensor(r, k, -1.934051513671875e-3, r, ALU.mult, ALU.add))
            step(v.scalar_tensor_tensor(r, k, -1.2556659146e-6, r, ALU.mult, ALU.add))
            mul(r2, r, r)
            step(v.tensor_scalar(p, r2, 1.0 / math.factorial(21), None, ALU.mult))
            for f in range(19, 1, -2):
                step(v.scalar_tensor_tensor(p, p, (-1) ** (f // 2) / math.factorial(f), r2, ALU.add, ALU.mult))
            step(v.scalar_tensor_tensor(t_(SIN), p, 1.0, r, ALU.add, ALU.mult))
            step(v.tensor_scalar(p, r2, 1.0 / math.factorial(20), None, ALU.mult))
            for f in range(18, 0, -2):
                step(v.scalar_tensor_tensor(p, p, (-1) ** (f // 2) / math.factorial(f), r2, ALU.add, ALU.mult))
            step(v.tensor_scalar(t_(COS), p, 1.0, None, ALU.add))
            aux_ready(v, "modt")
            step(v.tensor_tensor(modc[:, 0:16], abank("modt")[:, 0:16], colv[:, CV_ADA:CV_ADA + 16], ALU.add))
            v.sem_inc(afree("modt"), 1)
            v.scalar_tensor_tensor(modc[:, 8:16], modc[:, 8:16], 1.0, colv[:, CV_G:CV_G + 8], ALU.add, ALU.mult)\
                .then_inc(mod_done, 1)
            v.wait_ge(mod_done, 1)
            for k in range(1, KT, 2):
                aux_out(v, ("x", k))
                v.tensor_scalar(hT[:, k, :], hT[:, k, :], modc[:, 8 + k:9 + k], modc[:, k:k + 1], ALU.mult, ALU.add)\
                    .then_inc(h_ready, 1)

            def cmul(o_re, o_im, a_re_, a_im_, b_re_, b_im_, ta, tb, tc, td):
                v.tensor_tensor(ta, a_re_, b_re_, ALU.mult)
                v.tensor_tensor(tb, a_im_, b_im_, ALU.mult)
                v.tensor_tensor(tc, a_re_, b_im_, ALU.mult)
                step(v.tensor_tensor(td, a_im_, b_re_, ALU.mult))
                v.tensor_tensor(o_re, ta, tb, ALU.subtract)
                step(v.tensor_tensor(o_im, tc, td, ALU.add))

            v.memset(pw[:, 0, 0, :], 1.0)
            v.memset(pw[:, 1, 0, :], 0.0)
            mul(pw[:, 0, 1, :], t_(ER), t_(COS))
            mul(pw[:, 1, 1, :], t_(ER), t_(SIN))
            for n in (1, 2, 4):
                for m in range(1, n + 1):
                    cmul(pw[:, 0, n + m, :], pw[:, 1, n + m, :], pw[:, 0, n, :], pw[:, 1, n, :],
                         pw[:, 0, m, :], pw[:, 1, m, :], t_(20), t_(21), t_(22), t_(23))
            v.tensor_copy(t_(E8C), t_(COS))
            step(v.tensor_copy(t_(E8S), t_(SIN)))
            step(v.tensor_copy(t_(R8), t_(ER)))
            for n in range(3):
                cmul(t_(E8C), t_(E8S), t_(E8C), t_(E8S), t_(E8C), t_(E8S), t_(20), t_(21), t_(22), t_(23))
                mul(t_(R8), t_(R8), t_(R8))
            v.memset(far[:, 0, 0, :], 1.0)
            v.memset(far[:, 1, 0, :], 0.0)
            v.tensor_copy(near[:, 0, 0, :], t_(E8C))
            step(v.tensor_copy(near[:, 1, 0, :], t_(E8S)))
            zt_flat = Zt.rearrange("p a b c -> p (a b c)")
            for n in (1, 2, 4):
                for m in range(n):
                    cmul(near[:, 0, n + m, :], near[:, 1, n + m, :], near[:, 0, n - 1, :], near[:, 1, n - 1, :],
                         near[:, 0, m, :], near[:, 1, m, :], t_(20), t_(21), t_(22), t_(23))
            for n in range(1, 8):
                cmul(far[:, 0, n, :], far[:, 1, n, :], far[:, 0, n - 1, :], far[:, 1, n - 1, :],
                     near[:, 0, 7, :], near[:, 1, 7, :], t_(20), t_(21), t_(22), t_(23))
            for tab in (near, far):
                step(v.tensor_scalar(tab[64:128, 1, :, :], tab[64:128, 1, :, :], -1.0, None, ALU.mult))
            NR, DEN, FR, FI = 14, 15, 16, 17
            step(v.tensor_scalar(t_(NR), pw[:, 0, 1, :], -1.0, None, ALU.add))
            mul(t_(20), t_(LR), t_(LR))
            mul(t_(21), t_(LI), t_(LI))
            step(v.tensor_tensor(t_(DEN), t_(20), t_(21), ALU.add))
            step(v.reciprocal(t_(DEN), t_(DEN)))
            v.tensor_tensor(t_(20), t_(NR), t_(LR), ALU.mult)
            v.tensor_tensor(t_(21), pw[:, 1, 1, :], t_(LI), ALU.mult)
            v.tensor_tensor(t_(22), pw[:, 1, 1, :], t_(LR), ALU.mult)
            step(v.tensor_tensor(t_(23), t_(NR), t_(LI), ALU.mult))
            v.tensor_tensor(t_(20), t_(20), t_(21), ALU.add)
            step(v.tensor_tensor(t_(22), t_(22), t_(23), ALU.subtract))
            v.tensor_tensor(t_(FR), t_(20), t_(DEN), ALU.mult)
            step(v.tensor_tensor(t_(FI), t_(22), t_(DEN), ALU.mult))
            A1, A2, A3, A4 = 24, 25, 26, 27
            top, bot = slice(0, 64), slice(64, 128)
            for o, half, src, sgn in ((A1, top, FR, 1), (A1, bot, FI, 1), (A2, top, FI, -1), (A2, bot, FR, 1),
                                      (A3, top, FI, -1), (A3, bot, FR, 1), (A4, top, FR, -1), (A4, bot, FI, -1)):
                step(v.tensor_scalar(sp[half, o, :], sp[half, src, :], float(sgn), None, ALU.mult))
            v.wait_ge(b_in, 32)
            v.wait_ge(b_in2, 32)

            def gb(n):
                return t_(n).unsqueeze(2).broadcast_to((128, G, GC))

            v.tensor_tensor(Y1, bre, gb(A1), ALU.mult)
            v.tensor_tensor(Y2, bre, gb(A3), ALU.mult)
            za, zb = [zt_flat[:, o:o + 512].rearrange("p (a b) -> p a b", a=G) for o in (0, 512)]
            v.tensor_tensor(za, bim, gb(A2), ALU.mult)
            step(v.tensor_tensor(zb, bim, gb(A4), ALU.mult))
            v.tensor_tensor(Y1, Y1, za, ALU.add)
            step(v.tensor_tensor(Y2, Y2, zb, ALU.add))

            def flat(a, rows=slice(0, 128)):
                return a[rows, :, :].rearrange("p a b -> p (a b)")
            aux_out(v, "c1")
            aux_out(v, "c2")
            v.sem_inc(prep_done, 1)
            def scan(q):
                v.wait_ge(rot_done, q + 1)
                v.tensor_tensor_scan(g1[:, 0:512], flat(r8), flat(Vb), 0.0, ALU.mult, ALU.add).then_inc(scan_done, 1)

            scan(0)
            v.wait_ge(consts_in2, 80)
            aux_out(v, "wi")

            def scores(i, m):
                n = 128 * (i + 1)
                for h in range(8):
                    aux_out(v, ("rel", i, h))
                    if h == 0:
                        ins = v.tensor_scalar(score[:, i, 0:n], reluq[:, m % 2, 0:n], wi[:, i, h:h + 1], None, ALU.mult)
                    else:
                        v.wait_ge(rel_used, m)
                        ins = v.scalar_tensor_tensor(score[:, i, 0:n], reluq[:, m % 2, 0:n], wi[:, i, h:h + 1],
                                                     score[:, i, 0:n], ALU.mult, ALU.add)
                    ins.then_inc(rel_used, 1)
                    m += 1
                v.wait_ge(rel_used, m)
                d = score[:, i, 128 * i:128 * i + 128]
                step(v.tensor_tensor(d, d, tri, ALU.add))

            def topk(i, rounds, end=False):
                s = score[:, i, 0:128 * (i + 1)]
                for _ in range(rounds):
                    step(v.max(sml[:, 8:16], s))
                    step(v.match_replace(s, sml[:, 8:16], s, TAKEN))
                if end:
                    v.tensor_scalar(s, s, TAKEN, NEG, ALU.not_equal, ALU.mult).then_inc(topk_done, 1)

            def head_norm(name, gain, done, buf, heads=8, sq=sqt):
                for t in range(TT):
                    proj_out(v, (name, t))
                    r_ = buf[:, t, 0:64 * heads]
                    step(v.tensor_tensor(sq[:, 0:64 * heads], r_, r_, ALU.mult))
                    step(v.tensor_reduce(stat[:, 16 + heads * t:16 + heads * (t + 1)],
                                         sq[:, 0:64 * heads].rearrange("p (a b) -> p a b", a=heads), X, ALU.add))
                root(slice(16, 16 + heads * TT), 1.0 / 64)
                for t in range(TT):
                    rv = buf[:, t, 0:64 * heads].rearrange("p (a b) -> p a b", a=heads)
                    ss = stat[:, 16 + heads * t:16 + heads * (t + 1)]
                    step(v.tensor_tensor(rv, rv, ss.unsqueeze(2).broadcast_to((128, heads, 64)), ALU.mult))
                    v.tensor_tensor(rv, rv, gain.unsqueeze(1).broadcast_to((128, heads, 64)), ALU.mult)\
                        .then_inc(done, 1)

            scores(1, 0)
            scores(2, 8)
            scan(1)
            scores(3, 16)
            topk(1, TOPK // 8, True)
            v.wait_ge(gains_in, 16 * len(GAINS))
            step(v.tensor_scalar(gq1, gq1, 0.125, None, ALU.mult))
            head_norm("k", gk1, knorm_done, row)
            scan(2)
            topk(2, 5)
            head_norm("q", gq1, qnorm_done, row)
            scan(3)
            topk(2, TOPK // 8 - 5, True)

            def az_in(t):
                v.wait_ge(az_tanh, t + 1)
                v.scalar_tensor_tensor(az[:, t, :], az[:, t, :], 1.0, pbank(("az", t))[:, :], ALU.add, ALU.mult)\
                    .then_inc(pfree(("az", t)), 1)

            def fill1(name):
                if name in ("gate0", "gate1"):
                    j = int(name[4])
                    v.wait_ge(badr_in, 16)
                    proj_ready(v, name)
                    v.tensor_tensor(gate_b[:, 512 * j:512 * j + 512], pbank(name)[:, :],
                                    badr[:, 512 * j:512 * j + 512], ALU.add).then_inc(pfree(name), 1)
                elif name[0] == "az":
                    az_in(name[1])
                elif name[0] == "z":
                    j = name[1]
                    v.wait_ge(sz_tanh, j + 1)
                    v.scalar_tensor_tensor(sz[:, j, :].rearrange("p (s c) -> p s c", s=L),
                                           sz[:, j, :].rearrange("p (s c) -> p s c", s=L), 1.0,
                                           pbank(("z", j))[:, :].rearrange("p (c s) -> p s c", s=L),
                                           ALU.add, ALU.mult).then_inc(pfree(("z", j)), 1)
                else:
                    j = name[1]
                    proj_out(v, ("glu", j))
                    step(v.scalar_tensor_tensor(gt[:, j % 2, :], gt[:, j % 2, :], 1.0, zz[:, j, :], ALU.add, ALU.mult))
                    v.scalar_tensor_tensor(yT[:, j, :].rearrange("p (c s) -> p s c", s=L),
                                           gt[:, j % 2, :].rearrange("p (s c) -> p s c", s=L), 0.125,
                                           sz[:, j, :].rearrange("p (s c) -> p s c", s=L), ALU.mult, ALU.mult)\
                        .then_inc(ys_done, 1)

            v.wait_ge(aux_done, AUX[("y", 3)] + 1)
            v.wait_ge(y_back, 16 * NQ)
            v.tensor_copy(silb, silc[:, 0:8].unsqueeze(2).broadcast_to((128, KT, 128))).then_inc(silb_done, 1)
            def gelu_in(j):
                y = yT[:, j, :]
                if j >= 2:
                    v.wait_ge(z_done, j - 1)
                step(v.scalar_tensor_tensor(y, u[:, j, :], colv[:, CV_SKIP + j:CV_SKIP + j + 1], y, ALU.mult, ALU.add))
                step(v.tensor_tensor(gt[:, j % 2, :], y, y, ALU.mult))
                step(v.tensor_scalar(gt[:, j % 2, :], gt[:, j % 2, :], 0.044715, 1.0, ALU.mult, ALU.add))
                v.tensor_tensor(gt[:, j % 2, :], gt[:, j % 2, :], y, ALU.mult).then_inc(y_skip, 1)

            def gelu_out(j):
                v.wait_ge(y_tanh, j + 1)
                v.scalar_tensor_tensor(zz[:, j, :], gt[:, j % 2, :], 1.0, yT[:, j, :], ALU.add, ALU.mult)\
                    .then_inc(z_done, 1)

            for h in range(8):
                aux_ready(v, ("flip", h))
                v.tensor_copy(biasT[:, h, :], abank(("flip", h))[:, :]).then_inc(afree(("flip", h)), 1)
            for h in range(8):
                aux_out(v, ("flip", h))
            az_in(0)
            for n in range(NU1 + 2):
                if n < NU1:
                    i, h = UNITS1[n]
                    cols = 128 * (i + 1)
                    proj_ready(v, ("qk", n))
                    if i:
                        v.wait_ge(mb_done, n - 7)
                        bias = mb[:, n % 2, 0:cols]
                    else:
                        bias = biasT[:, h, 384:512]
                    if n >= 2:
                        v.wait_ge(exp_done, n - 1)
                    v.tensor_tensor_reduce(lg[:, n % 2, 0:cols], pbank(("qk", n))[:, 0:cols], bias, -1.0, 3.0e38,
                                           ALU.add, ALU.min, sml[:, n % 2:n % 2 + 1]).then_inc(lg_done, 1)
                    v.wait_ge(lg_done, n + 1)
                    v.memset(stat[:, 187:188], 0.0).then_inc(pfree(("qk", n)), 1)
                if n < TOPK // 8:
                    topk(3, 1, n == TOPK // 8 - 1)
                if n in (2, 5, 8, 11):
                    gelu_in(n // 3)
                if n >= 2:
                    i, h = UNITS1[n - 2]
                    c0 = 4 + n % 2
                    v.wait_ge(exp_done, n - 1)
                    step(v.reciprocal(sml[:, c0:c0 + 1], sml[:, 48 + (n - 2) % 4:49 + (n - 2) % 4]))
                    step(v.tensor_scalar(sml[:, c0:c0 + 1], sml[:, c0:c0 + 1], 0.5, None, ALU.mult))
                    aux_ready(v, ("pv", n - 2))
                    v.scalar_tensor_tensor(orow[:, i, 64 * h:64 * h + 64], abank(("pv", n - 2))[:, 0:64],
                                           sml[:, c0:c0 + 1], az[:, i, 64 * h:64 * h + 64], ALU.mult, ALU.mult)\
                        .then_inc(o_done, 1)
                    v.wait_ge(o_done, n - 1)
                    v.sem_inc(afree(("pv", n - 2)), 1)
                if n in (4, 7, 10, 13):
                    gelu_out((n - 4) // 3)
                if n - 1 in FILL1:
                    fill1(FILL1[n - 1])
            v.wait_ge(x_again, 16)
            for t in range(TT):
                for j in range(2):
                    proj_ready(v, (f"out{j}", t))
                    part = (row, v1)[j][:, t, :]
                    v.tensor_tensor(part, pbank((f"out{j}", t))[:, :], gate_b[:, 512 * j:512 * j + 512], ALU.mult)\
                        .then_inc(pfree((f"out{j}", t)), 1)
                    proj_out(v, (f"out{j}", t))
                    v.tensor_tensor(xrow[:, t, 512 * j:512 * j + 512], xrow[:, t, 512 * j:512 * j + 512],
                                    part, ALU.add).then_inc(x1_done, 1)
                v.wait_ge(x1_done, 2 * t + 2)
                row_square(t, lg.rearrange("p a b -> p (a b)"))

            row_scaled(xn2)
            for a in range(2):
                aux_ready(v, ("cvt", a))
                v.tensor_copy(cvw[:, a, :, :], abank(("cvt", a))[:, 0:88].rearrange("p (a b) -> p a b", a=4))\
                    .then_inc(cvw_done, 1)
                v.wait_ge(cvw_done, a + 1)
                v.sem_inc(afree(("cvt", a)), 1)
            for t in range(TT):
                proj_out(v, ("kv1", t))
                proj_out(v, ("kv2", t))
            sq2 = pT2[:, 1, 1, :]
            for b, c0 in enumerate((0, 256, 384)):
                kv = kvr[:, :, c0:c0 + 128]
                step(v.tensor_tensor(sq2.rearrange("p (t c) -> p t c", t=TT), kv, kv, ALU.mult))
                step(v.tensor_reduce(stat[:, 16 + 8 * b:24 + 8 * b], sq2.rearrange("p (t d) -> p t d", d=64), X, ALU.add))
            root(slice(16, 40), 1.0 / 64)
            for b, c0 in enumerate((0, 256, 384)):
                kv = kvr[:, :, c0:c0 + 128].rearrange("p t (h d) -> p t h d", h=2)
                rs = stat[:, 16 + 8 * b:24 + 8 * b].rearrange("p (t h) -> p t h", h=2).unsqueeze(3).broadcast_to((128, TT, 2, 64))
                step(v.tensor_tensor(kv, kv, rs, ALU.mult))
                gb_ = gains[:, 192 + 64 * b:256 + 64 * b].unsqueeze(1).unsqueeze(1).broadcast_to((128, TT, 2, 64))
                v.tensor_tensor(kv, kv, gb_, ALU.mult).then_inc(kgain_done, 1)
            v.tensor_scalar(ngs, ngs, 1.0, 0.5, ALU.add, ALU.mult).then_inc(ngs_done, 1)
            gq2 = gains[:, 128:192]
            step(v.tensor_scalar(gq2, gq2, 0.125, None, ALU.mult))
            v.wait_ge(krope_done, 1)
            for t in range(TT):
                v.tensor_copy(kcd[:, t, :].rearrange("p (a b d) -> p a b d", a=4, b=2),
                              kvr[:, t, 0:256].rearrange("p (a d) -> p a d", a=4).unsqueeze(2)
                              .broadcast_to((128, 4, 2, 64))).then_inc(kcd_done, 1)
            head_norm("q2a", gq2, qgain_done, row2, sq=sq2)
            head_norm("q2b", gq2, qgain_done, q2b, sq=sq2)
            step(v.memset(hid, 0.0))
            for a in range(2):
                aux_ready(v, ("hid", a))
                step(v.tensor_tensor(sml[:, 24 + a:25 + a], abank(("hid", a))[:, 2 * NCMP:2 * NCMP + 1],
                                     colv[:, CV_B1 + a:CV_B1 + a + 1], ALU.add))
                v.tensor_scalar(hid[:, a, :].rearrange("p (g n) -> p g n", g=2)[:, :, 0:NCMP],
                                abank(("hid", a))[:, 0:2 * NCMP].rearrange("p (g n) -> p g n", g=2),
                                sml[:, 24 + a:25 + a], None, ALU.add).then_inc(afree(("hid", a)), 1)
                aux_out(v, ("hid", a))
            hx = hid[:, 0:2, :].rearrange("p a b -> p (a b)")[:, 0:127]
            ht = hid[:, 2:4, :].rearrange("p a b -> p (a b)")[:, 0:127]
            step(v.tensor_tensor(ht, hx, hx, ALU.mult))
            step(v.tensor_scalar(ht, ht, 0.044715, 1.0, ALU.mult, ALU.add))
            v.tensor_tensor(ht, ht, hx, ALU.mult).then_inc(hid_in, 1)
            v.wait_ge(hid_tanh, 1)
            step(v.scalar_tensor_tensor(hx, ht, 1.0, hx, ALU.add, ALU.mult))
            step(v.tensor_scalar(hx, hx, 0.5, None, ALU.mult))
            v.sem_inc(hid_done, 2)
            step(v.memset(vbd, 0.0))
            aux_ready(v, ("qt2", 3))
            step(v.memset(pc, 0.0))
            aux_ready(v, "vcm")
            for r in range(4):
                for g in range(2):
                    ins = v.tensor_copy(vbd[32 * r:32 * r + NCMP, g, 64 * r:64 * r + 64],
                                        abank("vcm")[32 * r:32 * r + NCMP, 64 * g:64 * g + 64])
            ins.then_inc(afree("vcm"), 1)

            def gated(name, gate, t, c0):
                proj_out(v, (gate, t))
                proj_ready(v, (name, t))
                d = mg[:, t, c0:c0 + 512]
                v.scalar_tensor_tensor(d, d, 1.0, pbank((name, t))[:, :], ALU.add, ALU.mult)\
                    .then_inc(pfree((name, t)), 1)

            v.wait_ge(ngs_done, 1)

            def compressed_scores(i):
                if i >= 2:
                    v.wait_ge(aux_done, AUX[("cp", i - 2)] + 1)
                for odd in range(2):
                    aux_ready(v, ("cq", i, odd))
                    dst = pc[:, i % 2, :].rearrange("p (a o b) -> p a o b", a=8, o=2)[:, :, odd, 0:NCMP]
                    ps = abank(("cq", i, odd))[:, 0:256].rearrange("p (a b) -> p a b", a=8)[:, :, 0:NCMP]
                    v.tensor_tensor(dst, ps, cmpmask[:, i:i + 1, 0:NCMP].broadcast_to((128, 8, NCMP)), ALU.add)\
                        .then_inc(afree(("cq", i, odd)), 1)
                    aux_out(v, ("cq", i, odd))
                p_ = pc[:, i % 2, :].rearrange("p (a b) -> p a b", a=16)[:, :, 0:NCMP]
                step(v.tensor_reduce(stat[:, 64:80], p_, X, ALU.max))
                v.tensor_tensor(p_, p_, stat[:, 64:80].unsqueeze(2).broadcast_to((128, 16, NCMP)), ALU.subtract)\
                    .then_inc(clg_done, 1)

            def compressed_out(i):
                v.wait_ge(cexp_done, i + 1)
                p_ = pc[:, i % 2, :].rearrange("p (a b) -> p a b", a=16)[:, :, 0:NCMP]
                step(v.tensor_reduce(stat[:, 80:96], p_, X, ALU.add))
                step(v.reciprocal(stat[:, 80:96], stat[:, 80:96]))
                step(v.tensor_tensor(stat[:, 80:96], stat[:, 80:96],
                                     ngs[:, i, :].rearrange("p (a b) -> p a b", a=16)[:, :, 0], ALU.mult))
                step(v.tensor_scalar(stat[:, 80:96], stat[:, 80:96], rowvalid[:, i:i + 1], None, ALU.mult))
                for a in range(2):
                    aux_ready(v, ("cv", i, a))
                    v.tensor_tensor(ob[:, i, 512 * a:512 * a + 512].rearrange("p (a b) -> p a b", a=8),
                                    abank(("cv", i, a))[:, :].rearrange("p (a b) -> p a b", a=8),
                                    stat[:, 80 + 8 * a:88 + 8 * a].unsqueeze(2).broadcast_to((128, 8, 64)), ALU.mult)\
                        .then_inc(afree(("cv", i, a)), 1)
                    aux_out(v, ("cv", i, a))

            for i in range(TT + 1):
                if i < TT:
                    compressed_scores(i)
                if i >= 1:
                    compressed_out(i - 1)
                if i < TT:
                    gated("yp0", "m00", i, 0)
            for n in range(NU2 + 2):
                if n < NU2:
                    i, h = UNITS2[n]
                    cols = 128 * (i + 1)
                    if n >= 2:
                        v.wait_ge(aux_done, AUX[("pw", n - 2)] + 1)
                    for b, key in enumerate(("qs", "qw")):
                        proj_ready(v, (key, n))
                        v.tensor_tensor_reduce(pr2[:, n % 2, b, 0:cols], pbank((key, n))[:, 0:cols], trim[:, 512 - cols:512],
                                               -1.0, 3.0e38, ALU.add, ALU.min,
                                               sml[:, 16 + 2 * (n % 2) + b:17 + 2 * (n % 2) + b]).then_inc(lg2_done, 1)
                        v.wait_ge(lg2_done, 2 * n + b + 1)
                        v.sem_inc(pfree((key, n)), 1)
                if n >= 2:
                    i, h = UNITS2[n - 2]
                    c0 = 28 + 2 * (n % 2)
                    v.wait_ge(exp2_done, 2 * (n - 2) + 2)
                    m = (n - 2) % 4
                    step(v.reciprocal(sml[:, c0:c0 + 2], sml[:, 40 + 2 * m:42 + 2 * m]))
                    step(v.tensor_tensor(sml[:, c0:c0 + 2], sml[:, c0:c0 + 2], ngs[:, i, 3 * h + 1:3 * h + 3], ALU.mult))
                    aux_ready(v, ("pv2", n - 2))
                    o_ = ob[:, i, 64 * h:64 * h + 64]
                    step(v.scalar_tensor_tensor(o_, abank(("pv2", n - 2))[:, 0:64], sml[:, c0:c0 + 1], o_, ALU.mult, ALU.add))
                    v.scalar_tensor_tensor(o_, abank(("pv2", n - 2))[:, 64:128], sml[:, c0 + 1:c0 + 2], o_, ALU.mult, ALU.add)\
                        .then_inc(o2_done, 1)
                    v.wait_ge(o2_done, n - 1)
                    v.sem_inc(afree(("pv2", n - 2)), 1)
                if n in FILL2 and FILL2[n][0] == "yp1":
                    gated("yp1", "m01", FILL2[n][1], 512)
            for j in range(2):
                for t in range(TT):
                    buf = (row2, plT)[j]
                    proj_out(v, (f"m1{j}", t))
                    proj_ready(v, (f"ya{j}", t))
                    v.scalar_tensor_tensor(buf[:, t, :], buf[:, t, :], 1.0, pbank((f"ya{j}", t))[:, :], ALU.add, ALU.mult)\
                        .then_inc(pfree((f"ya{j}", t)), 1)
                    proj_out(v, (f"ya{j}", t))
                    d = mg[:, t, 512 * j:512 * j + 512]
                    v.tensor_tensor(d, d, buf[:, t, :], ALU.add).then_inc(mg_done, 1)

            def half_added(name, t, j, done):
                proj_ready(v, (f"{name}{j}", t))
                d = xrow[:, t, 512 * j:512 * j + 512]
                v.scalar_tensor_tensor(d, pbank((f"{name}{j}", t))[:, :], 0.5, d, ALU.mult, ALU.add).then_inc(done, 1)
                n_added[0] += 1
                v.wait_ge(done, n_added[0])
                v.sem_inc(pfree((f"{name}{j}", t)), 1)

            n_added = [0]
            for t in range(TT):
                for j in range(2):
                    half_added("wo", t, j, x2_done)
                row_square(t, aT[:, 8:10, :].rearrange("p a b -> p (a b)"))
            row_scaled(xn3)
            for j in range(FT):
                m = 128 if j < FT - 1 else 64
                for a, key in enumerate(("fg", "fv")):
                    v.wait_ge(tap_done, 2 * j + a + 1)
                    f_, ps = fc[0:m, j % 2, a, :], pbank((key, j))
                    step(v.scalar_tensor_tensor(f_[:, 1:S], ps[0:m, 0:S - 1], cvw[0:m, a, 1, j:j + 1], f_[:, 1:S],
                                                ALU.mult, ALU.add))
                    step(v.scalar_tensor_tensor(f_[:, 2:S], ps[0:m, 0:S - 2], cvw[0:m, a, 0, j:j + 1], f_[:, 2:S],
                                                ALU.mult, ALU.add))
                    v.sem_inc(pfree((key, j)), 1)
                    if a == 0:
                        v.sem_inc(gatec_done, 1)
                v.wait_ge(ftanh_done, j + 1)
                step(v.scalar_tensor_tensor(ft[0:m, j % 2, :], ft[0:m, j % 2, :], 1.0, fc[0:m, j % 2, 0, :],
                                            ALU.add, ALU.mult))
                v.tensor_tensor(aT[0:m, j, :], ft[0:m, j % 2, :], fc[0:m, j % 2, 1, :], ALU.mult).then_inc(act_done, 1)
            n_added = [0]
            for j in range(2):
                for t in range(TT):
                    half_added("dn", t, j, x3_done)


_INS = ["x", "c", "rel_bias", "norm_g", "w_ada", "b_ada", "w_in", "q_gain", "k_gain", "a_re", "a_im", "log_dt",
        "b_re", "b_im", "c_re", "c_im", "d_skip", "w_glu", "b_glu", "w_out", "attn_norm_w_2", "w_in_2",
        "pool_w_2", "pool_scale_2", "q_norm_w_2", "k_norm_w_2", "cmp_pos_2", "cmp_w1_2", "cmp_b1_2", "cmp_w2_2",
        "w_pool_br_2", "w_attn_br_2", "w_o_2", "ffn_norm_w_2", "w_up_2", "conv_w_2", "conv_b_2", "w_down_2"]


def shape_constants():
    f = np.float32
    ident = np.eye(128, dtype=f)
    bucket = np.zeros((33, 640), f)
    dist = np.arange(S, dtype=np.int32)
    large = 16 + (np.log(np.maximum(dist, 1).astype(f) / f(16)) / f(math.log(8)) * f(16)).astype(np.int32)
    b = np.where(dist < 16, dist, np.minimum(large, 31))
    bucket[b, S - 1 - dist] = 1.0
    bucket[32, S:] = NEG
    p = np.arange(128)
    tri = np.zeros((128, 512), f)
    tri[:, 384:] = np.where(p[None, :] <= p[:, None], 0.0, NEG)
    half = 32
    freqs = f(10000.0) ** (-np.arange(half, dtype=f) / f(half))
    ang = np.arange(S, dtype=f)[:, None] * freqs[None, :]
    rope = np.stack([np.cos(ang), np.sin(ang)], 1).astype(f)
    rope = np.ascontiguousarray(rope.reshape(TT, 128, 2, 32).transpose(1, 0, 2, 3))
    t = np.arange(S)
    ends = np.arange(32) * 16 + 31
    cm = np.where(ends[None, :] <= t[:, None], 0.0, NEG).astype(f)
    cm = np.ascontiguousarray(cm.reshape(TT, 128, 32).transpose(1, 0, 2))
    rv = np.ascontiguousarray((t >= 31).astype(f).reshape(TT, 128).T)
    cnt = np.ones((4, 16), f)
    for i, w in enumerate((2, 4, 8, 16)):
        cnt[i] = f(1) / np.minimum(np.arange(16) + 1, w).astype(f)
    cnt = np.ascontiguousarray(np.broadcast_to(cnt[None], (128, 4, 16)))
    return dict(k_ident=ident, k_bucket=bucket, k_tri=tri, k_rope=rope, k_cmpmask=cm, k_rowvalid=rv, k_cnt=cnt,
                k_flip=np.ascontiguousarray(ident[::-1]))


def kernel(**inputs):
    import concourse.bacc as _bacc
    from concourse.bass_utils import run_bass_kernel_spmd as _run

    nc = _bacc.Bacc("TRN2", target_bir_lowering=False, num_devices=1)
    arrays, args = {}, []
    named = [(name, np.ascontiguousarray(inputs[name])) for name in _INS] + list(shape_constants().items())
    for name, a in named:
        arrays[f"in_{name}"] = a
        args.append(nc.dram_tensor(f"in_{name}", a.shape, mybir.dt.from_np(a.dtype), kind="ExternalInput").ap())
    args.append(nc.dram_tensor("out_0", (1, S, D), mybir.dt.float32, kind="ExternalOutput").ap())
    program(nc, *args)
    r = _run(nc, [arrays], core_ids=[0])
    return r.results[0]["out_0"]
```
